# Optimizing a Trainium2 kernel written in Bass

```python
import math
import jax, jax.numpy as jnp
from jax import lax
import numpy as np

D_MODEL = 2048
BATCH = 1
SEQ = 256
DEPTH = 1
DEC_BATCH = 8
DEC_SEQ = 4
PAST_LEN = 2048
PAGE_SIZE = 128

D_MIX = D_MODEL
D_RG = D_MIX // 2
D_SC = D_MIX - D_RG
RG_HEADS = 16
RG_HEAD_DIM = D_RG // RG_HEADS
RG_CONV_W = 4
RG_C = 8.0
SC_GROUPS = 16
SC_CONV_W = 3
D_IN = 2 * D_RG + 3 * D_SC
N_MEM = 256
XA_HEADS = 4
XA_HEAD_DIM = D_MODEL // XA_HEADS
N_GROUPS = 4
EXPERTS_PER_GROUP = 4
N_EXPERTS = N_GROUPS * EXPERTS_PER_GROUP
TOP_K = 2
D_FF = D_MODEL // 4
EPS = 1e-6

kernel_name = "hymba_rglru_shortconv_memxattn_hmoe_step"

def rmsnorm(x, g):
    xf = x.astype(jnp.float32)
    y = xf * lax.rsqrt(jnp.mean(xf * xf, axis=-1, keepdims=True) + EPS)
    return (y * g.astype(jnp.float32)).astype(x.dtype)

def causal_dwconv(x, buf, w):
    width = w.shape[0]
    t_len = x.shape[1]
    xf = jnp.concatenate([buf.astype(x.dtype), x], axis=1)
    y = xf[:, 0:t_len] * w[0]
    for k in range(1, width):
        y = y + xf[:, k:k + t_len] * w[k]
    return y, xf[:, -(width - 1):]

def rglru_scan(a, b, h0):
    def step(h, ab):
        a_t, b_t = ab
        h = a_t * h + b_t
        return h, h
    h_last, hs = lax.scan(step, h0, (jnp.swapaxes(a, 0, 1), jnp.swapaxes(b, 0, 1)))
    return jnp.swapaxes(hs, 0, 1), h_last

def mixing_block(h, conv_buf, h0, sc_buf, w_in, rg_conv_w, rg_conv_b, rg_w_a, rg_b_a,
                 rg_w_x, rg_b_x, rg_lambda, sc_conv_w, norm_rg_out, norm_sc_out, w_out):
    bsz, t_len, _ = h.shape
    z = h @ w_in
    offs = [D_RG, 2 * D_RG, 2 * D_RG + D_SC, 2 * D_RG + 2 * D_SC]
    rg_x, rg_gate, sc_b, sc_c, sc_x = jnp.split(z, offs, axis=-1)
    xc, conv_buf_new = causal_dwconv(rg_x, conv_buf, rg_conv_w)
    xc = xc + rg_conv_b
    xh = xc.reshape(bsz, t_len, RG_HEADS, RG_HEAD_DIM)
    r = jax.nn.sigmoid(jnp.einsum('bthi,hij->bthj', xh, rg_w_a).reshape(bsz, t_len, D_RG) + rg_b_a)
    i = jax.nn.sigmoid(jnp.einsum('bthi,hij->bthj', xh, rg_w_x).reshape(bsz, t_len, D_RG) + rg_b_x)
    log_a = -RG_C * r.astype(jnp.float32) * jax.nn.softplus(-rg_lambda.astype(jnp.float32))
    a = jnp.exp(log_a)
    mult = jnp.sqrt(-jnp.expm1(2.0 * log_a))
    hs, h_last = rglru_scan(a, mult * (i * xc).astype(jnp.float32), h0.astype(jnp.float32))
    rg_out = rmsnorm(hs.astype(h.dtype) * jax.nn.gelu(rg_gate), norm_rg_out)
    u = sc_c * sc_x
    uc, sc_buf_new = causal_dwconv(u, sc_buf, sc_conv_w)
    sc_out = rmsnorm(sc_b * uc, norm_sc_out)
    y = jnp.concatenate([rg_out, sc_out], axis=-1) @ w_out
    return y, conv_buf_new, h_last.astype(h0.dtype), sc_buf_new

def mem_kv(mem, g_mem, w_k, w_v):
    bsz, n_mem, _ = mem.shape
    m = rmsnorm(mem, g_mem)
    k = (m @ w_k).reshape(bsz, n_mem, XA_HEADS, XA_HEAD_DIM)
    v = (m @ w_v).reshape(bsz, n_mem, XA_HEADS, XA_HEAD_DIM)
    return k, v

def cross_attention(h, k, v, w_q, w_o):
    bsz, t_len, _ = h.shape
    q = (h @ w_q).reshape(bsz, t_len, XA_HEADS, XA_HEAD_DIM)
    s = jnp.einsum('bthd,bmhd->bhtm', q, k.astype(h.dtype)).astype(jnp.float32) / math.sqrt(XA_HEAD_DIM)
    p = jax.nn.softmax(s, axis=-1).astype(h.dtype)
    o = jnp.einsum('bhtm,bmhd->bthd', p, v.astype(h.dtype)).reshape(bsz, t_len, D_MODEL)
    return o @ w_o

def hier_moe(h, wg, bg, we, be, w_gate, w_up, w_down):
    bsz, t_len, d = h.shape
    t = h.reshape(-1, d)
    p_g = jax.nn.softmax((t @ wg + bg).astype(jnp.float32), axis=-1)
    g_sel = jnp.argmax(p_g, axis=-1)
    pg_sel = jnp.take_along_axis(p_g, g_sel[:, None], axis=-1)
    e_logits = (t @ we + be).astype(jnp.float32).reshape(-1, N_GROUPS, EXPERTS_PER_GROUP)
    e_sel = jnp.take_along_axis(e_logits, g_sel[:, None, None], axis=1)[:, 0]
    top_p, top_i = lax.top_k(jax.nn.softmax(e_sel, axis=-1), TOP_K)
    wts = top_p / jnp.sum(top_p, axis=-1, keepdims=True) * pg_sel
    expert_idx = g_sel[:, None] * EXPERTS_PER_GROUP + top_i
    gate = jnp.sum(jax.nn.one_hot(expert_idx, N_EXPERTS, dtype=jnp.float32) * wts[..., None], axis=1)
    a = jnp.einsum('nd,edf->nef', t, w_gate)
    u = jnp.einsum('nd,edf->nef', t, w_up)
    act = jax.nn.silu(a) * u * gate[..., None].astype(h.dtype)
    out = jnp.einsum('nef,efd->nd', act, w_down)
    return out.reshape(bsz, t_len, d)

def setup_inputs(seed: int = 0) -> dict:
    key = jax.random.key(seed)
    ks = iter(jax.random.split(key, 48))
    f32 = jnp.float32

    def nrm(shape, scale):
        return jax.random.normal(next(ks), shape, f32) * scale

    def gain(shape):
        return 1.0 + 0.05 * jax.random.normal(next(ks), shape, f32)

    s = jax.random.uniform(next(ks), (DEPTH, D_RG), f32, 0.9, 0.999) ** (1.0 / RG_C)
    rg_lambda = jnp.log(s) - jnp.log1p(-s)
    return {
        'x_prompt': nrm((BATCH, SEQ, D_MODEL), 1.0),
        'x_sample': nrm((DEC_BATCH, DEC_SEQ, D_MODEL), 1.0),
        'state_rglru_h': nrm((DEPTH, DEC_BATCH, D_RG), 0.5),
        'state_rglru_conv': nrm((DEPTH, DEC_BATCH, RG_CONV_W - 1, D_RG), 1.0),
        'state_sconv': nrm((DEPTH, DEC_BATCH, SC_CONV_W - 1, D_SC), 1.0),
        'cache_mem_k': nrm((DEPTH, DEC_BATCH, N_MEM, XA_HEADS, XA_HEAD_DIM), 1.0),
        'cache_mem_v': nrm((DEPTH, DEC_BATCH, N_MEM, XA_HEADS, XA_HEAD_DIM), 1.0),
        'mem_prompt': nrm((BATCH, N_MEM, D_MODEL), 1.0),
        'norm_mix': gain((DEPTH, D_MODEL)),
        'w_in': nrm((DEPTH, D_MODEL, D_IN), D_MODEL ** -0.5),
        'rg_conv_w': nrm((DEPTH, RG_CONV_W, D_RG), RG_CONV_W ** -0.5),
        'rg_conv_b': nrm((DEPTH, D_RG), 0.02),
        'rg_w_a': nrm((DEPTH, RG_HEADS, RG_HEAD_DIM, RG_HEAD_DIM), RG_HEAD_DIM ** -0.5),
        'rg_b_a': nrm((DEPTH, D_RG), 0.02),
        'rg_w_x': nrm((DEPTH, RG_HEADS, RG_HEAD_DIM, RG_HEAD_DIM), RG_HEAD_DIM ** -0.5),
        'rg_b_x': nrm((DEPTH, D_RG), 0.02),
        'rg_lambda': rg_lambda,
        'sc_conv_w': nrm((DEPTH, SC_CONV_W, D_SC), SC_CONV_W ** -0.5),
        'norm_rg_out': gain((DEPTH, D_RG)),
        'norm_sc_out': gain((DEPTH, D_SC)),
        'w_out': nrm((DEPTH, D_MIX, D_MODEL), D_MIX ** -0.5),
        'norm_xattn': gain((DEPTH, D_MODEL)),
        'norm_mem': gain((DEPTH, D_MODEL)),
        'xa_w_q': nrm((DEPTH, D_MODEL, D_MODEL), D_MODEL ** -0.5),
        'xa_w_k': nrm((DEPTH, D_MODEL, D_MODEL), D_MODEL ** -0.5),
        'xa_w_v': nrm((DEPTH, D_MODEL, D_MODEL), D_MODEL ** -0.5),
        'xa_w_o': nrm((DEPTH, D_MODEL, D_MODEL), D_MODEL ** -0.5),
        'norm_moe': gain((DEPTH, D_MODEL)),
        'router_group_w': nrm((DEPTH, D_MODEL, N_GROUPS), D_MODEL ** -0.5),
        'router_group_b': nrm((DEPTH, N_GROUPS), 0.01),
        'router_expert_w': nrm((DEPTH, D_MODEL, N_EXPERTS), D_MODEL ** -0.5),
        'router_expert_b': nrm((DEPTH, N_EXPERTS), 0.01),
        'expert_w_gate': nrm((DEPTH, N_EXPERTS, D_MODEL, D_FF), D_MODEL ** -0.5),
        'expert_w_up': nrm((DEPTH, N_EXPERTS, D_MODEL, D_FF), D_MODEL ** -0.5),
        'expert_w_down': nrm((DEPTH, N_EXPERTS, D_FF, D_MODEL), D_FF ** -0.5),
        'norm_final': gain((D_MODEL,)),
    }

def reference(x_prompt, x_sample, state_rglru_h, state_rglru_conv, state_sconv, cache_mem_k,
              cache_mem_v, mem_prompt, norm_mix, w_in, rg_conv_w, rg_conv_b, rg_w_a, rg_b_a,
              rg_w_x, rg_b_x, rg_lambda, sc_conv_w, norm_rg_out, norm_sc_out, w_out, norm_xattn,
              norm_mem, xa_w_q, xa_w_k, xa_w_v, xa_w_o, norm_moe, router_group_w, router_group_b,
              router_expert_w, router_expert_b, expert_w_gate, expert_w_up, expert_w_down,
              norm_final):

    def trunk(x, conv_state, h_state, sc_state, mem_keys, mem_values):
        new_conv, new_h, new_sc = [], [], []
        for l in range(DEPTH):
            y, c, hh, sc = mixing_block(
                rmsnorm(x, norm_mix[l]), conv_state[l], h_state[l], sc_state[l], w_in[l],
                rg_conv_w[l], rg_conv_b[l], rg_w_a[l], rg_b_a[l], rg_w_x[l], rg_b_x[l],
                rg_lambda[l], sc_conv_w[l], norm_rg_out[l], norm_sc_out[l], w_out[l])
            x = x + y
            x = x + cross_attention(rmsnorm(x, norm_xattn[l]), mem_keys[l], mem_values[l],
                                    xa_w_q[l], xa_w_o[l])
            x = x + hier_moe(rmsnorm(x, norm_moe[l]), router_group_w[l], router_group_b[l],
                             router_expert_w[l], router_expert_b[l], expert_w_gate[l],
                             expert_w_up[l], expert_w_down[l])
            new_conv.append(c)
            new_h.append(hh)
            new_sc.append(sc)
        return (rmsnorm(x, norm_final), jnp.stack(new_conv), jnp.stack(new_h), jnp.stack(new_sc))

    bp = x_prompt.shape[0]
    dt = x_prompt.dtype
    p_conv0 = jnp.zeros((DEPTH, bp, RG_CONV_W - 1, D_RG), dt)
    p_h0 = jnp.zeros((DEPTH, bp, D_RG), dt)
    p_sc0 = jnp.zeros((DEPTH, bp, SC_CONV_W - 1, D_SC), dt)
    kv = [mem_kv(mem_prompt, norm_mem[l], xa_w_k[l], xa_w_v[l]) for l in range(DEPTH)]
    p_mem_k = jnp.stack([kv[l][0] for l in range(DEPTH)])
    p_mem_v = jnp.stack([kv[l][1] for l in range(DEPTH)])
    y_prompt, p_conv, p_h, p_sc = trunk(x_prompt, p_conv0, p_h0, p_sc0, p_mem_k, p_mem_v)

    y_sample, s_conv, s_h, s_sc = trunk(x_sample, state_rglru_conv, state_rglru_h, state_sconv,
                                        cache_mem_k, cache_mem_v)
    return (y_prompt, y_sample, p_h, p_conv, p_sc, p_mem_k, p_mem_v, s_h, s_conv, s_sc)


_drawn_inputs = setup_inputs


def setup_inputs(seed=0):
    import zlib

    import numpy as np

    out = dict(_drawn_inputs(seed))
    spreads = {}
    factors = {'rg_b_a': 8.0,
     'rg_b_x': 5.161,
     'norm_xattn': 8.0,
     'router_group_b': 4.386,
     'router_expert_b': 19.805}
    for name, (base, spread) in spreads.items():
        noise = np.random.default_rng([zlib.crc32(name.encode()), seed]).standard_normal(out[name].shape)
        drawn = base * np.exp(spread * noise) if base else spread * noise
        out[name] = __import__('jax').numpy.asarray(drawn.astype(out[name].dtype))
    for name, factor in factors.items():
        out[name] = (out[name] * factor).astype(out[name].dtype)
    return out
```

```python
import math
from contextlib import ExitStack

import numpy as np
import concourse.bass as bass
from concourse import mybir

ALU = mybir.AluOpType
ACT = mybir.ActivationFunctionType
AX = mybir.AxisListType
F32 = mybir.dt.float32

P = 128
D = 2048
DB = D // P
TP = 256
NB, ST = 8, 4
T = TP + NB * ST
RG = D // 2
GB = RG // P
CW, SW = 4, 3
NM = 256
NH = 4
HB = DB // NH
NG, EG = 4, 4
NE = NG * EG
FF = D // 4
EPS = 1e-6
RG_C = 8.0
SCALE = 1.0 / math.sqrt(D // NH)
XP = TP + NB * (CW - 1 + ST) + CW - 1
XO = XP - (CW - 1)
UP = TP + NB * (SW - 1 + ST) + SW - 1
UO = UP - (SW - 1)
SLOTS = 8
TW = 512
KT = 4

ROWS, _r = {}, 0
for _n, _c in (("norm_mix", 2), ("norm_xattn", 2), ("norm_mem", 2), ("norm_moe", 2), ("rg_conv_w", CW),
               ("rg_conv_b", 1), ("rg_b_a", 1), ("rg_b_x", 1), ("rg_lambda", 1), ("sc_conv_w", SW),
               ("norm_rg_out", 1), ("norm_sc_out", 1), ("state_rglru_conv", NB * (CW - 1)),
               ("state_rglru_h", NB), ("state_sconv", NB * (SW - 1)), ("norm_final", 2)):
    ROWS[_n] = _r
    _r += _c
NROWS = _r
S_CONV, S_H, S_SC = 0, (1 + NB) * (CW - 1), (1 + NB) * CW
NSTATE = S_SC + (1 + NB) * (SW - 1)

TILE, _t = {}, 0
for _n, _c in (("w_in", 40), ("w_k", 16), ("w_v", 16), ("w_out", 16), ("w_q", 16), ("cache", 4 * NB),
               ("prompt_kv", 4), ("w_o", 16), ("moe", 12 * NE)):
    TILE[_n] = _t
    _t += _c
UNIT, _u = {}, 0
for _n, _c in (("x", 3), ("mem", 2), ("pack", 1), ("x_stat", 1), ("mem_stat", 1), ("w_in", 10), ("gates", 4),
               ("w_k", 4), ("w_v", 4), ("mix_stat", 1), ("states", 1), ("w_out", 4), ("xattn_stat", 1), ("w_q", 4),
               ("sample", 5 * NB), ("prompt", 6), ("w_o", 4), ("moe_stat", 1), ("router", 1), ("gate_t", 1),
               ("moe", 7 * NE), ("final_stat", 1), ("y", 3)):
    UNIT[_n] = _u
    _u += _c
EVENT, _e = {}, 0
for _n, _c in (("x", 3), ("mem", 2), ("pack", 1), ("x_stat", 1), ("mem_stat", 1), ("gates", 4), ("mix_stat", 1),
               ("states", 1), ("xattn_stat", 1), ("sample", 2 * NB), ("prompt", 3), ("moe_stat", 1), ("router", 1),
               ("gate_t", 1), ("moe", NE), ("final_stat", 1), ("y", 3)):
    EVENT[_n] = _e
    _e += _c


class Count:

    def __init__(self, sem):
        self.sem, self.n, self.i, self.per = sem, 0, None, 0

    def tick(self, ins, by=1):
        ins.then_inc(self.sem, by)
        self.n += by
        return ins

    def value(self, n=None):
        n = self.n if n is None else n
        return n if self.i is None else n + self.i * self.per

    def enter(self, i, per):
        self.i, self.per, self.start = i, per, self.n

    def leave(self, times):
        assert self.n - self.start == self.per, (self.n - self.start, self.per)
        self.n = self.start + times * self.per
        self.i = None


def build(nc, a, o):
    ctx = ExitStack()
    with ctx:
        def sb(name, shape, dt=F32):
            return ctx.enter_context(nc.sbuf_tensor(name, shape, dt))

        def sem(name):
            return ctx.enter_context(nc.semaphore(name))

        ring = sb("ring", [P, SLOTS, KT * TW])
        xT = sb("xT", [P, DB, T])
        hT = sb("hT", [P, DB, T])
        mT = sb("mT", [P, DB, NM])
        kv_stage = sb("kv_stage", [P, 2, 2, TW])
        vec = sb("vec", [P, GB, NROWS])
        ident = sb("ident", [P, P])
        mean_d = sb("mean_d", [P, P])
        mean_g = sb("mean_g", [P, P])
        ones = sb("ones", [P, P])
        rstd = sb("rstd", [P, 2, T])
        small = sb("small", [P, 8, GB])
        consts = sb("consts", [P, 8])
        states = sb("states", [P, GB, NSTATE])
        wr = sb("wr", [P, DB, NG + NE])
        rbias = sb("rbias", [P, NG + NE])
        A = sb("A", [P, 17100])

        def cut(at, *shape):
            n = math.prod(shape)
            v = A[:, at:at + n]
            if len(shape) == 2:
                v = v.rearrange("p (a b) -> p a b", b=shape[1])
            if len(shape) == 3:
                v = v.rearrange("p (a b c) -> p a b c", b=shape[1], c=shape[2])
            return v, at + n

        x_nat, at = cut(0, 3, D)
        mem_nat, at = cut(at, 2, D)
        pack, at = cut(at, RG)
        mem_sq, at = cut(at, DB, NM)
        rgx, at = cut(0, GB, XP)
        gelu, at = cut(at, GB, T)
        scb, at = cut(at, GB, T)
        usc, at = cut(at, GB, UP)
        xc, at = cut(at, GB, XO)
        HG = GB // 2
        gr, at = cut(at, HG, XO)
        gi, at = cut(at, HG, XO)
        ge, at = cut(at, HG, XO)
        gE, at = cut(at, HG, XO)
        sq_mix, _ = cut(at - 4 * HG * XO, DB, T)
        uc, _ = cut(0, GB, UO)
        wbd = kv_stage[:, :, :, :].rearrange("p a b c -> p (a b c)").rearrange("p (a b c) -> p a b c", a=2, b=GB)
        oT = hT
        qT, at = cut(0, DB, T)
        kT, at = cut(at, DB, NM)
        pr, at = cut(at, 2 * NH, NM)
        pT, at = cut(at, 2, NH * TP)
        st, at = cut(at, 4, 2 * NH)
        lg, at = cut(0, 3, NG + NE)
        gt, at = cut(at, 3, 20 * 4)
        gate16, at = cut(at, 3, NE)
        gateT, at = cut(at, T)
        gmask, at = cut(at, T)
        gbc, at = cut(at, T)
        silu, at = cut(at, KT, T)
        actT, at = cut(at, KT, T)
        w4, at = cut(at, 4)
        y_nat, at = cut(at, 3, D)
        states_nat = kv_stage[:, :, :, :].rearrange("p a b c -> p (a b c)")[:, 0:RG]

        ps = ctx.enter_context(nc.psum_tensor("ps", [P, 8, 512], F32))

        ring_loaded = [sem(f"ring_loaded{s}") for s in range(SLOTS)]
        tile_used = sem("tile_used")
        unit_done = sem("unit_done")
        half_free = [sem("half0_free"), sem("half1_free")]
        x_loaded, mem_loaded, pack_loaded, wbd_loaded, wr_loaded = map(
            sem, ("x_loaded", "mem_loaded", "pack_loaded", "wbd_loaded", "wr_loaded"))
        consts_set, wbd_zeroed = sem("consts_set"), sem("wbd_zeroed")
        dve_step, act_step, pool_step = sem("dve_step"), sem("act_step"), sem("pool_step")
        squares_ready = sem("squares_ready")
        mem_sq_ready = sem("mem_sq_ready")
        h_ready = sem("h_ready")
        root_ready = sem("root_ready")
        m_ready, xc_ready, pads_ready = sem("m_ready"), sem("xc_ready"), sem("pads_ready")
        lam_in, lam_exp = sem("lam_in"), sem("lam_exp")
        clamp_ready, exp_ready, mult_in_ready, mult_ready, scanned = map(
            sem, ("clamp_ready", "exp_ready", "mult_in_ready", "mult_ready", "scanned"))
        kv_stored = [sem("kv_stored0"), sem("kv_stored1")]
        states_ready, states_stored = sem("states_ready"), sem("states_stored")
        max_ready, probs_scaled = sem("max_ready"), sem("probs_scaled")
        gate_in, gate_exp, gate_ready, gmask_ready = map(sem, ("gate_in", "gate_exp", "gate_ready", "gmask_ready"))
        y_stored = sem("y_stored")

        def G(n, w=4):
            return gt[:, :, 4 * n:4 * n + w]

        def gain(name, b):
            return vec[:, b % GB, ROWS[name] + b // GB:ROWS[name] + b // GB + 1]

        def plus(n, i, per):
            return n if i is None else n + i * per

        def start_unit(pe, u, i=None, per=0):
            if u >= 2:
                pe.wait_ge(half_free[u % 2], plus(2 * (u // 2), i, per))

        def read_out(eng, u, i=None, per=0):
            eng.wait_ge(half_free[u % 2], plus(2 * (u // 2) + 2, i, per))

        def after_event(eng, e, i=None, per=0):
            eng.wait_ge(unit_done, plus(e + 1, i, per))

        def after_tile(eng, t, i=None, per=0):
            eng.wait_ge(tile_used, plus(t + 1, i, per))

        def bank(u, b):
            return ps[:, 4 * (u % 2) + b, :]

        def half(u, n=T, banks=4):
            return ps[:, 4 * (u % 2):4 * (u % 2) + banks, 0:n]

        def from_banks(u, n=P):
            return ps[:, 4 * (u % 2):4 * (u % 2) + 4, :].rearrange("p b (k n) -> p b k n", k=4)[:, :, :, 0:n]

        def quads(x):
            return x.rearrange("p (b k) n -> p b k n", k=4)

        def wait_tile(pe, t, i=None, per=8):
            pe.wait_ge(ring_loaded[t % SLOTS], plus(16 * (t // SLOTS + 1), i, 16 * per // SLOTS))

        def tile_of(t):
            return ring[:, t % SLOTS, :].rearrange("p (k n) -> p k n", k=KT)

        def sample_cols(x, lead, per):
            return x.rearrange("p (b t) -> p b t", t=lead + ST)[:, :, lead + ST - per:]

        def tiles_of(w):
            return w.rearrange("(g k p) m -> g p k m", k=KT, p=P)

        w_in, w_out, w_q, w_k, w_v, w_o = (tiles_of(a[n][0]) for n in (
            "w_in", "w_out", "xa_w_q", "xa_w_k", "xa_w_v", "xa_w_o"))
        e_gate = a["expert_w_gate"][0].rearrange("e (g k p) f -> e g p k f", k=KT, p=P)
        e_up = a["expert_w_up"][0].rearrange("e (g k p) f -> e g p k f", k=KT, p=P)
        e_down = a["expert_w_down"][0].rearrange("e (k p) m -> e p k m", p=P)
        cache = [a[n][0].rearrange("b (c p) h d -> b c p (h d)", p=P) for n in ("cache_mem_k", "cache_mem_v")]
        mem_out = [o[n][0].rearrange("b (c p) h d -> p (b c) (h d)", p=P) for n in ("p_mem_k", "p_mem_v")]

        block = ctx.enter_context(nc.Block())

        @block.sync
        def _(sp):
            sp.dma_start(x_nat[:, 0:2, :], a["x_prompt"][0].rearrange("(c p) d -> p c d", p=P)).then_inc(x_loaded, 16)
            sp.dma_start(x_nat[0:NB * ST, 2, :], a["x_sample"].rearrange("b t d -> (b t) d")).then_inc(x_loaded, 16)
            for name, rows in (("norm_mix", 2), ("norm_xattn", 2), ("norm_mem", 2), ("norm_moe", 2), ("rg_conv_w", CW),
                               ("rg_conv_b", 1), ("rg_b_a", 1), ("rg_b_x", 1), ("rg_lambda", 1), ("sc_conv_w", SW),
                               ("norm_rg_out", 1), ("norm_sc_out", 1), ("state_rglru_conv", NB * (CW - 1)),
                               ("state_rglru_h", NB), ("state_sconv", NB * (SW - 1)), ("norm_final", 2)):
                src = a[name]
                if name == "norm_final":
                    src = src.rearrange("(r c) -> r c", c=RG)
                elif name.startswith("norm") and rows == 2:
                    src = src[0].rearrange("(r c) -> r c", c=RG)
                elif name in ("state_rglru_conv", "state_sconv"):
                    src = src[0].rearrange("b r c -> (b r) c")
                elif len(src.shape) == 3:
                    src = src[0]
                sp.dma_start(pack[ROWS[name]:ROWS[name] + rows, :], src).then_inc(pack_loaded, 16)
            sp.dma_start(mem_nat[:, :, :], a["mem_prompt"][0].rearrange("(c p) d -> p c d", p=P)).then_inc(mem_loaded, 16)
            sp.wait_ge(wbd_zeroed, 1)
            for n, name in enumerate(("rg_w_a", "rg_w_x")):
                for e in range(2):
                    src = a[name][0].rearrange("(b two) i j -> two i b j", two=2)[e]
                    sp.dma_start(wbd[64 * e:64 * e + 64, n, :, 64 * e:64 * e + 64], src).then_inc(wbd_loaded, 16)
            sp.dma_start(wr[:, :, 0:NG], a["router_group_w"][0].rearrange("(b p) g -> p b g", p=P)).then_inc(wr_loaded, 16)
            sp.dma_start(wr[:, :, NG:], a["router_expert_w"][0].rearrange("(b p) g -> p b g", p=P)).then_inc(wr_loaded, 16)
            sp.dma_start(rbias[:, 0:NG], a["router_group_b"][0].partition_broadcast(P)).then_inc(wr_loaded, 16)
            sp.dma_start(rbias[:, NG:], a["router_expert_b"][0].partition_broadcast(P)).then_inc(wr_loaded, 16)

            def load_tile(t, dst, src, i=None, per=8):
                if t >= SLOTS:
                    v = t - SLOTS + 1
                    sp.wait_ge(tile_used, v if i is None else v + i * per)
                sp.dma_start(dst, src).then_inc(ring_loaded[t % SLOTS], 16)

            def load_matrix(name, w, pairs):
                if name == "w_in":
                    for j in range(8):
                        load_tile(j, tile_of(j), w[j % 4, :, :, TW * (j // 4):TW * (j // 4) + TW])
                first = 1 if name == "w_in" else 0
                with sp.Fori(first, pairs) as i:
                    for j in range(8):
                        t = TILE[name] + j
                        v = t - SLOTS + 1
                        sp.wait_ge(tile_used, v + i * 8)
                        sp.dma_start(tile_of(t), w[j % 4, :, :, bass.ds(i * (2 * TW) + TW * (j // 4), TW)]
                                     ).then_inc(ring_loaded[t % SLOTS], 16)

            load_matrix("w_in", w_in, 5)
            load_matrix("w_k", w_k, 2)
            load_matrix("w_v", w_v, 2)
            load_matrix("w_out", w_out, 2)
            load_matrix("w_q", w_q, 2)
            with sp.Fori(0, NB // 2) as i:
                for j in range(8):
                    src = cache[(j // 2) % 2][bass.ds(i * 2 + j // 4, 1), j % 2].rearrange("o p f -> (o p) f")
                    load_tile(TILE["cache"] + j, ring[:, (TILE["cache"] + j) % SLOTS, :], src, i)
            sp.wait_ge(kv_stored[0], 16 * 4)
            sp.wait_ge(kv_stored[1], 16 * 4)
            for j in range(4):
                load_tile(TILE["prompt_kv"] + j, ring[:, (TILE["prompt_kv"] + j) % SLOTS, :],
                          mem_out[j // 2][:, j % 2, :])
            load_matrix("w_o", w_o, 2)
            with sp.Fori(0, NE // 2) as i:
                for j in range(24):
                    e, part, g = j // 12, j % 12 // 4, j % 4
                    pick = bass.ds(i * 2 + e, 1)
                    if part < 2:
                        src = (e_gate, e_up)[part][pick, g].rearrange("o p k f -> (o p) k f")
                    else:
                        src = e_down[pick, :, :, g * TW:(g + 1) * TW].rearrange("o p k f -> (o p) k f")
                    load_tile(TILE["moe"] + j, tile_of(TILE["moe"] + j), src, i, per=24)

        @block.gpsimd
        def _(pool):
            nc.gpsimd.memset(wbd[:, :, :, :].rearrange("p a b c -> p (a b c)"), 0.0).then_inc(wbd_zeroed, 1)
            nc.gpsimd.memset(ident[:, :], 0.0).then_inc(pool_step, 1)
            pool.wait_ge(pool_step, 1)
            nc.gpsimd.affine_select(out=ident[:, :], in_=ident[:, :], compare_op=ALU.not_equal, fill=1.0, base=0,
                                    pattern=[[-1, P]], channel_multiplier=1).then_inc(consts_set, 1)
            nc.gpsimd.memset(mean_d[:, :], 1.0 / D).then_inc(consts_set, 1)
            nc.gpsimd.memset(mean_g[:, :], 1.0 / RG).then_inc(consts_set, 1)
            nc.gpsimd.memset(ones[:, :], 1.0).then_inc(consts_set, 1)
            nc.gpsimd.memset(consts[:, 0:1], EPS).then_inc(consts_set, 1)
            nc.gpsimd.memset(consts[:, 1:2], -0.5).then_inc(consts_set, 1)
            for n, name in enumerate(("w_k", "w_v")):
                for g in range(4):
                    read_out(pool, UNIT[name] + g)
                    pool.dma_start(mem_out[n][:, :, g * TW:(g + 1) * TW], kv_stage[:, g % 2, :, :]
                                   ).then_inc(kv_stored[g % 2], 16)
            read_out(pool, UNIT["states"])
            s = states_nat

            def out_rows(name, r0, n):
                dst = o[name][0]
                if len(dst.shape) == 3:
                    dst = dst.rearrange("b r c -> (b r) c")
                pool.dma_start(dst, s[r0:r0 + n, :]).then_inc(states_stored, 16)

            out_rows("p_conv", S_CONV, CW - 1)
            out_rows("s_conv", S_CONV + CW - 1, NB * (CW - 1))
            out_rows("p_h", S_H, 1)
            out_rows("s_h", S_H + 1, NB)
            out_rows("p_sc", S_SC, SW - 1)
            out_rows("s_sc", S_SC + SW - 1, NB * (SW - 1))
            for c in range(3):
                read_out(pool, UNIT["y"] + c)
                if c < 2:
                    pool.dma_start(o["y_prompt"][0, c * P:(c + 1) * P, :], y_nat[:, c, :]).then_inc(y_stored, 16)
                else:
                    pool.dma_start(o["y_sample"].rearrange("b t d -> (b t) d"), y_nat[0:NB * ST, 2, :]
                                   ).then_inc(y_stored, 16)
            pool.wait_ge(states_stored, 16 * 6)
            pool.wait_ge(y_stored, 16 * 3)

        @block.tensor
        def _(pe):
            mm = nc.tensor.matmul

            def turn(u, src_of, rows, blocks=DB):
                start_unit(pe, u)
                for b in range(blocks):
                    t = nc.tensor.transpose(bank(u, b // 4)[:, b % 4 * P:b % 4 * P + rows], src_of(b),
                                            ident[0:rows, 0:rows])
                t.then_inc(unit_done, 1)

            pe.wait_ge(consts_set, 6)
            pe.wait_ge(x_loaded, 32)
            for c in range(3):
                rows = P if c < 2 else NB * ST
                turn(UNIT["x"] + c, lambda b: x_nat[0:rows, c, b * P:(b + 1) * P], rows)
            pe.wait_ge(mem_loaded, 16)
            for c in range(2):
                turn(UNIT["mem"] + c, lambda b: mem_nat[:, c, b * P:(b + 1) * P], P)
            pe.wait_ge(pack_loaded, 16 * 16)
            turn(UNIT["pack"], lambda b: pack[0:NROWS, b * P:(b + 1) * P], NROWS, GB)

            def stat(u, parts):
                start_unit(pe, u)
                for b, (w, sq, blocks, n) in enumerate(parts):
                    for k in blocks:
                        m = mm(bank(u, b)[:, 0:n], w[:, :], sq[:, k, :], start=(k == blocks[0]), stop=(k == blocks[-1]))
                m.then_inc(unit_done, 1)

            pe.wait_ge(squares_ready, 1)
            stat(UNIT["x_stat"], [(mean_d, hT, range(DB), T)])
            pe.wait_ge(mem_sq_ready, 2)
            stat(UNIT["mem_stat"], [(mean_d, mem_sq, range(DB), NM)])

            def project(name, pairs):
                with pe.Fori(0, pairs) as i:
                    for cg in range(2):
                        u = UNIT[name] + cg
                        start_unit(pe, u, i, 2)
                        for g in range(4):
                            t = TILE[name] + 4 * cg + g
                            wait_tile(pe, t, i)
                            for k in range(KT):
                                for b in range(4):
                                    m = mm(bank(u, b)[:, 0:T], tile_of(t)[:, k, b * P:(b + 1) * P], hT[:, KT * g + k, :],
                                           start=(g == 0 and k == 0), stop=(g == 3 and k == KT - 1))
                            m.then_inc(tile_used, 1)

            pe.wait_ge(h_ready, 1)
            project("w_in", 5)

            pe.wait_ge(wbd_loaded, 16 * 4)
            pe.wait_ge(xc_ready, 1)
            for h in range(2):
                for n in range(2):
                    u = UNIT["gates"] + 2 * h + n
                    start_unit(pe, u)
                    for b in range(HG):
                        m = mm(bank(u, b)[:, 0:XO], wbd[:, n, HG * h + b, :], xc[:, HG * h + b, :], start=True, stop=True)
                    m.then_inc(unit_done, 1)

            pe.wait_ge(m_ready, 1)
            for name in ("w_k", "w_v"):
                with pe.Fori(0, 2) as i:
                    for cg in range(2):
                        u = UNIT[name] + cg
                        start_unit(pe, u, i, 2)
                        for g in range(4):
                            t = TILE[name] + 4 * cg + g
                            wait_tile(pe, t, i)
                            for k in range(KT):
                                for c in range(2):
                                    m = mm(bank(u, c), mT[:, KT * g + k, c * P:(c + 1) * P], tile_of(t)[:, k, :],
                                           start=(g == 0 and k == 0), stop=(g == 3 and k == KT - 1))
                            m.then_inc(tile_used, 1)

            pe.wait_ge(squares_ready, 2)
            stat(UNIT["mix_stat"], [(mean_g, sq_mix, range(GB), T), (mean_g, sq_mix, range(GB, DB), T)])
            u = UNIT["states"]
            start_unit(pe, u)
            pe.wait_ge(states_ready, 1)
            for b in range(GB):
                t = nc.tensor.transpose(bank(u, b // 4)[0:NSTATE, b % 4 * P:b % 4 * P + P], states[:, b, :], ident[:, :])
            t.then_inc(unit_done, 1)

            pe.wait_ge(h_ready, 2)
            project("w_out", 2)
            pe.wait_ge(squares_ready, 3)
            stat(UNIT["xattn_stat"], [(mean_d, hT, range(DB), T)])
            pe.wait_ge(h_ready, 3)
            project("w_q", 2)

            def keys(u, t, i=None, step=0, per=8):
                for c in range(2):
                    start_unit(pe, u + c, i, step)
                    wait_tile(pe, t + c, i, per)
                    for b in range(DB):
                        m = nc.tensor.transpose(bank(u + c, b // 4)[:, b % 4 * P:(b % 4 + 1) * P],
                                                ring[:, (t + c) % SLOTS, b * P:(b + 1) * P], ident[:, :])
                    m.then_inc(tile_used, 1)

            for g in range(2):
                read_out(pe, UNIT["w_q"] + 2 + g)
            with pe.Fori(0, NB // 2) as i:
                for s in range(2):
                    u, t = UNIT["sample"] + 5 * s, TILE["cache"] + 4 * s
                    keys(u, t, i, 10)
                    start_unit(pe, u + 2, i, 10)
                    read_out(pe, u, i, 10)
                    read_out(pe, u + 1, i, 10)
                    for h in range(NH):
                        for k in range(HB):
                            m = mm(bank(u + 2, 0)[32 * h:32 * h + 32, 0:NM], qT[:, HB * h + k, TP:T], kT[:, HB * h + k, :],
                                   start=(k == 0), stop=(k == HB - 1))
                    m.then_inc(unit_done, 1)
                    start_unit(pe, u + 3, i, 10)
                    pe.wait_ge(probs_scaled, s + 1 + i * 2)
                    for c in range(2):
                        m = nc.tensor.transpose(bank(u + 3, 0)[:, c * P:(c + 1) * P], pr[:, 0, c * P:(c + 1) * P], ident[:, :])
                    m.then_inc(unit_done, 1)
                    start_unit(pe, u + 4, i, 10)
                    read_out(pe, u + 3, i, 10)
                    wait_tile(pe, t + 2, i)
                    wait_tile(pe, t + 3, i)
                    for b in range(DB):
                        for c in range(2):
                            m = mm(bank(u + 4, 0)[:, 32 * b:32 * b + 32], ring[:, (t + 2 + c) % SLOTS, b * P:(b + 1) * P],
                                   pT[:, c, 32 * (b // HB):32 * (b // HB) + 32], start=(c == 0), stop=(c == 1))
                    m.then_inc(tile_used, 2)

            u, t = UNIT["prompt"], TILE["prompt_kv"]
            keys(u, t)
            start_unit(pe, u + 2)
            read_out(pe, u)
            read_out(pe, u + 1)
            for c in range(2):
                for h in range(NH):
                    n = NH * c + h
                    for k in range(HB):
                        m = mm(bank(u + 2, n // 2)[:, n % 2 * NM:(n % 2 + 1) * NM], qT[:, HB * h + k, c * P:(c + 1) * P],
                               kT[:, HB * h + k, :], start=(k == 0), stop=(k == HB - 1))
            m.then_inc(unit_done, 1)
            start_unit(pe, u + 3)
            pe.wait_ge(probs_scaled, NB + 1)
            for mc in range(2):
                for h in range(NH):
                    for c in range(2):
                        n = 8 * mc + 2 * h + c
                        m = nc.tensor.transpose(bank(u + 3, n // 4)[:, n % 4 * P:(n % 4 + 1) * P],
                                                pr[:, NH * c + h, mc * P:(mc + 1) * P], ident[:, :])
            m.then_inc(unit_done, 1)
            read_out(pe, u + 3)
            for c in range(2):
                wait_tile(pe, t + 2 + c)
            for hf in range(2):
                start_unit(pe, u + 4 + hf)
                for b8 in range(8):
                    b = 8 * hf + b8
                    for c in range(2):
                        m = mm(bank(u + 4 + hf, b8 // 2)[:, b8 % 2 * TP:(b8 % 2 + 1) * TP],
                               ring[:, (t + 2 + c) % SLOTS, b * P:(b + 1) * P],
                               pT[:, c, TP * (b // HB):TP * (b // HB + 1)], start=(c == 0), stop=(c == 1))
                m.then_inc(*((tile_used, 2) if hf else (unit_done, 1)))
            for hf in range(2):
                read_out(pe, u + 4 + hf)
            project("w_o", 2)
            pe.wait_ge(squares_ready, 4)
            stat(UNIT["moe_stat"], [(mean_d, hT, range(DB), T)])

            pe.wait_ge(h_ready, 4)
            pe.wait_ge(wr_loaded, 16 * 4)
            u = UNIT["router"]
            start_unit(pe, u)
            for c in range(3):
                rows = P if c < 2 else NB * ST
                for k in range(DB):
                    m = mm(bank(u, c)[0:rows, 0:NG + NE], hT[:, k, c * P:c * P + rows], wr[:, k, :],
                           start=(k == 0), stop=(k == DB - 1))
            m.then_inc(unit_done, 1)
            u = UNIT["gate_t"]
            start_unit(pe, u)
            pe.wait_ge(gate_ready, 1)
            for c in range(3):
                rows = P if c < 2 else NB * ST
                m = nc.tensor.transpose(bank(u, 0)[0:NE, c * P:c * P + rows], gate16[0:rows, c, :], ident[0:rows, 0:rows])
            m.then_inc(unit_done, 1)

            with pe.Fori(0, NE // 2) as i:
                for e in range(2):
                    u, t = UNIT["moe"] + 7 * e, TILE["moe"] + 12 * e
                    start_unit(pe, u, i, 14)
                    pe.wait_ge(gmask_ready, e + 1 + i * 2)
                    mm(bank(u, 0)[:, 0:T], ones[0:NE, :], gmask[0:NE, :], start=True, stop=True).then_inc(unit_done, 1)
                    for part in range(2):
                        v = u + 1 + part
                        start_unit(pe, v, i, 14)
                        for g in range(4):
                            tt = t + 4 * part + g
                            wait_tile(pe, tt, i, 24)
                            for k in range(KT):
                                for b in range(4):
                                    m = mm(bank(v, b)[:, 0:T], tile_of(tt)[:, k, b * P:(b + 1) * P], hT[:, KT * g + k, :],
                                           start=(g == 0 and k == 0), stop=(g == 3 and k == KT - 1))
                            m.then_inc(tile_used, 1)
                    read_out(pe, u + 2, i, 14)
                    for g in range(4):
                        v, tt = u + 3 + g, t + 8 + g
                        start_unit(pe, v, i, 14)
                        wait_tile(pe, tt, i, 24)
                        for b in range(4):
                            for k in range(KT):
                                m = mm(bank(v, b)[:, 0:T], tile_of(tt)[:, k, b * P:(b + 1) * P], actT[:, k, :],
                                       start=(k == 0), stop=(k == KT - 1))
                        m.then_inc(tile_used, 1)

            pe.wait_ge(squares_ready, 5)
            stat(UNIT["final_stat"], [(mean_d, hT, range(DB), T)])
            pe.wait_ge(h_ready, 5)
            for c in range(3):
                rows = P if c < 2 else NB * ST
                u = UNIT["y"] + c
                start_unit(pe, u)
                for b in range(DB):
                    m = nc.tensor.transpose(bank(u, b // 4)[0:rows, b % 4 * P:(b % 4 + 1) * P],
                                            hT[:, b, c * P:c * P + rows], ident[:, :])
                m.then_inc(unit_done, 1)

        @block.scalar
        def _(act):
            step = Count(act_step)
            fn, copy = nc.scalar.activation, nc.scalar.copy

            u = UNIT["x"] + 1
            after_event(act, EVENT["x"] + 1)
            copy(quads(xT[:, :, P:2 * P]), from_banks(u)).then_inc(half_free[u % 2], 2)
            for c in range(2):
                u = UNIT["mem"] + c
                after_event(act, EVENT["mem"] + c)
                copy(quads(mT[:, :, c * P:(c + 1) * P]), from_banks(u)).then_inc(half_free[u % 2], 2)
                read_out(act, u)
                fn(mem_sq[:, :, c * P:(c + 1) * P], mT[:, :, c * P:(c + 1) * P], ACT.Square).then_inc(mem_sq_ready, 1)
            u = UNIT["pack"]
            after_event(act, EVENT["pack"])
            copy(vec[:, :, :].rearrange("p (b k) n -> p b k n", k=4), from_banks(u, NROWS)[:, 0:2]
                 ).then_inc(half_free[u % 2], 2)
            act.wait_ge(lam_in, 1)
            fn(small[:, 1, :], small[:, 0, :], ACT.Exp, scale=-1.0)
            fn(consts[:, 2:3], consts[:, 1:2], ACT.Exp).then_inc(lam_exp, 1)

            def root(name, dst, src):
                after_event(act, EVENT[name])
                fn(dst, src, ACT.Sqrt, bias=consts[:, 0:1]).then_inc(half_free[UNIT[name] % 2], 2)

            root("x_stat", rstd[:, 0, :], bank(UNIT["x_stat"], 0)[:, 0:T])
            root("mem_stat", rstd[:, 1, 0:NM], bank(UNIT["mem_stat"], 0)[:, 0:NM])

            def to_padded(dst, u, g, lead):
                copy(dst[:, 4 * g:4 * g + 4, lead:lead + TP], half(u, TP)).then_inc(half_free[u % 2], 1)
                for b in range(4):
                    m = copy(sample_cols(dst[:, 4 * g + b, lead + TP:], lead, ST),
                             bank(u, b)[:, TP:T].rearrange("p (b t) -> p b t", t=ST))
                m.then_inc(half_free[u % 2], 1)

            act.wait_ge(pads_ready, 1)
            for g in range(2):
                after_tile(act, TILE["w_in"] + 4 * g + 3)
                to_padded(rgx, UNIT["w_in"] + g, g, CW - 1)
            for g in range(2):
                u = UNIT["w_in"] + 2 + g
                after_tile(act, TILE["w_in"] + 4 * (2 + g) + 3)
                fn(gelu[:, 4 * g:4 * g + 4, :], half(u), ACT.Gelu_apprx_tanh).then_inc(half_free[u % 2], 2)
            for g in range(2):
                after_tile(act, TILE["w_in"] + 4 * (6 + g) + 3)
                to_padded(usc, UNIT["w_in"] + 6 + g, g, SW - 1)

            for h in range(2):
                if h:
                    act.wait_ge(scanned, 1)
                for n, (dst, bias) in enumerate(((gr, "rg_b_a"), (gi, "rg_b_x"))):
                    u = UNIT["gates"] + 2 * h + n
                    after_event(act, EVENT["gates"] + 2 * h + n)
                    for b in range(HG):
                        c = ROWS[bias]
                        m = fn(dst[:, b, :], bank(u, b)[:, 0:XO], ACT.Sigmoid, bias=vec[:, HG * h + b, c:c + 1])
                    m.then_inc(half_free[u % 2], 2)
                act.wait_ge(clamp_ready, h + 1)
                fn(gE[:, :, :], gE[:, :, :], ACT.Exp).then_inc(exp_ready, 1)
                act.wait_ge(mult_in_ready, h + 1)
                fn(gr[:, :, :], gr[:, :, :], ACT.Sqrt, scale=-1.0).then_inc(mult_ready, 1)

            for n, name in enumerate(("w_k", "w_v")):
                for g in range(4):
                    u = UNIT[name] + g
                    after_tile(act, TILE[name] + 4 * g + 3)
                    if n or g >= 2:
                        act.wait_ge(kv_stored[g % 2], 16 * ((4 * n + g) // 2))
                    copy(kv_stage[:, g % 2, :, :], half(u, TW, 2)).then_inc(half_free[u % 2], 2)
            u = UNIT["mix_stat"]
            after_event(act, EVENT["mix_stat"])
            fn(rstd[:, :, :], half(u, T, 2), ACT.Sqrt, bias=consts[:, 0:1]).then_inc(half_free[u % 2], 2)
            u = UNIT["states"]
            after_event(act, EVENT["states"])
            act.wait_ge(kv_stored[0], 16 * 4)
            act.wait_ge(kv_stored[1], 16 * 4)
            copy(states_nat[0:NSTATE, :].rearrange("p (a b) -> p a b", a=2), half(u, 512, 2)[0:NSTATE]
                 ).then_inc(half_free[u % 2], 2)
            root("xattn_stat", rstd[:, 0, :], bank(UNIT["xattn_stat"], 0)[:, 0:T])

            for g in range(4):
                u = UNIT["w_q"] + g
                after_tile(act, TILE["w_q"] + 4 * g + 3)
                copy(qT[:, 4 * g:4 * g + 4, :], half(u)).then_inc(half_free[u % 2], 2)

            with act.Fori(0, NB // 2) as i:
                for s in range(2):
                    u = UNIT["sample"] + 5 * s
                    after_tile(act, TILE["cache"] + 4 * s, i, 8)
                    copy(quads(kT[:, :, 0:P]), from_banks(u)).then_inc(half_free[u % 2], 2)
                    act.wait_ge(max_ready, s + 1 + i * 2)
                    fn(pr[:, 0, :], bank(u + 2, 0)[:, 0:NM], ACT.Exp, bias=st[:, 1, 0:1], scale=SCALE,
                       accum_out=st[:, 2, 0:1]).then_inc(half_free[u % 2], 2)
            u = UNIT["prompt"]
            after_tile(act, TILE["prompt_kv"])
            copy(quads(kT[:, :, 0:P]), from_banks(u)).then_inc(half_free[u % 2], 2)
            act.wait_ge(max_ready, NB + 1)
            for n in range(2 * NH):
                m = fn(pr[:, n, :], bank(u + 2, n // 2)[:, n % 2 * NM:(n % 2 + 1) * NM], ACT.Exp,
                       bias=st[:, 1, n:n + 1], scale=SCALE, accum_out=st[:, 2, n:n + 1])
            m.then_inc(half_free[u % 2], 2)
            root("moe_stat", rstd[:, 0, :], bank(UNIT["moe_stat"], 0)[:, 0:T])

            act.wait_ge(gate_in, 1)
            fn(G(4), G(3), ACT.Exp).then_inc(gate_exp, 1)
            act.wait_ge(gate_in, 2)
            fn(G(17, 1), G(16, 1), ACT.Exp).then_inc(gate_exp, 1)
            with act.Fori(0, NE // 2) as i:
                for e in range(2):
                    u = UNIT["moe"] + 7 * e + 1
                    after_tile(act, TILE["moe"] + 12 * e + 3, i, 24)
                    fn(silu[:, :, :], half(u), ACT.Silu).then_inc(half_free[u % 2], 2)
            root("final_stat", rstd[:, 0, :], bank(UNIT["final_stat"], 0)[:, 0:T])
            for c in range(3):
                rows = P if c < 2 else NB * ST
                u = UNIT["y"] + c
                after_event(act, EVENT["y"] + c)
                copy(y_nat[0:rows, c, :].rearrange("p (a b) -> p a b", a=4), half(u, 512)[0:rows]
                     ).then_inc(half_free[u % 2], 2)

        @block.vector
        def _(dve):
            step = Count(dve_step)
            v = nc.vector
            tt, ts, stt = v.tensor_tensor, v.tensor_scalar, v.scalar_tensor_tensor

            def then(ins):
                step.tick(ins)
                dve.wait_ge(dve_step, step.value())

            for c, rows in ((0, P), (2, NB * ST)):
                u = UNIT["x"] + c
                after_event(dve, EVENT["x"] + c)
                v.tensor_copy(quads(xT[:, :, c * P:c * P + rows]), from_banks(u, rows)).then_inc(half_free[u % 2], 2)
            for c in range(3):
                read_out(dve, UNIT["x"] + c)
            tt(hT[:, :, :], xT[:, :, :], xT[:, :, :], ALU.mult).then_inc(squares_ready, 1)

            read_out(dve, UNIT["pack"])
            lam = vec[:, :, ROWS["rg_lambda"]]
            stt(out=small[:, 0, :], in0=lam, scalar=-1.0, in1=lam, op0=ALU.mult, op1=ALU.max).then_inc(lam_in, 1)

            def apply_norm(name, u, src, dst, blocks, rs, n, ready=None):
                if u is not None:
                    read_out(dve, u)
                    then(v.reciprocal(rs, rs))
                for b in blocks:
                    m = stt(out=dst[:, b, 0:n], in0=src[:, b, 0:n], scalar=gain(name, b % (2 * GB)), in1=rs,
                            op0=ALU.mult, op1=ALU.mult)
                if ready is not None:
                    m.then_inc(ready, 1)

            apply_norm("norm_mix", UNIT["x_stat"], xT, hT, range(DB), rstd[:, 0, :], T, h_ready)
            apply_norm("norm_mem", UNIT["mem_stat"], mT, mT, range(DB), rstd[:, 1, 0:NM], NM, m_ready)

            v.memset(rgx[:, :, 0:CW - 1], 0.0)
            v.memset(usc[:, :, 0:SW - 1], 0.0)
            for b in range(GB):
                for dst, lead, rows in ((rgx, CW - 1, ROWS["state_rglru_conv"]), (usc, SW - 1, ROWS["state_sconv"])):
                    m = v.tensor_copy(
                        dst[:, b, lead + TP:].rearrange("p (b t) -> p b t", t=lead + ST)[:, :, 0:lead],
                        vec[:, b, rows:rows + NB * lead].rearrange("p (b t) -> p b t", t=lead))
            m.then_inc(pads_ready, 1)

            S = [small[:, n, :] for n in range(8)]
            dve.wait_ge(lam_exp, 1)
            then(ts(S[2], S[1], 2.0, None, ALU.add))
            then(v.reciprocal(S[2], S[2]))
            then(tt(S[3], S[1], S[2], ALU.mult))
            then(tt(S[4], S[3], S[3], ALU.mult))
            then(ts(S[5], S[4], 1.0 / 17, None, ALU.mult))
            for n in (15, 13, 11, 9, 7, 5, 3):
                then(stt(out=S[5], in0=S[5], scalar=1.0 / n, in1=S[4], op0=ALU.add, op1=ALU.mult))
            then(stt(out=S[5], in0=S[5], scalar=1.0, in1=S[3], op0=ALU.add, op1=ALU.mult))
            then(ts(S[7], lam, -1.0, 0.0, ALU.mult, ALU.max))
            then(stt(out=S[5], in0=S[5], scalar=2.0, in1=S[7], op0=ALU.mult, op1=ALU.add))
            then(ts(S[6], S[5], -RG_C, None, ALU.mult))

            def conv(dst, src, n, w, taps, bias):
                for k in range(taps):
                    for b in range(GB):
                        wk = vec[:, b, ROWS[w] + k:ROWS[w] + k + 1]
                        if k:
                            m = stt(out=dst[:, b, :], in0=src[:, b, k:k + n], scalar=wk, in1=dst[:, b, :],
                                    op0=ALU.mult, op1=ALU.add)
                        elif bias:
                            m = ts(dst[:, b, :], src[:, b, 0:n], wk, vec[:, b, ROWS[bias]:ROWS[bias] + 1],
                                   ALU.mult, ALU.add)
                        else:
                            m = ts(dst[:, b, :], src[:, b, 0:n], wk, None, ALU.mult)
                    if k < taps - 1:
                        then(m)
                return m

            for g in range(2):
                read_out(dve, UNIT["w_in"] + g)
            conv(xc, rgx, XO, "rg_conv_w", CW, "rg_conv_b").then_inc(xc_ready, 1)
            v.tensor_copy(states[:, :, S_CONV:S_CONV + CW - 1], rgx[:, :, TP:TP + CW - 1])
            for b in range(GB):
                m = v.tensor_copy(states[:, b, S_CONV + CW - 1:S_H].rearrange("p (b t) -> p b t", t=CW - 1),
                                  sample_cols(rgx[:, b, CW - 1 + TP:], CW - 1, CW - 1))
            then(m)

            for g in range(2):
                u = UNIT["w_in"] + 4 + g
                after_tile(dve, TILE["w_in"] + 4 * (4 + g) + 3)
                v.tensor_copy(scb[:, 4 * g:4 * g + 4, :], half(u)).then_inc(half_free[u % 2], 2)
            for g in range(2):
                u = UNIT["w_in"] + 8 + g
                read_out(dve, UNIT["w_in"] + 6 + g)
                after_tile(dve, TILE["w_in"] + 4 * (8 + g) + 3)
                x = usc[:, 4 * g:4 * g + 4, SW - 1:SW - 1 + TP]
                tt(x, x, half(u, TP), ALU.mult)
                for b in range(4):
                    x = sample_cols(usc[:, 4 * g + b, SW - 1 + TP:], SW - 1, ST)
                    m = tt(x, x, bank(u, b)[:, TP:T].rearrange("p (b t) -> p b t", t=ST), ALU.mult)
                m.then_inc(half_free[u % 2], 2)
            for g in range(2):
                read_out(dve, UNIT["w_in"] + 8 + g)
            v.tensor_copy(states[:, :, S_SC:S_SC + SW - 1], usc[:, :, TP:TP + SW - 1])
            for b in range(GB):
                v.tensor_copy(states[:, b, S_SC + SW - 1:NSTATE].rearrange("p (b t) -> p b t", t=SW - 1),
                              sample_cols(usc[:, b, SW - 1 + TP:], SW - 1, SW - 1))

            for h in range(2):
                blocks = range(HG * h, HG * h + HG)
                read_out(dve, UNIT["gates"] + 2 * h)
                read_out(dve, UNIT["gates"] + 2 * h + 1)
                for b in range(HG):
                    m = ts(gr[:, b, :], gr[:, b, :], small[:, 6, HG * h + b:HG * h + b + 1], None, ALU.mult)
                then(m)
                ts(gE[:, :, :], gr[:, :, :], -0.5, None, ALU.min).then_inc(clamp_ready, 1)
                then(ts(gr[:, :, :], gr[:, :, :], -0.5, None, ALU.max))
                then(ts(ge[:, :, :], gr[:, :, :], 1.0 / math.factorial(8), None, ALU.mult))
                for n in range(7, 0, -1):
                    then(stt(out=ge[:, :, :], in0=ge[:, :, :], scalar=1.0 / math.factorial(n), in1=gr[:, :, :],
                             op0=ALU.add, op1=ALU.mult))
                dve.wait_ge(exp_ready, h + 1)
                then(stt(out=ge[:, :, :], in0=gE[:, :, :], scalar=consts[:, 2:3], in1=ge[:, :, :],
                         op0=ALU.subtract, op1=ALU.add))
                stt(out=gr[:, :, :], in0=ge[:, :, :], scalar=2.0, in1=ge[:, :, :], op0=ALU.add, op1=ALU.mult
                    ).then_inc(mult_in_ready, 1)
                then(ts(gE[:, :, :], ge[:, :, :], 1.0, None, ALU.add))
                then(tt(gi[:, :, :], gi[:, :, :], xc[:, HG * h:HG * h + HG, :], ALU.mult))
                dve.wait_ge(mult_ready, h + 1)
                then(tt(gi[:, :, :], gi[:, :, :], gr[:, :, :], ALU.mult))
                for b in range(HG):
                    r = ROWS["state_rglru_h"]
                    at = lambda x: x[:, b, TP:].rearrange("p (b t) -> p b t", t=CW - 1 + ST)[:, :, CW - 2:CW - 1]
                    v.memset(at(gE), 0.0)
                    m = v.tensor_copy(at(gi), vec[:, HG * h + b, r:r + NB].rearrange("p (b t) -> p b t", t=1))
                then(m)
                for b in range(HG):
                    m = v.tensor_tensor_scan(xc[:, HG * h + b, :], gE[:, b, :], gi[:, b, :], 0.0, ALU.mult, ALU.add)
                m.then_inc(scanned, 1)
            dve.wait_ge(scanned, 2)
            v.tensor_copy(states[:, :, S_H:S_H + 1], xc[:, :, TP - 1:TP])
            for b in range(GB):
                m = v.tensor_copy(states[:, b, S_H + 1:S_SC].rearrange("p (b t) -> p b t", t=1),
                                  sample_cols(xc[:, b, TP:], CW - 1, 1))
            m.then_inc(states_ready, 1)
            tt(hT[:, 0:GB, 0:TP], xc[:, :, 0:TP], gelu[:, :, 0:TP], ALU.mult)
            for b in range(GB):
                tt(hT[:, b, TP:T].rearrange("p (b t) -> p b t", t=ST), sample_cols(xc[:, b, TP:], CW - 1, ST),
                   gelu[:, b, TP:T].rearrange("p (b t) -> p b t", t=ST), ALU.mult)
            then(conv(uc, usc, UO, "sc_conv_w", SW, None))
            tt(hT[:, GB:DB, 0:TP], uc[:, :, 0:TP], scb[:, :, 0:TP], ALU.mult)
            for b in range(GB):
                m = tt(hT[:, GB + b, TP:T].rearrange("p (b t) -> p b t", t=ST), sample_cols(uc[:, b, TP:], SW - 1, ST),
                       scb[:, b, TP:T].rearrange("p (b t) -> p b t", t=ST), ALU.mult)
            then(m)
            tt(sq_mix[:, :, :], hT[:, :, :], hT[:, :, :], ALU.mult).then_inc(squares_ready, 1)
            read_out(dve, UNIT["mix_stat"])
            then(v.reciprocal(rstd[:, :, :], rstd[:, :, :]))
            for n, name in enumerate(("norm_rg_out", "norm_sc_out")):
                for b in range(GB):
                    x = hT[:, GB * n + b, :]
                    m = stt(out=x, in0=x, scalar=vec[:, b, ROWS[name]:ROWS[name] + 1], in1=rstd[:, n, :],
                            op0=ALU.mult, op1=ALU.mult)
            m.then_inc(h_ready, 1)

            def add_residual(name):
                for g in range(4):
                    u = UNIT[name] + g
                    after_tile(dve, TILE[name] + 4 * g + 3)
                    x = xT[:, 4 * g:4 * g + 4, :]
                    tt(x, x, half(u), ALU.add).then_inc(half_free[u % 2], 2)
                read_out(dve, UNIT[name] + 2)
                read_out(dve, UNIT[name] + 3)
                tt(hT[:, :, :], xT[:, :, :], xT[:, :, :], ALU.mult).then_inc(squares_ready, 1)

            add_residual("w_out")
            apply_norm("norm_xattn", UNIT["xattn_stat"], xT, hT, range(DB), rstd[:, 0, :], T, h_ready)

            with dve.Fori(0, NB // 2) as i:
                step.enter(i, 4)
                for s in range(2):
                    u, e = UNIT["sample"] + 5 * s, EVENT["sample"] + 2 * s
                    after_tile(dve, TILE["cache"] + 4 * s + 1, i, 8)
                    v.tensor_copy(quads(kT[:, :, P:NM]), from_banks(u + 1)).then_inc(half_free[(u + 1) % 2], 2)
                    after_event(dve, e, i, 4)
                    then(v.tensor_reduce(st[:, 0, 0:1], bank(u + 2, 0)[:, 0:NM], AX.X, ALU.max))
                    ts(st[:, 1, 0:1], st[:, 0, 0:1], -SCALE, None, ALU.mult).then_inc(max_ready, 1)
                    read_out(dve, u + 2, i, 10)
                    then(v.reciprocal(st[:, 3, 0:1], st[:, 2, 0:1]))
                    ts(pr[:, 0, :], pr[:, 0, :], st[:, 3, 0:1], None, ALU.mult).then_inc(probs_scaled, 1)
                    after_event(dve, e + 1, i, 4)
                    v.tensor_copy(pT[:, :, 0:P], bank(u + 3, 0)[:, 0:NM].rearrange("p (c n) -> p c n", c=2)
                                  ).then_inc(half_free[(u + 3) % 2], 2)
                    after_tile(dve, TILE["cache"] + 4 * s + 3, i, 8)
                    v.tensor_copy(
                        oT[:, :, bass.ds(i * (2 * ST) + (TP + ST * s), ST)],
                        bank(u + 4, 0).rearrange("p (b n) -> p b n", n=NB * ST)[:, :, bass.ds(i * (2 * ST) + ST * s, ST)]
                    ).then_inc(half_free[(u + 4) % 2], 2)
                step.leave(NB // 2)
            u, e = UNIT["prompt"], EVENT["prompt"]
            after_tile(dve, TILE["prompt_kv"] + 1)
            v.tensor_copy(quads(kT[:, :, P:NM]), from_banks(u + 1)).then_inc(half_free[(u + 1) % 2], 2)
            after_event(dve, e)
            scores = half(u + 2, 512).rearrange("p b (two n) -> p b two n", two=2)
            then(v.tensor_reduce(st[:, 0, :].rearrange("p (a b) -> p a b", a=4), scores, AX.X, ALU.max))
            ts(st[:, 1, :], st[:, 0, :], -SCALE, None, ALU.mult).then_inc(max_ready, 1)
            read_out(dve, u + 2)
            then(v.reciprocal(st[:, 3, :], st[:, 2, :]))
            tt(pr[:, :, :], pr[:, :, :], st[:, 3, :].unsqueeze(2).broadcast_to([P, 2 * NH, NM]), ALU.mult
               ).then_inc(probs_scaled, 1)
            after_event(dve, e + 1)
            v.tensor_copy(pT[:, :, :].rearrange("p c n -> p (c n)").rearrange("p (b n) -> p b n", b=4), half(u + 3, 512)
                          ).then_inc(half_free[(u + 3) % 2], 2)
            for hf in range(2):
                if hf:
                    after_tile(dve, TILE["prompt_kv"] + 3)
                else:
                    after_event(dve, e + 2)
                v.tensor_copy(oT[:, 8 * hf:8 * hf + 8, 0:TP].rearrange("p (b two) n -> p b two n", two=2),
                              half(u + 4 + hf, 512).rearrange("p b (two n) -> p b two n", two=2)
                              ).then_inc(half_free[(u + 4 + hf) % 2], 2)
            add_residual("w_o")
            apply_norm("norm_moe", UNIT["moe_stat"], xT, hT, range(DB), rstd[:, 0, :], T, h_ready)

            def over(x, n):
                return x.broadcast_to([P, 3, n])

            def first_max(x, top, onehot, tmp):
                then(v.tensor_reduce(top, x, AX.X, ALU.max))
                then(tt(tmp, x, over(top, 4), ALU.is_equal))
                then(tt(tmp, tmp, w4.unsqueeze(1).broadcast_to([P, 3, 4]), ALU.mult))
                then(v.tensor_reduce(G(15, 1), tmp, AX.X, ALU.max))
                then(tt(onehot, tmp, over(G(15, 1), 4), ALU.is_equal))

            for n in range(4):
                v.memset(w4[:, n:n + 1], 4.0 - n)
            then(v.memset(lg[:, :, :], 0.0))
            dve.wait_ge(wr_loaded, 16 * 4)
            u = UNIT["router"]
            after_event(dve, EVENT["router"])
            for c in range(3):
                rows = P if c < 2 else NB * ST
                m = tt(lg[0:rows, c, :], bank(u, c)[0:rows, 0:NG + NE], rbias[0:rows, :], ALU.add)
            m.then_inc(half_free[u % 2], 2)
            read_out(dve, u)
            first_max(lg[:, :, 0:NG], G(0, 1), G(1), G(2))
            tt(G(3), lg[:, :, 0:NG], over(G(0, 1), 4), ALU.subtract).then_inc(gate_in, 1)
            by_expert = gt[:, :, 4 * 5:4 * 9].rearrange("p c (g j) -> p c g j", g=NG)
            for c in range(3):
                m = tt(by_expert[:, c], lg[:, c, NG:].rearrange("p (g j) -> p g j", g=NG),
                       G(1)[:, c].unsqueeze(2).broadcast_to([P, NG, EG]), ALU.mult)
            then(m)
            for c in range(3):
                m = v.tensor_reduce(G(9)[:, c], by_expert[:, c].rearrange("p g j -> p j g"), AX.X, ALU.add)
            then(m)
            first_max(G(9), G(10, 1), G(11), G(2))
            then(stt(out=G(12), in0=G(11), scalar=-1e30, in1=G(9), op0=ALU.mult, op1=ALU.add))
            first_max(G(12), G(13, 1), G(14), G(2))
            tt(G(16, 1), G(13, 1), G(10, 1), ALU.subtract).then_inc(gate_in, 1)
            dve.wait_ge(gate_exp, 2)
            then(v.tensor_reduce(G(18, 1), G(4), AX.X, ALU.add))
            then(stt(out=G(18, 1), in0=G(17, 1), scalar=1.0, in1=G(18, 1), op0=ALU.add, op1=ALU.mult))
            then(v.reciprocal(G(18, 1), G(18, 1)))
            then(tt(G(11), G(11), over(G(18, 1), 4), ALU.mult))
            then(tt(G(18, 1), G(18, 1), G(17, 1), ALU.mult))
            then(tt(G(14), G(14), over(G(18, 1), 4), ALU.mult))
            then(tt(G(11), G(11), G(14), ALU.add))
            for c in range(3):
                m = tt(gate16[:, c, :].rearrange("p (g j) -> p g j", g=NG), G(1)[:, c].unsqueeze(2).broadcast_to([P, NG, EG]),
                       G(11)[:, c].unsqueeze(1).broadcast_to([P, NG, EG]), ALU.mult)
            m.then_inc(gate_ready, 1)
            u = UNIT["gate_t"]
            after_event(dve, EVENT["gate_t"])
            v.tensor_copy(gateT[0:NE, :], bank(u, 0)[0:NE, 0:T]).then_inc(half_free[u % 2], 2)
            read_out(dve, u)

            with dve.Fori(0, NE // 2) as i:
                step.enter(i, 2)
                for e in range(2):
                    u, t = UNIT["moe"] + 7 * e, TILE["moe"] + 12 * e
                    ts(gmask[0:NE, :], gateT[0:NE, :], ident[0:NE, bass.ds(i * 2 + e, 1)], None, ALU.mult
                       ).then_inc(gmask_ready, 1)
                    after_event(dve, EVENT["moe"] + e, i, 2)
                    v.tensor_copy(gbc[:, :], bank(u, 0)[:, 0:T]).then_inc(half_free[u % 2], 2)
                    read_out(dve, u, i, 14)
                    read_out(dve, u + 1, i, 14)
                    then(tt(silu[:, :, :], silu[:, :, :], gbc.unsqueeze(1).broadcast_to([P, KT, T]), ALU.mult))
                    after_tile(dve, t + 7, i, 24)
                    tt(actT[:, :, :], silu[:, :, :], half(u + 2), ALU.mult).then_inc(half_free[(u + 2) % 2], 2)
                    for g in range(4):
                        after_tile(dve, t + 8 + g, i, 24)
                        x = xT[:, 4 * g:4 * g + 4, :]
                        tt(x, x, half(u + 3 + g), ALU.add).then_inc(half_free[(u + 3 + g) % 2], 2)
                step.leave(NE // 2)
            for g in range(2):
                read_out(dve, UNIT["moe"] + 7 * NE - 2 + g)
            tt(hT[:, :, :], xT[:, :, :], xT[:, :, :], ALU.mult).then_inc(squares_ready, 1)
            apply_norm("norm_final", UNIT["final_stat"], xT, hT, range(DB), rstd[:, 0, :], T, h_ready)
    return nc


_INS = ['x_prompt', 'x_sample', 'state_rglru_h', 'state_rglru_conv', 'state_sconv', 'cache_mem_k', 'cache_mem_v',
        'mem_prompt', 'norm_mix', 'w_in', 'rg_conv_w', 'rg_conv_b', 'rg_w_a', 'rg_b_a', 'rg_w_x', 'rg_b_x',
        'rg_lambda', 'sc_conv_w', 'norm_rg_out', 'norm_sc_out', 'w_out', 'norm_xattn', 'norm_mem', 'xa_w_q',
        'xa_w_k', 'xa_w_v', 'xa_w_o', 'norm_moe', 'router_group_w', 'router_group_b', 'router_expert_w',
        'router_expert_b', 'expert_w_gate', 'expert_w_up', 'expert_w_down', 'norm_final']
_OUTS = [('y_prompt', (1, TP, D)), ('y_sample', (NB, ST, D)), ('p_h', (1, 1, RG)), ('p_conv', (1, 1, CW - 1, RG)),
         ('p_sc', (1, 1, SW - 1, RG)), ('p_mem_k', (1, 1, NM, NH, D // NH)), ('p_mem_v', (1, 1, NM, NH, D // NH)),
         ('s_h', (1, NB, RG)), ('s_conv', (1, NB, CW - 1, RG)), ('s_sc', (1, NB, SW - 1, RG))]


def kernel(**inputs):
    import numpy as _np
    import concourse.bacc as _bacc
    from concourse import mybir as _mybir
    from concourse.bass_utils import run_bass_kernel_spmd as _run

    nc = _bacc.Bacc("TRN2", target_bir_lowering=False, num_devices=1)
    arrays, a, o = {}, {}, {}
    for name in _INS:
        x = _np.ascontiguousarray(inputs[name])
        arrays[f"in_{name}"] = x
        a[name] = nc.dram_tensor(f"in_{name}", x.shape, _mybir.dt.from_np(x.dtype), kind="ExternalInput").ap()
    for name, shape in _OUTS:
        o[name] = nc.dram_tensor(f"out_{name}", shape, _mybir.dt.float32, kind="ExternalOutput").ap()
    build(nc, a, o)
    r = _run(nc, [arrays], core_ids=[0])
    return tuple(r.results[0][f"out_{name}"] for name, _ in _OUTS)
```

```python
import math
from contextlib import ExitStack

import numpy as np
import concourse.bass as bass
from concourse import mybir

ALU = mybir.AluOpType
ACT = mybir.ActivationFunctionType
AX = mybir.AxisListType
F32 = mybir.dt.float32
I32 = mybir.dt.int32

P = 128
D = 2048
DB = D // P
TP = 256
NB, ST = 8, 4
T = TP + NB * ST
RG = D // 2
GB = RG // P
CW, SW = 4, 3
NM = 256
NH = 4
HB = DB // NH
NG, EG = 4, 4
NE = NG * EG
TOP_K = 2
FF = D // 4
EPS = 1e-6
RG_C = 8.0
SCALE = 1.0 / math.sqrt(D // NH)
XP = TP + NB * (CW - 1 + ST) + CW - 1
XO = XP - (CW - 1)
UP = TP + NB * (SW - 1 + ST) + SW - 1
UO = UP - (SW - 1)
SLOTS = 8
TW = 512
KT = 4
C = 64
NJ = 2 * -(-((TOP_K * T + NE * (C - 1)) // C) // 2)
NOWHERE = 1000

ROWS, _r = {}, 0
for _n, _c in (("norm_mix", 2), ("norm_xattn", 2), ("norm_mem", 2), ("norm_moe", 2), ("rg_conv_w", CW),
               ("rg_conv_b", 1), ("rg_b_a", 1), ("rg_b_x", 1), ("rg_lambda", 1), ("sc_conv_w", SW),
               ("norm_rg_out", 1), ("norm_sc_out", 1), ("state_rglru_conv", NB * (CW - 1)),
               ("state_rglru_h", NB), ("state_sconv", NB * (SW - 1)), ("norm_final", 2)):
    ROWS[_n] = _r
    _r += _c
NROWS = _r
S_CONV, S_H, S_SC = 0, (1 + NB) * (CW - 1), (1 + NB) * CW
NSTATE = S_SC + (1 + NB) * (SW - 1)

PU, PE_EVENTS = 2 * 9, 2 * 7
TILE, _t = {}, 0
for _n, _c in (("w_in", 40), ("w_k", 16), ("w_v", 16), ("w_out", 16), ("w_q", 16), ("cache", 4 * NB),
               ("prompt_kv", 4), ("w_o", 16), ("moe", 24)):
    TILE[_n] = _t
    _t += _c
UNIT, _u = {}, 0
for _n, _c in (("x", 3), ("mem", 2), ("pack", 1), ("x_stat", 1), ("mem_stat", 1), ("w_in", 10), ("gates", 4),
               ("w_k", 4), ("w_v", 4), ("mix_stat", 1), ("states", 1), ("w_out", 4), ("xattn_stat", 1), ("w_q", 4),
               ("sample", 5 * NB), ("prompt", 6), ("w_o", 4), ("moe_stat", 1), ("router", 1), ("h_tok", 3),
               ("places", 1), ("moe", PU), ("final_stat", 1), ("y", 3)):
    UNIT[_n] = _u
    _u += _c
EVENT, _e = {}, 0
for _n, _c in (("x", 3), ("mem", 2), ("pack", 1), ("x_stat", 1), ("mem_stat", 1), ("gates", 4), ("mix_stat", 1),
               ("states", 1), ("xattn_stat", 1), ("sample", 2 * NB), ("prompt", 3), ("moe_stat", 1), ("router", 1),
               ("h_tok", 3), ("places", 1), ("moe", PE_EVENTS), ("final_stat", 1), ("y", 3)):
    EVENT[_n] = _e
    _e += _c


class Count:

    def __init__(self, sem):
        self.sem, self.n, self.i, self.per = sem, 0, None, 0

    def tick(self, ins, by=1):
        ins.then_inc(self.sem, by)
        self.n += by
        return ins

    def value(self, n=None):
        n = self.n if n is None else n
        return n if self.i is None else n + self.i * self.per

    def enter(self, i, per):
        self.i, self.per, self.start = i, per, self.n

    def leave_dynamic(self, times):
        assert self.n - self.start == self.per, (self.n - self.start, self.per)
        self.n, self.i = self.start, times

    def leave(self, times):
        assert self.n - self.start == self.per, (self.n - self.start, self.per)
        self.n = self.start + times * self.per
        self.i = None


def build(nc, a, o):
    ctx = ExitStack()
    with ctx:
        def sb(name, shape, dt=F32):
            return ctx.enter_context(nc.sbuf_tensor(name, shape, dt))

        def sem(name):
            return ctx.enter_context(nc.semaphore(name))

        ring = sb("ring", [P, SLOTS, KT * TW])
        xT = sb("xT", [P, DB, T])
        hT = sb("hT", [P, DB, T])
        mT = sb("mT", [P, DB, NM])
        kv_stage = sb("kv_stage", [P, 2, 2, TW])
        vec = sb("vec", [P, GB, NROWS])
        ident = sb("ident", [P, P])
        mean_d = sb("mean_d", [P, P])
        mean_g = sb("mean_g", [P, P])
        ones = sb("ones", [P, P])
        rstd = sb("rstd", [P, 2, T])
        small = sb("small", [P, 8, GB])
        consts = sb("consts", [P, 8])
        states = sb("states", [P, GB, NSTATE])
        wr = sb("wr", [P, DB, NG + NE])
        rbias = sb("rbias", [P, NG + NE])
        before = sb("before", [P, P])
        place_iota = sb("place_iota", [P, 2, C])
        expert_of = sb("expert_of", [1, NJ], I32)
        loops = sb("loops", [1, 1], I32)
        A = sb("A", [P, 17100])

        def cut(at, *shape):
            n = math.prod(shape)
            v = A[:, at:at + n]
            if len(shape) == 2:
                v = v.rearrange("p (a b) -> p a b", b=shape[1])
            if len(shape) == 3:
                v = v.rearrange("p (a b c) -> p a b c", b=shape[1], c=shape[2])
            return v, at + n

        x_nat, at = cut(0, 3, D)
        mem_nat, at = cut(at, 2, D)
        pack, at = cut(at, RG)
        mem_sq, at = cut(at, DB, NM)
        rgx, at = cut(0, GB, XP)
        gelu, at = cut(at, GB, T)
        scb, at = cut(at, GB, T)
        usc, at = cut(at, GB, UP)
        xc, at = cut(at, GB, XO)
        HG = GB // 2
        gr, at = cut(at, HG, XO)
        gi, at = cut(at, HG, XO)
        ge, at = cut(at, HG, XO)
        gE, at = cut(at, HG, XO)
        sq_mix, _ = cut(at - 4 * HG * XO, DB, T)
        uc, _ = cut(0, GB, UO)
        wbd = kv_stage[:, :, :, :].rearrange("p a b c -> p (a b c)").rearrange("p (a b c) -> p a b c", a=2, b=GB)
        oT = hT
        qT, at = cut(0, DB, T)
        kT, at = cut(at, DB, NM)
        pr, at = cut(at, 2 * NH, NM)
        pT, at = cut(at, 2, NH * TP)
        st, at = cut(at, 4, 2 * NH)
        A_all, A = A, mT[:, :, :].rearrange("p a b -> p (a b)")
        lg, at = cut(0, 3, NG + NE)
        gt, at = cut(at, 3, 20 * 4)
        gate16, at = cut(at, 3, NE)
        mask16, at = cut(at, 3, NE)
        posm, at = cut(at, 3, NE)
        w4, at = cut(at, 4)
        tab, at = cut(at, 6, NE)
        cmp, at = cut(at, NJ, NE)
        jt, at = cut(at, 6, NJ)
        job_first = jt[:, 5, :]
        shifted, at = cut(at, 2, 4)
        job_gate, at = cut(at, 2, 4)
        place_gate, at = cut(at, 2, 4)
        silu, at = cut(at, TW)
        act_nat, at = cut(at, TW)
        actT, at = cut(at, KT, C)
        assert at <= DB * NM
        A = A_all
        h_tok, at = cut(0, 3, D)
        pick, at = cut(at, 2, 3, 2 * C)
        spread, at = cut(at, 2, T)
        x_half, at = cut(at, 2, TW)
        xe, at = cut(at, GB, 2, C)
        y_half, at = cut(at, 2 * TW)
        job_iota, at = cut(at, NJ)
        y_nat = ring[:, 0:3, :]
        states_nat = kv_stage[:, :, :, :].rearrange("p a b c -> p (a b c)")[:, 0:RG]

        ps = ctx.enter_context(nc.psum_tensor("ps", [P, 8, 512], F32))

        ring_loaded = [sem(f"ring_loaded{s}") for s in range(SLOTS)]
        tile_used = sem("tile_used")
        unit_done = sem("unit_done")
        half_free = [sem("half0_free"), sem("half1_free")]
        x_loaded, mem_loaded, pack_loaded, wbd_loaded, wr_loaded = map(
            sem, ("x_loaded", "mem_loaded", "pack_loaded", "wbd_loaded", "wr_loaded"))
        consts_set, wbd_zeroed = sem("consts_set"), sem("wbd_zeroed")
        dve_step, act_step, pool_step = sem("dve_step"), sem("act_step"), sem("pool_step")
        squares_ready = sem("squares_ready")
        mem_sq_ready = sem("mem_sq_ready")
        h_ready = sem("h_ready")
        root_ready = sem("root_ready")
        m_ready, xc_ready, pads_ready = sem("m_ready"), sem("xc_ready"), sem("pads_ready")
        lam_in, lam_exp = sem("lam_in"), sem("lam_exp")
        clamp_ready, exp_ready, mult_in_ready, mult_ready, scanned = map(
            sem, ("clamp_ready", "exp_ready", "mult_in_ready", "mult_ready", "scanned"))
        kv_stored = [sem("kv_stored0"), sem("kv_stored1")]
        states_ready, states_stored = sem("states_ready"), sem("states_stored")
        max_ready, probs_scaled = sem("max_ready"), sem("probs_scaled")
        gate_in, gate_exp, mask_ready, jobs_ready = map(sem, ("gate_in", "gate_exp", "mask_ready", "jobs_ready"))
        pick_ready, silu_ready = sem("pick_ready"), sem("silu_ready")
        y_stored = sem("y_stored")

        def G(n, w=4):
            return gt[:, :, 4 * n:4 * n + w]

        def gain(name, b):
            return vec[:, b % GB, ROWS[name] + b // GB:ROWS[name] + b // GB + 1]

        def plus(n, i, per):
            return n if i is None else n + i * per

        def start_unit(pe, u, i=None, per=0):
            if u >= 2:
                pe.wait_ge(half_free[u % 2], plus(2 * (u // 2), i, per))

        def read_out(eng, u, i=None, per=0):
            eng.wait_ge(half_free[u % 2], plus(2 * (u // 2) + 2, i, per))

        def after_event(eng, e, i=None, per=0):
            eng.wait_ge(unit_done, plus(e + 1, i, per))

        def after_tile(eng, t, i=None, per=0):
            eng.wait_ge(tile_used, plus(t + 1, i, per))

        def bank(u, b):
            return ps[:, 4 * (u % 2) + b, :]

        def half(u, n=T, banks=4):
            return ps[:, 4 * (u % 2):4 * (u % 2) + banks, 0:n]

        def from_banks(u, n=P):
            return ps[:, 4 * (u % 2):4 * (u % 2) + 4, :].rearrange("p b (k n) -> p b k n", k=4)[:, :, :, 0:n]

        def quads(x):
            return x.rearrange("p (b k) n -> p b k n", k=4)

        def wait_tile(pe, t, i=None, per=8):
            pe.wait_ge(ring_loaded[t % SLOTS], plus(16 * (t // SLOTS + 1), i, 16 * per // SLOTS))

        def tile_of(t):
            return ring[:, t % SLOTS, :].rearrange("p (k n) -> p k n", k=KT)

        def sample_cols(x, lead, per):
            return x.rearrange("p (b t) -> p b t", t=lead + ST)[:, :, lead + ST - per:]

        def tiles_of(w):
            return w.rearrange("(g k p) m -> g p k m", k=KT, p=P)

        w_in, w_out, w_q, w_k, w_v, w_o = (tiles_of(a[n][0]) for n in (
            "w_in", "w_out", "xa_w_q", "xa_w_k", "xa_w_v", "xa_w_o"))
        e_gate = a["expert_w_gate"][0].rearrange("e (g k p) f -> e g p k f", k=KT, p=P)
        e_up = a["expert_w_up"][0].rearrange("e (g k p) f -> e g p k f", k=KT, p=P)
        e_down = a["expert_w_down"][0].rearrange("e (k p) m -> e p k m", p=P)
        cache = [a[n][0].rearrange("b (c p) h d -> b c p (h d)", p=P) for n in ("cache_mem_k", "cache_mem_v")]
        mem_out = [o[n][0].rearrange("b (c p) h d -> p (b c) (h d)", p=P) for n in ("p_mem_k", "p_mem_v")]

        block = ctx.enter_context(nc.Block())

        @block.sync
        def _(sp):
            sp.dma_start(x_nat[:, 0:2, :], a["x_prompt"][0].rearrange("(c p) d -> p c d", p=P)).then_inc(x_loaded, 16)
            sp.dma_start(x_nat[0:NB * ST, 2, :], a["x_sample"].rearrange("b t d -> (b t) d")).then_inc(x_loaded, 16)
            for name, rows in (("norm_mix", 2), ("norm_xattn", 2), ("norm_mem", 2), ("norm_moe", 2), ("rg_conv_w", CW),
                               ("rg_conv_b", 1), ("rg_b_a", 1), ("rg_b_x", 1), ("rg_lambda", 1), ("sc_conv_w", SW),
                               ("norm_rg_out", 1), ("norm_sc_out", 1), ("state_rglru_conv", NB * (CW - 1)),
                               ("state_rglru_h", NB), ("state_sconv", NB * (SW - 1)), ("norm_final", 2)):
                src = a[name]
                if name == "norm_final":
                    src = src.rearrange("(r c) -> r c", c=RG)
                elif name.startswith("norm") and rows == 2:
                    src = src[0].rearrange("(r c) -> r c", c=RG)
                elif name in ("state_rglru_conv", "state_sconv"):
                    src = src[0].rearrange("b r c -> (b r) c")
                elif len(src.shape) == 3:
                    src = src[0]
                sp.dma_start(pack[ROWS[name]:ROWS[name] + rows, :], src).then_inc(pack_loaded, 16)
            sp.dma_start(mem_nat[:, :, :], a["mem_prompt"][0].rearrange("(c p) d -> p c d", p=P)).then_inc(mem_loaded, 16)
            sp.wait_ge(wbd_zeroed, 1)
            for n, name in enumerate(("rg_w_a", "rg_w_x")):
                for e in range(2):
                    src = a[name][0].rearrange("(b two) i j -> two i b j", two=2)[e]
                    sp.dma_start(wbd[64 * e:64 * e + 64, n, :, 64 * e:64 * e + 64], src).then_inc(wbd_loaded, 16)
            sp.dma_start(wr[:, :, 0:NG], a["router_group_w"][0].rearrange("(b p) g -> p b g", p=P)).then_inc(wr_loaded, 16)
            sp.dma_start(wr[:, :, NG:], a["router_expert_w"][0].rearrange("(b p) g -> p b g", p=P)).then_inc(wr_loaded, 16)
            sp.dma_start(rbias[:, 0:NG], a["router_group_b"][0].partition_broadcast(P)).then_inc(wr_loaded, 16)
            sp.dma_start(rbias[:, NG:], a["router_expert_b"][0].partition_broadcast(P)).then_inc(wr_loaded, 16)

            def load_tile(t, dst, src, i=None, per=8):
                if t >= SLOTS:
                    v = t - SLOTS + 1
                    sp.wait_ge(tile_used, v if i is None else v + i * per)
                sp.dma_start(dst, src).then_inc(ring_loaded[t % SLOTS], 16)

            def load_matrix(name, w, pairs):
                if name == "w_in":
                    for j in range(8):
                        load_tile(j, tile_of(j), w[j % 4, :, :, TW * (j // 4):TW * (j // 4) + TW])
                first = 1 if name == "w_in" else 0
                with sp.Fori(first, pairs) as i:
                    for j in range(8):
                        t = TILE[name] + j
                        v = t - SLOTS + 1
                        sp.wait_ge(tile_used, v + i * 8)
                        sp.dma_start(tile_of(t), w[j % 4, :, :, bass.ds(i * (2 * TW) + TW * (j // 4), TW)]
                                     ).then_inc(ring_loaded[t % SLOTS], 16)

            load_matrix("w_in", w_in, 5)
            load_matrix("w_k", w_k, 2)
            load_matrix("w_v", w_v, 2)
            load_matrix("w_out", w_out, 2)
            load_matrix("w_q", w_q, 2)
            with sp.Fori(0, NB // 2) as i:
                for j in range(8):
                    src = cache[(j // 2) % 2][bass.ds(i * 2 + j // 4, 1), j % 2].rearrange("o p f -> (o p) f")
                    load_tile(TILE["cache"] + j, ring[:, (TILE["cache"] + j) % SLOTS, :], src, i)
            sp.wait_ge(kv_stored[0], 16 * 4)
            sp.wait_ge(kv_stored[1], 16 * 4)
            for j in range(4):
                load_tile(TILE["prompt_kv"] + j, ring[:, (TILE["prompt_kv"] + j) % SLOTS, :],
                          mem_out[j // 2][:, j % 2, :])
            load_matrix("w_o", w_o, 2)
            def expert_tile(e, j, t, i=None):
                if j < 8:
                    src = (e_gate, e_up)[j % 2][bass.ds(e, 1), j // 2].rearrange("o p k f -> (o p) k f")
                else:
                    g = (0, 2, 1, 3)[j - 8]
                    src = e_down[bass.ds(e, 1), :, :, g * TW:(g + 1) * TW].rearrange("o p k f -> (o p) k f")
                load_tile(t, tile_of(t), src, i, per=24)

            for j in range(8):
                expert_tile(0, j, TILE["moe"] + j)
            sp.wait_ge(jobs_ready, 2)

            def pair_of_jobs(i, last):
                for n in range(2 if last else 3):
                    e = sp.value_load(expert_of[0:1, bass.ds(i * 2 + n, 1)], min_val=0, max_val=NE - 1)
                    for j in range(8 if n == 0 else 0, 8 if n == 2 else 12):
                        expert_tile(e, j, TILE["moe"] + 12 * n + j, i)

            n_loops = sp.value_load(loops[0:1, 0:1], min_val=NE // 2 - 1, max_val=NJ // 2 - 1)
            with sp.Fori(0, n_loops) as i:
                pair_of_jobs(i, False)
            pair_of_jobs(n_loops, True)
            for c in range(3):
                read_out(sp, UNIT["y"] + c, n_loops, PU)
                if c < 2:
                    sp.dma_start(o["y_prompt"][0, c * P:(c + 1) * P, :], y_nat[:, c, :]).then_inc(y_stored, 16)
                else:
                    sp.dma_start(o["y_sample"].rearrange("b t d -> (b t) d"), y_nat[0:NB * ST, 2, :]
                                 ).then_inc(y_stored, 16)
            sp.wait_ge(y_stored, 16 * 3)

        @block.gpsimd
        def _(pool):
            nc.gpsimd.memset(wbd[:, :, :, :].rearrange("p a b c -> p (a b c)"), 0.0).then_inc(wbd_zeroed, 1)
            nc.gpsimd.memset(ident[:, :], 0.0).then_inc(pool_step, 1)
            pool.wait_ge(pool_step, 1)
            nc.gpsimd.affine_select(out=ident[:, :], in_=ident[:, :], compare_op=ALU.not_equal, fill=1.0, base=0,
                                    pattern=[[-1, P]], channel_multiplier=1).then_inc(consts_set, 1)
            nc.gpsimd.memset(mean_d[:, :], 1.0 / D).then_inc(consts_set, 1)
            nc.gpsimd.memset(mean_g[:, :], 1.0 / RG).then_inc(consts_set, 1)
            nc.gpsimd.memset(ones[:, :], 1.0).then_inc(consts_set, 1)
            nc.gpsimd.memset(consts[:, 0:1], EPS).then_inc(consts_set, 1)
            nc.gpsimd.memset(consts[:, 1:2], -0.5).then_inc(consts_set, 1)
            pool.wait_ge(consts_set, 6)
            nc.gpsimd.affine_select(out=before[:, :], in_=ones[:, :], compare_op=ALU.is_gt, fill=0.0, base=0,
                                    pattern=[[1, P]], channel_multiplier=-1).then_inc(consts_set, 1)
            nc.gpsimd.iota(place_iota[:, :, :], pattern=[[0, 2], [1, C]], base=0, channel_multiplier=0,
                           allow_small_or_imprecise_dtypes=True).then_inc(consts_set, 1)
            for n, name in enumerate(("w_k", "w_v")):
                for g in range(4):
                    read_out(pool, UNIT[name] + g)
                    pool.dma_start(mem_out[n][:, :, g * TW:(g + 1) * TW], kv_stage[:, g % 2, :, :]
                                   ).then_inc(kv_stored[g % 2], 16)
            read_out(pool, UNIT["states"])
            s = states_nat

            def out_rows(name, r0, n):
                dst = o[name][0]
                if len(dst.shape) == 3:
                    dst = dst.rearrange("b r c -> (b r) c")
                pool.dma_start(dst, s[r0:r0 + n, :]).then_inc(states_stored, 16)

            out_rows("p_conv", S_CONV, CW - 1)
            out_rows("s_conv", S_CONV + CW - 1, NB * (CW - 1))
            out_rows("p_h", S_H, 1)
            out_rows("s_h", S_H + 1, NB)
            out_rows("p_sc", S_SC, SW - 1)
            out_rows("s_sc", S_SC + SW - 1, NB * (SW - 1))
            pool.wait_ge(states_stored, 16 * 6)

        @block.tensor
        def _(pe):
            mm = nc.tensor.matmul

            def turn(u, src_of, rows, blocks=DB):
                start_unit(pe, u)
                for b in range(blocks):
                    t = nc.tensor.transpose(bank(u, b // 4)[:, b % 4 * P:b % 4 * P + rows], src_of(b),
                                            ident[0:rows, 0:rows])
                t.then_inc(unit_done, 1)

            pe.wait_ge(consts_set, 6)
            pe.wait_ge(x_loaded, 32)
            for c in range(3):
                rows = P if c < 2 else NB * ST
                turn(UNIT["x"] + c, lambda b: x_nat[0:rows, c, b * P:(b + 1) * P], rows)
            pe.wait_ge(mem_loaded, 16)
            for c in range(2):
                turn(UNIT["mem"] + c, lambda b: mem_nat[:, c, b * P:(b + 1) * P], P)
            pe.wait_ge(pack_loaded, 16 * 16)
            turn(UNIT["pack"], lambda b: pack[0:NROWS, b * P:(b + 1) * P], NROWS, GB)

            def stat(u, parts, i=None, per=0):
                start_unit(pe, u, i, per)
                for b, (w, sq, blocks, n) in enumerate(parts):
                    for k in blocks:
                        m = mm(bank(u, b)[:, 0:n], w[:, :], sq[:, k, :], start=(k == blocks[0]), stop=(k == blocks[-1]))
                m.then_inc(unit_done, 1)

            pe.wait_ge(squares_ready, 1)
            stat(UNIT["x_stat"], [(mean_d, hT, range(DB), T)])
            pe.wait_ge(mem_sq_ready, 2)
            stat(UNIT["mem_stat"], [(mean_d, mem_sq, range(DB), NM)])

            def project(name, pairs):
                with pe.Fori(0, pairs) as i:
                    for cg in range(2):
                        u = UNIT[name] + cg
                        start_unit(pe, u, i, 2)
                        for g in range(4):
                            t = TILE[name] + 4 * cg + g
                            wait_tile(pe, t, i)
                            for k in range(KT):
                                for b in range(4):
                                    m = mm(bank(u, b)[:, 0:T], tile_of(t)[:, k, b * P:(b + 1) * P], hT[:, KT * g + k, :],
                                           start=(g == 0 and k == 0), stop=(g == 3 and k == KT - 1))
                            m.then_inc(tile_used, 1)

            pe.wait_ge(h_ready, 1)
            project("w_in", 5)

            pe.wait_ge(wbd_loaded, 16 * 4)
            pe.wait_ge(xc_ready, 1)
            for h in range(2):
                for n in range(2):
                    u = UNIT["gates"] + 2 * h + n
                    start_unit(pe, u)
                    for b in range(HG):
                        m = mm(bank(u, b)[:, 0:XO], wbd[:, n, HG * h + b, :], xc[:, HG * h + b, :], start=True, stop=True)
                    m.then_inc(unit_done, 1)

            pe.wait_ge(m_ready, 1)
            for name in ("w_k", "w_v"):
                with pe.Fori(0, 2) as i:
                    for cg in range(2):
                        u = UNIT[name] + cg
                        start_unit(pe, u, i, 2)
                        for g in range(4):
                            t = TILE[name] + 4 * cg + g
                            wait_tile(pe, t, i)
                            for k in range(KT):
                                for c in range(2):
                                    m = mm(bank(u, c), mT[:, KT * g + k, c * P:(c + 1) * P], tile_of(t)[:, k, :],
                                           start=(g == 0 and k == 0), stop=(g == 3 and k == KT - 1))
                            m.then_inc(tile_used, 1)

            pe.wait_ge(squares_ready, 2)
            stat(UNIT["mix_stat"], [(mean_g, sq_mix, range(GB), T), (mean_g, sq_mix, range(GB, DB), T)])
            u = UNIT["states"]
            start_unit(pe, u)
            pe.wait_ge(states_ready, 1)
            for b in range(GB):
                t = nc.tensor.transpose(bank(u, b // 4)[0:NSTATE, b % 4 * P:b % 4 * P + P], states[:, b, :], ident[:, :])
            t.then_inc(unit_done, 1)

            pe.wait_ge(h_ready, 2)
            project("w_out", 2)
            pe.wait_ge(squares_ready, 3)
            stat(UNIT["xattn_stat"], [(mean_d, hT, range(DB), T)])
            pe.wait_ge(h_ready, 3)
            project("w_q", 2)

            def keys(u, t, i=None, step=0, per=8):
                for c in range(2):
                    start_unit(pe, u + c, i, step)
                    wait_tile(pe, t + c, i, per)
                    for b in range(DB):
                        m = nc.tensor.transpose(bank(u + c, b // 4)[:, b % 4 * P:(b % 4 + 1) * P],
                                                ring[:, (t + c) % SLOTS, b * P:(b + 1) * P], ident[:, :])
                    m.then_inc(tile_used, 1)

            for g in range(2):
                read_out(pe, UNIT["w_q"] + 2 + g)
            with pe.Fori(0, NB // 2) as i:
                for s in range(2):
                    u, t = UNIT["sample"] + 5 * s, TILE["cache"] + 4 * s
                    keys(u, t, i, 10)
                    start_unit(pe, u + 2, i, 10)
                    read_out(pe, u, i, 10)
                    read_out(pe, u + 1, i, 10)
                    for h in range(NH):
                        for k in range(HB):
                            m = mm(bank(u + 2, 0)[32 * h:32 * h + 32, 0:NM], qT[:, HB * h + k, TP:T], kT[:, HB * h + k, :],
                                   start=(k == 0), stop=(k == HB - 1))
                    m.then_inc(unit_done, 1)
                    start_unit(pe, u + 3, i, 10)
                    pe.wait_ge(probs_scaled, s + 1 + i * 2)
                    for c in range(2):
                        m = nc.tensor.transpose(bank(u + 3, 0)[:, c * P:(c + 1) * P], pr[:, 0, c * P:(c + 1) * P], ident[:, :])
                    m.then_inc(unit_done, 1)
                    start_unit(pe, u + 4, i, 10)
                    read_out(pe, u + 3, i, 10)
                    wait_tile(pe, t + 2, i)
                    wait_tile(pe, t + 3, i)
                    for b in range(DB):
                        for c in range(2):
                            m = mm(bank(u + 4, 0)[:, 32 * b:32 * b + 32], ring[:, (t + 2 + c) % SLOTS, b * P:(b + 1) * P],
                                   pT[:, c, 32 * (b // HB):32 * (b // HB) + 32], start=(c == 0), stop=(c == 1))
                    m.then_inc(tile_used, 2)

            u, t = UNIT["prompt"], TILE["prompt_kv"]
            keys(u, t)
            start_unit(pe, u + 2)
            read_out(pe, u)
            read_out(pe, u + 1)
            for c in range(2):
                for h in range(NH):
                    n = NH * c + h
                    for k in range(HB):
                        m = mm(bank(u + 2, n // 2)[:, n % 2 * NM:(n % 2 + 1) * NM], qT[:, HB * h + k, c * P:(c + 1) * P],
                               kT[:, HB * h + k, :], start=(k == 0), stop=(k == HB - 1))
            m.then_inc(unit_done, 1)
            start_unit(pe, u + 3)
            pe.wait_ge(probs_scaled, NB + 1)
            for mc in range(2):
                for h in range(NH):
                    for c in range(2):
                        n = 8 * mc + 2 * h + c
                        m = nc.tensor.transpose(bank(u + 3, n // 4)[:, n % 4 * P:(n % 4 + 1) * P],
                                                pr[:, NH * c + h, mc * P:(mc + 1) * P], ident[:, :])
            m.then_inc(unit_done, 1)
            read_out(pe, u + 3)
            for c in range(2):
                wait_tile(pe, t + 2 + c)
            for hf in range(2):
                start_unit(pe, u + 4 + hf)
                for b8 in range(8):
                    b = 8 * hf + b8
                    for c in range(2):
                        m = mm(bank(u + 4 + hf, b8 // 2)[:, b8 % 2 * TP:(b8 % 2 + 1) * TP],
                               ring[:, (t + 2 + c) % SLOTS, b * P:(b + 1) * P],
                               pT[:, c, TP * (b // HB):TP * (b // HB + 1)], start=(c == 0), stop=(c == 1))
                m.then_inc(*((tile_used, 2) if hf else (unit_done, 1)))
            for hf in range(2):
                read_out(pe, u + 4 + hf)
            project("w_o", 2)
            pe.wait_ge(squares_ready, 4)
            stat(UNIT["moe_stat"], [(mean_d, hT, range(DB), T)])

            pe.wait_ge(h_ready, 4)
            pe.wait_ge(wr_loaded, 16 * 4)
            u = UNIT["router"]
            start_unit(pe, u)
            for c in range(3):
                rows = P if c < 2 else NB * ST
                for k in range(DB):
                    m = mm(bank(u, c)[0:rows, 0:NG + NE], hT[:, k, c * P:c * P + rows], wr[:, k, :],
                           start=(k == 0), stop=(k == DB - 1))
            m.then_inc(unit_done, 1)
            for c in range(3):
                rows = P if c < 2 else NB * ST
                u = UNIT["h_tok"] + c
                start_unit(pe, u)
                for b in range(DB):
                    m = nc.tensor.transpose(bank(u, b // 4)[0:rows, b % 4 * P:(b % 4 + 1) * P],
                                            hT[:, b, c * P:c * P + rows], ident[:, :])
                m.then_inc(unit_done, 1)
            u = UNIT["places"]
            start_unit(pe, u)
            pe.wait_ge(consts_set, 8)
            pe.wait_ge(mask_ready, 1)
            for c in range(3):
                for k in range(c + 1):
                    mm(bank(u, c)[:, 0:NE], before[:, :] if k == c else ones[:, :], mask16[:, k, :],
                       start=(k == 0), stop=(k == c))
            for k in range(3):
                m = mm(bank(u, 3)[:, 0:NE], ones[:, :], mask16[:, k, :], start=(k == 0), stop=(k == 2))
            m.then_inc(unit_done, 1)

            def pick_unit(u, s, i):
                start_unit(pe, u, i, PU)
                for b in range(2):
                    for c in range(3):
                        rows = P if c < 2 else NB * ST
                        for h in range(2):
                            mm(bank(u, b)[C * h:C * h + C, :], pick[0:rows, s, c, 0:C],
                               h_tok[0:rows, c, RG * h + TW * b:RG * h + TW * (b + 1)], start=(c == 0), stop=(c == 2))
                for c in range(3):
                    rows = P if c < 2 else NB * ST
                    mm(bank(u, 2)[:, 0:1], pick[0:rows, s, c, :], job_gate[0:rows, s, c:c + 1], start=(c == 0), stop=(c == 2))
                for c in range(3):
                    rows = P if c < 2 else NB * ST
                    m = nc.tensor.transpose(bank(u, 3)[:, c * P:c * P + rows], pick[0:rows, s, c, :], ident[0:rows, 0:rows])
                m.then_inc(unit_done, 1)

            def turn_unit(u, picked, i):
                start_unit(pe, u, i, PU)
                read_out(pe, picked, i, PU)
                for j in range(GB):
                    m = nc.tensor.transpose(bank(u, j // 4)[:, j % 4 * P:(j % 4 + 1) * P],
                                            x_half[:, j // 4, j % 4 * P:(j % 4 + 1) * P], ident[:, :])
                m.then_inc(unit_done, 1)

            def branch_unit(u, turned, t, i):
                start_unit(pe, u, i, PU)
                read_out(pe, turned, i, PU)
                for g in range(4):
                    wait_tile(pe, t + 2 * g, i, 24)
                    wait_tile(pe, t + 2 * g + 1, i, 24)
                    for k in range(KT):
                        b = KT * g + k
                        for n in range(2):
                            m = mm(bank(u, 0)[C * n:C * n + C, :], xe[:, b % GB, b // GB, :], tile_of(t + 2 * g + n)[:, k, :],
                                   start=(b == 0), stop=(b == DB - 1))
                    m.then_inc(tile_used, 2)

            def pair(i, last):
                for s in range(2):
                    end = last and s == 1
                    u, t = UNIT["moe"] + 3 + 9 * s, TILE["moe"] + 12 * s
                    uP, uA, uQ, uD, uB, uS = (u, u + 1, u + 2, u + 3, u + 4, u + 5) if not end else (0, u, 0, u + 1, 0, u + 2)
                    if not end:
                        pe.wait_ge(pick_ready, s + 2 + i * 2)
                        pick_unit(uP, 1 - s, i)
                    start_unit(pe, uA, i, PU)
                    read_out(pe, u - 1, i, PU)
                    for k in range(KT):
                        m = mm(bank(uA, 0)[:, k * C:(k + 1) * C], act_nat[0:C, k * P:(k + 1) * P], ident[0:C, 0:C],
                               start=True, stop=True)
                    m.then_inc(unit_done, 1)
                    if not end:
                        turn_unit(uQ, uP, i)
                    start_unit(pe, uD, i, PU)
                    read_out(pe, uA, i, PU)
                    for b in range(2):
                        wait_tile(pe, t + 8 + 2 * b, i, 24)
                        wait_tile(pe, t + 9 + 2 * b, i, 24)
                        for k in range(KT):
                            for h in range(2):
                                m = mm(bank(uD, b)[C * h:C * h + C, :], actT[:, k, :], tile_of(t + 8 + 2 * b + h)[:, k, :],
                                       start=(k == 0), stop=(k == KT - 1))
                        m.then_inc(tile_used, 2)
                    if not end:
                        branch_unit(uB, uQ, t + 12, i)
                    read_out(pe, uD, i, PU)
                    for q in range(4):
                        start_unit(pe, uS + q, i, PU)
                        for jj in range(2):
                            j = 2 * q + jj
                            for h in range(2):
                                m = mm(bank(uS + q, 2 * h + jj)[:, 0:T], y_half[C * h:C * h + C, j * P:(j + 1) * P],
                                       spread[C * h:C * h + C, s, :], start=True, stop=True)
                        m.then_inc(unit_done, 1)

            for c in range(3):
                read_out(pe, UNIT["h_tok"] + c)
            pe.wait_ge(jobs_ready, 2)
            n_loops = pe.value_load(loops[0:1, 0:1], min_val=NE // 2 - 1, max_val=NJ // 2 - 1)
            pe.wait_ge(pick_ready, 1)
            pick_unit(UNIT["moe"], 0, None)
            turn_unit(UNIT["moe"] + 1, UNIT["moe"], None)
            branch_unit(UNIT["moe"] + 2, UNIT["moe"] + 1, TILE["moe"], None)
            with pe.Fori(0, n_loops) as i:
                pair(i, False)
            pair(n_loops, True)

            pe.wait_ge(squares_ready, 5)
            stat(UNIT["final_stat"], [(mean_d, hT, range(DB), T)], n_loops, PU)
            pe.wait_ge(h_ready, 5)
            for c in range(3):
                rows = P if c < 2 else NB * ST
                u = UNIT["y"] + c
                start_unit(pe, u, n_loops, PU)
                for b in range(DB):
                    m = nc.tensor.transpose(bank(u, b // 4)[0:rows, b % 4 * P:(b % 4 + 1) * P],
                                            hT[:, b, c * P:c * P + rows], ident[:, :])
                m.then_inc(unit_done, 1)

        @block.scalar
        def _(act):
            step = Count(act_step)
            fn, copy = nc.scalar.activation, nc.scalar.copy

            u = UNIT["x"] + 1
            after_event(act, EVENT["x"] + 1)
            copy(quads(xT[:, :, P:2 * P]), from_banks(u)).then_inc(half_free[u % 2], 2)
            for c in range(2):
                u = UNIT["mem"] + c
                after_event(act, EVENT["mem"] + c)
                copy(quads(mT[:, :, c * P:(c + 1) * P]), from_banks(u)).then_inc(half_free[u % 2], 2)
                read_out(act, u)
                fn(mem_sq[:, :, c * P:(c + 1) * P], mT[:, :, c * P:(c + 1) * P], ACT.Square).then_inc(mem_sq_ready, 1)
            u = UNIT["pack"]
            after_event(act, EVENT["pack"])
            copy(vec[:, :, :].rearrange("p (b k) n -> p b k n", k=4), from_banks(u, NROWS)[:, 0:2]
                 ).then_inc(half_free[u % 2], 2)
            act.wait_ge(lam_in, 1)
            fn(small[:, 1, :], small[:, 0, :], ACT.Exp, scale=-1.0)
            fn(consts[:, 2:3], consts[:, 1:2], ACT.Exp).then_inc(lam_exp, 1)

            def root(name, dst, src, i=None):
                after_event(act, EVENT[name], i, PE_EVENTS)
                fn(dst, src, ACT.Sqrt, bias=consts[:, 0:1]).then_inc(half_free[UNIT[name] % 2], 2)

            root("x_stat", rstd[:, 0, :], bank(UNIT["x_stat"], 0)[:, 0:T])
            root("mem_stat", rstd[:, 1, 0:NM], bank(UNIT["mem_stat"], 0)[:, 0:NM])

            def to_padded(dst, u, g, lead):
                copy(dst[:, 4 * g:4 * g + 4, lead:lead + TP], half(u, TP)).then_inc(half_free[u % 2], 1)
                for b in range(4):
                    m = copy(sample_cols(dst[:, 4 * g + b, lead + TP:], lead, ST),
                             bank(u, b)[:, TP:T].rearrange("p (b t) -> p b t", t=ST))
                m.then_inc(half_free[u % 2], 1)

            act.wait_ge(pads_ready, 1)
            for g in range(2):
                after_tile(act, TILE["w_in"] + 4 * g + 3)
                to_padded(rgx, UNIT["w_in"] + g, g, CW - 1)
            for g in range(2):
                u = UNIT["w_in"] + 2 + g
                after_tile(act, TILE["w_in"] + 4 * (2 + g) + 3)
                fn(gelu[:, 4 * g:4 * g + 4, :], half(u), ACT.Gelu_apprx_tanh).then_inc(half_free[u % 2], 2)
            for g in range(2):
                after_tile(act, TILE["w_in"] + 4 * (6 + g) + 3)
                to_padded(usc, UNIT["w_in"] + 6 + g, g, SW - 1)

            for h in range(2):
                if h:
                    act.wait_ge(scanned, 1)
                for n, (dst, bias) in enumerate(((gr, "rg_b_a"), (gi, "rg_b_x"))):
                    u = UNIT["gates"] + 2 * h + n
                    after_event(act, EVENT["gates"] + 2 * h + n)
                    for b in range(HG):
                        c = ROWS[bias]
                        m = fn(dst[:, b, :], bank(u, b)[:, 0:XO], ACT.Sigmoid, bias=vec[:, HG * h + b, c:c + 1])
                    m.then_inc(half_free[u % 2], 2)
                act.wait_ge(clamp_ready, h + 1)
                fn(gE[:, :, :], gE[:, :, :], ACT.Exp).then_inc(exp_ready, 1)
                act.wait_ge(mult_in_ready, h + 1)
                fn(gr[:, :, :], gr[:, :, :], ACT.Sqrt, scale=-1.0).then_inc(mult_ready, 1)

            for n, name in enumerate(("w_k", "w_v")):
                for g in range(4):
                    u = UNIT[name] + g
                    after_tile(act, TILE[name] + 4 * g + 3)
                    if n or g >= 2:
                        act.wait_ge(kv_stored[g % 2], 16 * ((4 * n + g) // 2))
                    copy(kv_stage[:, g % 2, :, :], half(u, TW, 2)).then_inc(half_free[u % 2], 2)
            u = UNIT["mix_stat"]
            after_event(act, EVENT["mix_stat"])
            fn(rstd[:, :, :], half(u, T, 2), ACT.Sqrt, bias=consts[:, 0:1]).then_inc(half_free[u % 2], 2)
            u = UNIT["states"]
            after_event(act, EVENT["states"])
            act.wait_ge(kv_stored[0], 16 * 4)
            act.wait_ge(kv_stored[1], 16 * 4)
            copy(states_nat[0:NSTATE, :].rearrange("p (a b) -> p a b", a=2), half(u, 512, 2)[0:NSTATE]
                 ).then_inc(half_free[u % 2], 2)
            root("xattn_stat", rstd[:, 0, :], bank(UNIT["xattn_stat"], 0)[:, 0:T])

            for g in range(4):
                u = UNIT["w_q"] + g
                after_tile(act, TILE["w_q"] + 4 * g + 3)
                copy(qT[:, 4 * g:4 * g + 4, :], half(u)).then_inc(half_free[u % 2], 2)

            with act.Fori(0, NB // 2) as i:
                for s in range(2):
                    u = UNIT["sample"] + 5 * s
                    after_tile(act, TILE["cache"] + 4 * s, i, 8)
                    copy(quads(kT[:, :, 0:P]), from_banks(u)).then_inc(half_free[u % 2], 2)
                    act.wait_ge(max_ready, s + 1 + i * 2)
                    fn(pr[:, 0, :], bank(u + 2, 0)[:, 0:NM], ACT.Exp, bias=st[:, 1, 0:1], scale=SCALE,
                       accum_out=st[:, 2, 0:1]).then_inc(half_free[u % 2], 2)
            u = UNIT["prompt"]
            after_tile(act, TILE["prompt_kv"])
            copy(quads(kT[:, :, 0:P]), from_banks(u)).then_inc(half_free[u % 2], 2)
            act.wait_ge(max_ready, NB + 1)
            for n in range(2 * NH):
                m = fn(pr[:, n, :], bank(u + 2, n // 2)[:, n % 2 * NM:(n % 2 + 1) * NM], ACT.Exp,
                       bias=st[:, 1, n:n + 1], scale=SCALE, accum_out=st[:, 2, n:n + 1])
            m.then_inc(half_free[u % 2], 2)
            root("moe_stat", rstd[:, 0, :], bank(UNIT["moe_stat"], 0)[:, 0:T])

            act.wait_ge(gate_in, 1)
            fn(G(4), G(3), ACT.Exp).then_inc(gate_exp, 1)
            act.wait_ge(gate_in, 2)
            fn(G(17, 1), G(16, 1), ACT.Exp).then_inc(gate_exp, 1)
            for c in range(3):
                rows = P if c < 2 else NB * ST
                u = UNIT["h_tok"] + c
                after_event(act, EVENT["h_tok"] + c)
                copy(h_tok[0:rows, c, :].rearrange("p (a b) -> p a b", a=4), half(u, 512)[0:rows]
                     ).then_inc(half_free[u % 2], 2)

            act.wait_ge(jobs_ready, 2)
            n_loops = act.value_load(loops[0:1, 0:1], min_val=NE // 2 - 1, max_val=NJ // 2 - 1)

            def picked(u, s, i, e):
                after_event(act, e, i, PE_EVENTS)
                copy(place_gate[:, s, 0:1], bank(u, 2)[:, 0:1])
                copy(spread[:, s, :], bank(u, 3)[:, 0:T])
                copy(x_half[:, :, :], half(u, TW, 2)).then_inc(half_free[u % 2], 2)

            def turned(u, i, e):
                after_event(act, e, i, PE_EVENTS)
                copy(xe[:, :, :, :].rearrange("p (a j) h c -> p a (j h c)", a=2), half(u, TW, 2)
                     ).then_inc(half_free[u % 2], 2)

            def gate_branch(u, t, i):
                after_tile(act, t + 7, i, 24)
                fn(silu[0:C, :], bank(u, 0)[0:C, :], ACT.Silu).then_inc(silu_ready, 1)

            def pair(i, last):
                for s in range(2):
                    end = last and s == 1
                    u, t, e = UNIT["moe"] + 3 + 9 * s, TILE["moe"] + 12 * s, EVENT["moe"] + 2 + 7 * s
                    if not end:
                        picked(u, 1 - s, i, e)
                        turned(u + 2, i, e + 2)
                    d = u + (1 if end else 3)
                    after_tile(act, t + 11, i, 24)
                    fn(y_half[:, :].rearrange("p (a b) -> p a b", a=2), half(d, TW, 2), ACT.Copy,
                       scale=place_gate[:, s, 0:1]).then_inc(half_free[d % 2], 2)
                    if not end:
                        gate_branch(u + 4, t + 12, i)

            picked(UNIT["moe"], 0, None, EVENT["moe"])
            turned(UNIT["moe"] + 1, None, EVENT["moe"] + 1)
            gate_branch(UNIT["moe"] + 2, TILE["moe"], None)
            with act.Fori(0, n_loops) as i:
                pair(i, False)
            pair(n_loops, True)
            root("final_stat", rstd[:, 0, :], bank(UNIT["final_stat"], 0)[:, 0:T], n_loops)
            for c in range(3):
                rows = P if c < 2 else NB * ST
                u = UNIT["y"] + c
                after_event(act, EVENT["y"] + c, n_loops, PE_EVENTS)
                copy(y_nat[0:rows, c, :].rearrange("p (a b) -> p a b", a=4), half(u, 512)[0:rows]
                     ).then_inc(half_free[u % 2], 2)

        @block.vector
        def _(dve):
            step = Count(dve_step)
            v = nc.vector
            tt, ts, stt = v.tensor_tensor, v.tensor_scalar, v.scalar_tensor_tensor

            def then(ins):
                step.tick(ins)
                dve.wait_ge(dve_step, step.value())

            for c, rows in ((0, P), (2, NB * ST)):
                u = UNIT["x"] + c
                after_event(dve, EVENT["x"] + c)
                v.tensor_copy(quads(xT[:, :, c * P:c * P + rows]), from_banks(u, rows)).then_inc(half_free[u % 2], 2)
            for c in range(3):
                read_out(dve, UNIT["x"] + c)
            tt(hT[:, :, :], xT[:, :, :], xT[:, :, :], ALU.mult).then_inc(squares_ready, 1)

            read_out(dve, UNIT["pack"])
            lam = vec[:, :, ROWS["rg_lambda"]]
            stt(out=small[:, 0, :], in0=lam, scalar=-1.0, in1=lam, op0=ALU.mult, op1=ALU.max).then_inc(lam_in, 1)

            def apply_norm(name, u, src, dst, blocks, rs, n, ready=None, i=None):
                read_out(dve, u, i, PU)
                then(v.reciprocal(rs, rs))
                for b in blocks:
                    m = stt(out=dst[:, b, 0:n], in0=src[:, b, 0:n], scalar=gain(name, b % (2 * GB)), in1=rs,
                            op0=ALU.mult, op1=ALU.mult)
                if ready is not None:
                    m.then_inc(ready, 1)

            apply_norm("norm_mix", UNIT["x_stat"], xT, hT, range(DB), rstd[:, 0, :], T, h_ready)
            apply_norm("norm_mem", UNIT["mem_stat"], mT, mT, range(DB), rstd[:, 1, 0:NM], NM, m_ready)

            v.memset(rgx[:, :, 0:CW - 1], 0.0)
            v.memset(usc[:, :, 0:SW - 1], 0.0)
            for b in range(GB):
                for dst, lead, rows in ((rgx, CW - 1, ROWS["state_rglru_conv"]), (usc, SW - 1, ROWS["state_sconv"])):
                    m = v.tensor_copy(
                        dst[:, b, lead + TP:].rearrange("p (b t) -> p b t", t=lead + ST)[:, :, 0:lead],
                        vec[:, b, rows:rows + NB * lead].rearrange("p (b t) -> p b t", t=lead))
            m.then_inc(pads_ready, 1)

            S = [small[:, n, :] for n in range(8)]
            dve.wait_ge(lam_exp, 1)
            then(ts(S[2], S[1], 2.0, None, ALU.add))
            then(v.reciprocal(S[2], S[2]))
            then(tt(S[3], S[1], S[2], ALU.mult))
            then(tt(S[4], S[3], S[3], ALU.mult))
            then(ts(S[5], S[4], 1.0 / 17, None, ALU.mult))
            for n in (15, 13, 11, 9, 7, 5, 3):
                then(stt(out=S[5], in0=S[5], scalar=1.0 / n, in1=S[4], op0=ALU.add, op1=ALU.mult))
            then(stt(out=S[5], in0=S[5], scalar=1.0, in1=S[3], op0=ALU.add, op1=ALU.mult))
            then(ts(S[7], lam, -1.0, 0.0, ALU.mult, ALU.max))
            then(stt(out=S[5], in0=S[5], scalar=2.0, in1=S[7], op0=ALU.mult, op1=ALU.add))
            then(ts(S[6], S[5], -RG_C, None, ALU.mult))

            def conv(dst, src, n, w, taps, bias):
                for k in range(taps):
                    for b in range(GB):
                        wk = vec[:, b, ROWS[w] + k:ROWS[w] + k + 1]
                        if k:
                            m = stt(out=dst[:, b, :], in0=src[:, b, k:k + n], scalar=wk, in1=dst[:, b, :],
                                    op0=ALU.mult, op1=ALU.add)
                        elif bias:
                            m = ts(dst[:, b, :], src[:, b, 0:n], wk, vec[:, b, ROWS[bias]:ROWS[bias] + 1],
                                   ALU.mult, ALU.add)
                        else:
                            m = ts(dst[:, b, :], src[:, b, 0:n], wk, None, ALU.mult)
                    if k < taps - 1:
                        then(m)
                return m

            for g in range(2):
                read_out(dve, UNIT["w_in"] + g)
            conv(xc, rgx, XO, "rg_conv_w", CW, "rg_conv_b").then_inc(xc_ready, 1)
            v.tensor_copy(states[:, :, S_CONV:S_CONV + CW - 1], rgx[:, :, TP:TP + CW - 1])
            for b in range(GB):
                m = v.tensor_copy(states[:, b, S_CONV + CW - 1:S_H].rearrange("p (b t) -> p b t", t=CW - 1),
                                  sample_cols(rgx[:, b, CW - 1 + TP:], CW - 1, CW - 1))
            then(m)

            for g in range(2):
                u = UNIT["w_in"] + 4 + g
                after_tile(dve, TILE["w_in"] + 4 * (4 + g) + 3)
                v.tensor_copy(scb[:, 4 * g:4 * g + 4, :], half(u)).then_inc(half_free[u % 2], 2)
            for g in range(2):
                u = UNIT["w_in"] + 8 + g
                read_out(dve, UNIT["w_in"] + 6 + g)
                after_tile(dve, TILE["w_in"] + 4 * (8 + g) + 3)
                x = usc[:, 4 * g:4 * g + 4, SW - 1:SW - 1 + TP]
                tt(x, x, half(u, TP), ALU.mult)
                for b in range(4):
                    x = sample_cols(usc[:, 4 * g + b, SW - 1 + TP:], SW - 1, ST)
                    m = tt(x, x, bank(u, b)[:, TP:T].rearrange("p (b t) -> p b t", t=ST), ALU.mult)
                m.then_inc(half_free[u % 2], 2)
            for g in range(2):
                read_out(dve, UNIT["w_in"] + 8 + g)
            v.tensor_copy(states[:, :, S_SC:S_SC + SW - 1], usc[:, :, TP:TP + SW - 1])
            for b in range(GB):
                v.tensor_copy(states[:, b, S_SC + SW - 1:NSTATE].rearrange("p (b t) -> p b t", t=SW - 1),
                              sample_cols(usc[:, b, SW - 1 + TP:], SW - 1, SW - 1))

            for h in range(2):
                blocks = range(HG * h, HG * h + HG)
                read_out(dve, UNIT["gates"] + 2 * h)
                read_out(dve, UNIT["gates"] + 2 * h + 1)
                for b in range(HG):
                    m = ts(gr[:, b, :], gr[:, b, :], small[:, 6, HG * h + b:HG * h + b + 1], None, ALU.mult)
                then(m)
                ts(gE[:, :, :], gr[:, :, :], -0.5, None, ALU.min).then_inc(clamp_ready, 1)
                then(ts(gr[:, :, :], gr[:, :, :], -0.5, None, ALU.max))
                then(ts(ge[:, :, :], gr[:, :, :], 1.0 / math.factorial(8), None, ALU.mult))
                for n in range(7, 0, -1):
                    then(stt(out=ge[:, :, :], in0=ge[:, :, :], scalar=1.0 / math.factorial(n), in1=gr[:, :, :],
                             op0=ALU.add, op1=ALU.mult))
                dve.wait_ge(exp_ready, h + 1)
                then(stt(out=ge[:, :, :], in0=gE[:, :, :], scalar=consts[:, 2:3], in1=ge[:, :, :],
                         op0=ALU.subtract, op1=ALU.add))
                stt(out=gr[:, :, :], in0=ge[:, :, :], scalar=2.0, in1=ge[:, :, :], op0=ALU.add, op1=ALU.mult
                    ).then_inc(mult_in_ready, 1)
                then(ts(gE[:, :, :], ge[:, :, :], 1.0, None, ALU.add))
                then(tt(gi[:, :, :], gi[:, :, :], xc[:, HG * h:HG * h + HG, :], ALU.mult))
                dve.wait_ge(mult_ready, h + 1)
                then(tt(gi[:, :, :], gi[:, :, :], gr[:, :, :], ALU.mult))
                for b in range(HG):
                    r = ROWS["state_rglru_h"]
                    at = lambda x: x[:, b, TP:].rearrange("p (b t) -> p b t", t=CW - 1 + ST)[:, :, CW - 2:CW - 1]
                    v.memset(at(gE), 0.0)
                    m = v.tensor_copy(at(gi), vec[:, HG * h + b, r:r + NB].rearrange("p (b t) -> p b t", t=1))
                then(m)
                for b in range(HG):
                    m = v.tensor_tensor_scan(xc[:, HG * h + b, :], gE[:, b, :], gi[:, b, :], 0.0, ALU.mult, ALU.add)
                m.then_inc(scanned, 1)
            dve.wait_ge(scanned, 2)
            v.tensor_copy(states[:, :, S_H:S_H + 1], xc[:, :, TP - 1:TP])
            for b in range(GB):
                m = v.tensor_copy(states[:, b, S_H + 1:S_SC].rearrange("p (b t) -> p b t", t=1),
                                  sample_cols(xc[:, b, TP:], CW - 1, 1))
            m.then_inc(states_ready, 1)
            tt(hT[:, 0:GB, 0:TP], xc[:, :, 0:TP], gelu[:, :, 0:TP], ALU.mult)
            for b in range(GB):
                tt(hT[:, b, TP:T].rearrange("p (b t) -> p b t", t=ST), sample_cols(xc[:, b, TP:], CW - 1, ST),
                   gelu[:, b, TP:T].rearrange("p (b t) -> p b t", t=ST), ALU.mult)
            then(conv(uc, usc, UO, "sc_conv_w", SW, None))
            tt(hT[:, GB:DB, 0:TP], uc[:, :, 0:TP], scb[:, :, 0:TP], ALU.mult)
            for b in range(GB):
                m = tt(hT[:, GB + b, TP:T].rearrange("p (b t) -> p b t", t=ST), sample_cols(uc[:, b, TP:], SW - 1, ST),
                       scb[:, b, TP:T].rearrange("p (b t) -> p b t", t=ST), ALU.mult)
            then(m)
            tt(sq_mix[:, :, :], hT[:, :, :], hT[:, :, :], ALU.mult).then_inc(squares_ready, 1)
            read_out(dve, UNIT["mix_stat"])
            then(v.reciprocal(rstd[:, :, :], rstd[:, :, :]))
            for n, name in enumerate(("norm_rg_out", "norm_sc_out")):
                for b in range(GB):
                    x = hT[:, GB * n + b, :]
                    m = stt(out=x, in0=x, scalar=vec[:, b, ROWS[name]:ROWS[name] + 1], in1=rstd[:, n, :],
                            op0=ALU.mult, op1=ALU.mult)
            m.then_inc(h_ready, 1)

            def add_residual(name):
                for g in range(4):
                    u = UNIT[name] + g
                    after_tile(dve, TILE[name] + 4 * g + 3)
                    x = xT[:, 4 * g:4 * g + 4, :]
                    tt(x, x, half(u), ALU.add).then_inc(half_free[u % 2], 2)
                read_out(dve, UNIT[name] + 2)
                read_out(dve, UNIT[name] + 3)
                tt(hT[:, :, :], xT[:, :, :], xT[:, :, :], ALU.mult).then_inc(squares_ready, 1)

            add_residual("w_out")
            apply_norm("norm_xattn", UNIT["xattn_stat"], xT, hT, range(DB), rstd[:, 0, :], T, h_ready)

            with dve.Fori(0, NB // 2) as i:
                step.enter(i, 4)
                for s in range(2):
                    u, e = UNIT["sample"] + 5 * s, EVENT["sample"] + 2 * s
                    after_tile(dve, TILE["cache"] + 4 * s + 1, i, 8)
                    v.tensor_copy(quads(kT[:, :, P:NM]), from_banks(u + 1)).then_inc(half_free[(u + 1) % 2], 2)
                    after_event(dve, e, i, 4)
                    then(v.tensor_reduce(st[:, 0, 0:1], bank(u + 2, 0)[:, 0:NM], AX.X, ALU.max))
                    ts(st[:, 1, 0:1], st[:, 0, 0:1], -SCALE, None, ALU.mult).then_inc(max_ready, 1)
                    read_out(dve, u + 2, i, 10)
                    then(v.reciprocal(st[:, 3, 0:1], st[:, 2, 0:1]))
                    ts(pr[:, 0, :], pr[:, 0, :], st[:, 3, 0:1], None, ALU.mult).then_inc(probs_scaled, 1)
                    after_event(dve, e + 1, i, 4)
                    v.tensor_copy(pT[:, :, 0:P], bank(u + 3, 0)[:, 0:NM].rearrange("p (c n) -> p c n", c=2)
                                  ).then_inc(half_free[(u + 3) % 2], 2)
                    after_tile(dve, TILE["cache"] + 4 * s + 3, i, 8)
                    v.tensor_copy(
                        oT[:, :, bass.ds(i * (2 * ST) + (TP + ST * s), ST)],
                        bank(u + 4, 0).rearrange("p (b n) -> p b n", n=NB * ST)[:, :, bass.ds(i * (2 * ST) + ST * s, ST)]
                    ).then_inc(half_free[(u + 4) % 2], 2)
                step.leave(NB // 2)
            u, e = UNIT["prompt"], EVENT["prompt"]
            after_tile(dve, TILE["prompt_kv"] + 1)
            v.tensor_copy(quads(kT[:, :, P:NM]), from_banks(u + 1)).then_inc(half_free[(u + 1) % 2], 2)
            after_event(dve, e)
            scores = half(u + 2, 512).rearrange("p b (two n) -> p b two n", two=2)
            then(v.tensor_reduce(st[:, 0, :].rearrange("p (a b) -> p a b", a=4), scores, AX.X, ALU.max))
            ts(st[:, 1, :], st[:, 0, :], -SCALE, None, ALU.mult).then_inc(max_ready, 1)
            read_out(dve, u + 2)
            then(v.reciprocal(st[:, 3, :], st[:, 2, :]))
            tt(pr[:, :, :], pr[:, :, :], st[:, 3, :].unsqueeze(2).broadcast_to([P, 2 * NH, NM]), ALU.mult
               ).then_inc(probs_scaled, 1)
            after_event(dve, e + 1)
            v.tensor_copy(pT[:, :, :].rearrange("p c n -> p (c n)").rearrange("p (b n) -> p b n", b=4), half(u + 3, 512)
                          ).then_inc(half_free[(u + 3) % 2], 2)
            for hf in range(2):
                if hf:
                    after_tile(dve, TILE["prompt_kv"] + 3)
                else:
                    after_event(dve, e + 2)
                v.tensor_copy(oT[:, 8 * hf:8 * hf + 8, 0:TP].rearrange("p (b two) n -> p b two n", two=2),
                              half(u + 4 + hf, 512).rearrange("p b (two n) -> p b two n", two=2)
                              ).then_inc(half_free[(u + 4 + hf) % 2], 2)
            add_residual("w_o")
            apply_norm("norm_moe", UNIT["moe_stat"], xT, hT, range(DB), rstd[:, 0, :], T, h_ready)

            def over(x, n):
                return x.broadcast_to([P, 3, n])

            def first_max(x, top, onehot, tmp):
                then(v.tensor_reduce(top, x, AX.X, ALU.max))
                then(tt(tmp, x, over(top, 4), ALU.is_equal))
                then(tt(tmp, tmp, w4.unsqueeze(1).broadcast_to([P, 3, 4]), ALU.mult))
                then(v.tensor_reduce(G(15, 1), tmp, AX.X, ALU.max))
                then(tt(onehot, tmp, over(G(15, 1), 4), ALU.is_equal))

            for n in range(4):
                v.memset(w4[:, n:n + 1], 4.0 - n)
            then(v.memset(lg[:, :, :], 0.0))
            dve.wait_ge(wr_loaded, 16 * 4)
            u = UNIT["router"]
            after_event(dve, EVENT["router"])
            for c in range(3):
                rows = P if c < 2 else NB * ST
                m = tt(lg[0:rows, c, :], bank(u, c)[0:rows, 0:NG + NE], rbias[0:rows, :], ALU.add)
            m.then_inc(half_free[u % 2], 2)
            read_out(dve, u)
            first_max(lg[:, :, 0:NG], G(0, 1), G(1), G(2))
            tt(G(3), lg[:, :, 0:NG], over(G(0, 1), 4), ALU.subtract).then_inc(gate_in, 1)
            by_expert = gt[:, :, 4 * 5:4 * 9].rearrange("p c (g j) -> p c g j", g=NG)
            for c in range(3):
                m = tt(by_expert[:, c], lg[:, c, NG:].rearrange("p (g j) -> p g j", g=NG),
                       G(1)[:, c].unsqueeze(2).broadcast_to([P, NG, EG]), ALU.mult)
            then(m)
            for c in range(3):
                m = v.tensor_reduce(G(9)[:, c], by_expert[:, c].rearrange("p g j -> p j g"), AX.X, ALU.add)
            then(m)
            first_max(G(9), G(10, 1), G(11), G(2))
            then(stt(out=G(12), in0=G(11), scalar=-1e30, in1=G(9), op0=ALU.mult, op1=ALU.add))
            first_max(G(12), G(13, 1), G(14), G(2))
            tt(G(16, 1), G(13, 1), G(10, 1), ALU.subtract).then_inc(gate_in, 1)
            dve.wait_ge(gate_exp, 2)
            then(tt(G(2), G(11), G(14), ALU.add))
            for c in range(3):
                m = tt(mask16[:, c, :].rearrange("p (g j) -> p g j", g=NG), G(1)[:, c].unsqueeze(2).broadcast_to([P, NG, EG]),
                       G(2)[:, c].unsqueeze(1).broadcast_to([P, NG, EG]), ALU.mult)
            then(m)
            v.memset(mask16[NB * ST:64, 2, :], 0.0)
            v.memset(mask16[64:P, 2, :], 0.0).then_inc(mask_ready, 1)
            then(v.tensor_reduce(G(18, 1), G(4), AX.X, ALU.add))
            then(stt(out=G(18, 1), in0=G(17, 1), scalar=1.0, in1=G(18, 1), op0=ALU.add, op1=ALU.mult))
            then(v.reciprocal(G(18, 1), G(18, 1)))
            then(tt(G(11), G(11), over(G(18, 1), 4), ALU.mult))
            then(tt(G(18, 1), G(18, 1), G(17, 1), ALU.mult))
            then(tt(G(14), G(14), over(G(18, 1), 4), ALU.mult))
            then(tt(G(11), G(11), G(14), ALU.add))
            for c in range(3):
                m = tt(gate16[:, c, :].rearrange("p (g j) -> p g j", g=NG), G(1)[:, c].unsqueeze(2).broadcast_to([P, NG, EG]),
                       G(11)[:, c].unsqueeze(1).broadcast_to([P, NG, EG]), ALU.mult)
            then(m)

            u = UNIT["places"]
            after_event(dve, EVENT["places"])
            for c in range(3):
                m = stt(out=posm[:, c, :], in0=bank(u, c)[:, 0:NE], scalar=4.0 * NOWHERE, in1=mask16[:, c, :],
                        op0=ALU.add, op1=ALU.mult)
            then(m)
            v.tensor_copy(tab[:, 0, :], bank(u, 3)[:, 0:NE]).then_inc(half_free[u % 2], 2)
            ts(posm[:, :, :], posm[:, :, :], -4.0 * NOWHERE, None, ALU.add)
            read_out(dve, u)
            counts, jobs, ends, onesr = (tab[:, n, :] for n in range(4))
            v.memset(onesr, 1.0)
            then(ts(jobs, counts, float(C), 1.0, ALU.is_gt, ALU.add))
            for n in range(2, -(-T // C)):
                then(stt(out=jobs, in0=counts, scalar=float(C * n), in1=jobs, op0=ALU.is_gt, op1=ALU.add))
            then(v.tensor_tensor_scan(ends, onesr, jobs, 0.0, ALU.mult, ALU.add))
            dve.wait_ge(consts_set, 8)
            iota_g = place_iota[:, 0, 0:NJ]
            over_e = ends.unsqueeze(1).broadcast_to([P, NJ, NE])
            then(tt(cmp[:, :, :], over_e, iota_g.unsqueeze(2).broadcast_to([P, NJ, NE]), ALU.is_le))
            then(v.tensor_reduce(jt[:, 0, :], cmp[:, :, :], AX.X, ALU.add))
            then(tt(cmp[:, :, :], cmp[:, :, :], jobs.unsqueeze(1).broadcast_to([P, NJ, NE]), ALU.mult))
            then(v.tensor_reduce(jt[:, 1, :], cmp[:, :, :], AX.X, ALU.add))
            then(tt(jt[:, 2, :], iota_g, jt[:, 1, :], ALU.subtract))
            then(ts(jt[:, 3, :], jt[:, 0, :], float(NE), float(NOWHERE), ALU.is_ge, ALU.mult))
            then(stt(out=job_first, in0=jt[:, 2, :], scalar=float(C), in1=jt[:, 3, :], op0=ALU.mult, op1=ALU.add))
            then(ts(jt[:, 0, :], jt[:, 0, :], float(NE - 1), None, ALU.min))
            v.tensor_copy(expert_of[0:1, :], jt[0:1, 0, :]).then_inc(jobs_ready, 1)
            then(ts(jt[:, 2, 0:NJ // 2], iota_g[:, 0:NJ // 2], 2.0, ends[:, NE - 1:NE], ALU.mult, ALU.is_lt))
            then(v.tensor_reduce(jt[:, 4, 0:1], jt[:, 2, 1:NJ // 2], AX.X, ALU.add))
            v.tensor_copy(loops[0:1, 0:1], jt[0:1, 4, 0:1]).then_inc(jobs_ready, 1)
            dve.wait_ge(jobs_ready, 2)
            n_loops = dve.value_load(loops[0:1, 0:1], min_val=NE // 2 - 1, max_val=NJ // 2 - 1)

            def make_picks(s, g):
                if isinstance(g, int) and g == 0:
                    e, first = 0, job_first[:, 0:1]
                    cols = lambda x: x[:, :, 0]
                else:
                    e = dve.value_load(expert_of[0:1, bass.ds(g, 1)], min_val=0, max_val=NE - 1)
                    first = job_first[:, bass.ds(g, 1)]
                    cols = lambda x: x[:, :, bass.ds(e, 1)].rearrange("p c o -> p (c o)")
                v.tensor_copy(job_gate[:, s, 0:3], cols(gate16))
                then(ts(shifted[:, s, 0:3], cols(posm), first, None, ALU.subtract))
                for c in range(3):
                    m = ts(pick[:, s, c, :], place_iota[:, :, :].rearrange("p a c -> p (a c)"), shifted[:, s, c:c + 1], None,
                           ALU.is_equal)
                m.then_inc(pick_ready, 1)

            def product(u, t, n, i):
                after_tile(dve, t + 7, i, 24)
                dve.wait_ge(silu_ready, plus(n, i, 2))
                tt(act_nat[0:C, :], silu[0:C, :], bank(u, 0)[C:2 * C, :], ALU.mult).then_inc(half_free[u % 2], 2)

            def pair(i, last):
                for s in range(2):
                    end = last and s == 1
                    u, t, e = UNIT["moe"] + 3 + 9 * s, TILE["moe"] + 12 * s, EVENT["moe"] + 2 + 7 * s
                    uA, uS = (u, u + 2) if end else (u + 1, u + 5)
                    if not last:
                        make_picks(s, i * 2 + (s + 2))
                    after_event(dve, e + (0 if end else 1), i, PE_EVENTS)
                    v.tensor_copy(actT[:, :, :].rearrange("p k c -> p (k c)"), bank(uA, 0)[:, 0:KT * C]
                                  ).then_inc(half_free[uA % 2], 2)
                    if not end:
                        product(u + 4, t + 12, s + 2, i)
                    for q in range(4):
                        after_event(dve, e + (1 if end else 3) + q, i, PE_EVENTS)
                        x = xT[:, :, :].rearrange("p (h j) t -> p h j t", h=2)[:, :, 2 * q:2 * q + 2, :]
                        y = half(uS + q).rearrange("p (h j) t -> p h j t", h=2)
                        tt(x, x, y, ALU.add).then_inc(half_free[(uS + q) % 2], 2)

            make_picks(0, 0)
            make_picks(1, 1)
            product(UNIT["moe"] + 2, TILE["moe"], 1, None)
            with dve.Fori(0, n_loops) as i:
                step.enter(i, 2)
                pair(i, False)
            step.leave_dynamic(n_loops)
            pair(n_loops, True)
            for q in range(4):
                read_out(dve, UNIT["final_stat"] - 4 + q, n_loops, PU)
            tt(hT[:, :, :], xT[:, :, :], xT[:, :, :], ALU.mult).then_inc(squares_ready, 1)
            apply_norm("norm_final", UNIT["final_stat"], xT, hT, range(DB), rstd[:, 0, :], T, h_ready, n_loops)
    return nc


_INS = ['x_prompt', 'x_sample', 'state_rglru_h', 'state_rglru_conv', 'state_sconv', 'cache_mem_k', 'cache_mem_v',
        'mem_prompt', 'norm_mix', 'w_in', 'rg_conv_w', 'rg_conv_b', 'rg_w_a', 'rg_b_a', 'rg_w_x', 'rg_b_x',
        'rg_lambda', 'sc_conv_w', 'norm_rg_out', 'norm_sc_out', 'w_out', 'norm_xattn', 'norm_mem', 'xa_w_q',
        'xa_w_k', 'xa_w_v', 'xa_w_o', 'norm_moe', 'router_group_w', 'router_group_b', 'router_expert_w',
        'router_expert_b', 'expert_w_gate', 'expert_w_up', 'expert_w_down', 'norm_final']
_OUTS = [('y_prompt', (1, TP, D)), ('y_sample', (NB, ST, D)), ('p_h', (1, 1, RG)), ('p_conv', (1, 1, CW - 1, RG)),
         ('p_sc', (1, 1, SW - 1, RG)), ('p_mem_k', (1, 1, NM, NH, D // NH)), ('p_mem_v', (1, 1, NM, NH, D // NH)),
         ('s_h', (1, NB, RG)), ('s_conv', (1, NB, CW - 1, RG)), ('s_sc', (1, NB, SW - 1, RG))]


def kernel(**inputs):
    import numpy as _np
    import concourse.bacc as _bacc
    from concourse import mybir as _mybir
    from concourse.bass_utils import run_bass_kernel_spmd as _run

    nc = _bacc.Bacc("TRN2", target_bir_lowering=False, num_devices=1)
    arrays, a, o = {}, {}, {}
    for name in _INS:
        x = _np.ascontiguousarray(inputs[name])
        arrays[f"in_{name}"] = x
        a[name] = nc.dram_tensor(f"in_{name}", x.shape, _mybir.dt.from_np(x.dtype), kind="ExternalInput").ap()
    for name, shape in _OUTS:
        o[name] = nc.dram_tensor(f"out_{name}", shape, _mybir.dt.float32, kind="ExternalOutput").ap()
    build(nc, a, o)
    r = _run(nc, [arrays], core_ids=[0])
    return tuple(r.results[0][f"out_{name}"] for name, _ in _OUTS)
```

```python
import math
from contextlib import ExitStack

import numpy as np
import concourse.bass as bass
from concourse import mybir

ALU = mybir.AluOpType
ACT = mybir.ActivationFunctionType
AX = mybir.AxisListType
F32 = mybir.dt.float32
I32 = mybir.dt.int32

P = 128
D = 2048
DB = D // P
TP = 256
NB, ST = 8, 4
T = TP + NB * ST
RG = D // 2
GB = RG // P
CW, SW = 4, 3
NM = 256
NH = 4
HB = DB // NH
NG, EG = 4, 4
NE = NG * EG
TOP_K = 2
FF = D // 4
EPS = 1e-6
RG_C = 8.0
SCALE = 1.0 / math.sqrt(D // NH)
XP = TP + NB * (CW - 1 + ST) + CW - 1
XO = XP - (CW - 1)
UP = TP + NB * (SW - 1 + ST) + SW - 1
UO = UP - (SW - 1)
SLOTS = 8
TW = 512
KT = 4
C = 64
NJ = 2 * -(-((TOP_K * T + NE * (C - 1)) // C) // 2)
NOWHERE = 1000

ROWS, _r = {}, 0
for _n, _c in (("norm_mix", 2), ("norm_xattn", 2), ("norm_mem", 2), ("norm_moe", 2), ("rg_conv_w", CW),
               ("rg_conv_b", 1), ("rg_b_a", 1), ("rg_b_x", 1), ("rg_lambda", 1), ("sc_conv_w", SW),
               ("norm_rg_out", 1), ("norm_sc_out", 1), ("state_rglru_conv", NB * (CW - 1)),
               ("state_rglru_h", NB), ("state_sconv", NB * (SW - 1)), ("norm_final", 2)):
    ROWS[_n] = _r
    _r += _c
NROWS = _r
S_CONV, S_H, S_SC = 0, (1 + NB) * (CW - 1), (1 + NB) * CW
NSTATE = S_SC + (1 + NB) * (SW - 1)

PU, PE_EVENTS = 12, 9
TILE, _t = {}, 0
for _n, _c in (("w_in", 32), ("w_last", 8), ("w_k", 16), ("w_v", 16), ("w_out", 16), ("w_q", 16), ("keys_0", 2),
               ("attention", 4 * NB), ("prompt_v", 2), ("w_o", 16), ("moe", 24)):
    TILE[_n] = _t
    _t += _c
UNIT, _u = {}, 0
for _n, _c in (("x", 3), ("mem", 2), ("pack", 1), ("x_stat", 1), ("mem_stat", 1), ("w_in", 8), ("gates", 2),
               ("w_last", 2), ("gates_b", 2),
               ("w_k", 4), ("mix_stat", 1), ("w_v", 4), ("states", 1), ("w_out", 4), ("xattn_stat", 1), ("w_q", 4),
               ("keys_0", 2), ("sample", 5 * NB), ("prompt", 7), ("w_o", 4), ("moe_stat", 1), ("router", 1), ("logits", 1), ("h_tok", 3),
               ("places", 1), ("moe", 12), ("final_stat", 1), ("y", 3)):
    UNIT[_n] = _u
    _u += _c
EVENT, _e = {}, 0
for _n, _c in (("x", 3), ("mem", 2), ("pack", 1), ("x_stat", 2), ("mem_stat", 2), ("gates", 4), ("mix_stat", 2),
               ("states", 1), ("xattn_stat", 2), ("sample", 2 * NB), ("prompt", 6), ("moe_stat", 2), ("router", 1), ("logits", 1),
               ("h_tok", 3), ("places", 1), ("moe", 9), ("final_stat", 2), ("y", 3)):
    EVENT[_n] = _e
    _e += _c


class Count:

    def __init__(self, sem):
        self.sem, self.n, self.i, self.per = sem, 0, None, 0

    def tick(self, ins, by=1):
        ins.then_inc(self.sem, by)
        self.n += by
        return ins

    def value(self, n=None):
        n = self.n if n is None else n
        return n if self.i is None else n + self.i * self.per

    def enter(self, i, per):
        self.i, self.per, self.start = i, per, self.n

    def leave_dynamic(self, times):
        assert self.n - self.start == self.per, (self.n - self.start, self.per)
        self.n, self.i = self.start, times

    def leave(self, times):
        assert self.n - self.start == self.per, (self.n - self.start, self.per)
        self.n = self.start + times * self.per
        self.i = None


def build(nc, a, o):
    ctx = ExitStack()
    with ctx:
        def sb(name, shape, dt=F32):
            return ctx.enter_context(nc.sbuf_tensor(name, shape, dt))

        def sem(name):
            return ctx.enter_context(nc.semaphore(name))

        ring = sb("ring", [P, SLOTS, KT * TW])
        xT = sb("xT", [P, DB, T])
        hT = sb("hT", [P, DB, T])
        mT = sb("mT", [P, DB, NM])
        kv_stage = sb("kv_stage", [P, 2, 2, TW])
        vec = sb("vec", [P, GB, NROWS])
        ident = sb("ident", [P, P])
        mean_d = sb("mean_d", [P, 32])
        mean_g = sb("mean_g", [P, 32])
        ones = sb("ones", [P, P])
        rstd = sb("rstd", [P, 2, T])
        small = sb("small", [P, 8, GB])
        consts = sb("consts", [P, 8])
        states = sb("states", [P, GB, NSTATE])
        wr = sb("wr", [P, DB, 32])
        rbias = sb("rbias", [P, NG + NE])
        before = sb("before", [P, P])
        place_iota = sb("place_iota", [P, 2, C])
        expert_of = sb("expert_of", [1, NJ], I32)
        seq_select = sb("seq_select", [P, NH * NB])
        seq_mask = sb("seq_mask", [P, NB])
        loops = sb("loops", [1, 1], I32)
        A = sb("A", [P, 17100])

        def cut(at, *shape):
            n = math.prod(shape)
            v = A[:, at:at + n]
            if len(shape) == 2:
                v = v.rearrange("p (a b) -> p a b", b=shape[1])
            if len(shape) == 3:
                v = v.rearrange("p (a b c) -> p a b c", b=shape[1], c=shape[2])
            return v, at + n

        x_nat, at = cut(0, 3, D)
        mem_nat, at = cut(at, 2, D)
        pack, at = cut(at, RG)
        mem_sq, at = cut(at, DB, NM)
        rgx, at = cut(0, GB, XP)
        gelu, at = cut(at, GB, T)
        scb, at = cut(at, GB, T)
        usc, at = cut(at, GB, UP)
        xc, at = cut(at, GB, XO)
        HG = GB // 2
        gr, at = cut(at, HG, XO)
        gi, at = cut(at, HG, XO)
        ge, at = cut(at, HG, XO)
        gE, at = cut(at, HG, XO)
        sq_mix, _ = cut(at - 4 * HG * XO, DB, T)
        uc, _ = cut(0, GB, UO)
        wbd = kv_stage[:, :, :, :].rearrange("p a b c -> p (a b c)").rearrange("p (a b c) -> p a b c", a=2, b=GB)
        sq_res, _ = cut(0, DB, T)
        oT = hT
        qT, at = cut(0, DB, T)
        kT, at = cut(at, DB, NM)
        pr, at = cut(at, 2 * NH, NM)
        pT, at = cut(at, 2, NH * TP)
        st, at = cut(at, 4, 2 * NH)
        o_nat, at = cut(at, TW)
        A_all, A = A, mT[:, :, :].rearrange("p a b -> p (a b)")
        lg, at = cut(0, 3, NG + NE)
        gt, at = cut(at, 3, 20 * 4)
        same_logit, at = cut(at, NG + NE)
        gate16, at = cut(at, 3, NE)
        mask16, at = cut(at, 3, NE)
        posm, at = cut(at, 3, NE)
        w4, at = cut(at, 4)
        tab, at = cut(at, 6, NE)
        cmp, at = cut(at, NJ, NE)
        jt, at = cut(at, 6, NJ)
        job_first = jt[:, 5, :]
        shifted, at = cut(at, 2, 4)
        job_gate, at = cut(at, 3, 2)
        place_gate, at = cut(at, 2)
        silu, at = cut(at, TW)
        act_nat, at = cut(at, TW)
        actT, at = cut(at, 2, KT, C)
        assert at <= DB * NM
        A = A_all
        h_tok, at = cut(0, 3, D)
        pick, at = cut(at, 3, 2 * C)
        spread, at = cut(at, T)
        x_pair, at = cut(at, D)
        xe, at = cut(at, DB, 2 * C)
        y_pair, at = cut(at, D)
        y_nat = ring[:, 0:3, :]
        states_nat = kv_stage[:, :, :, :].rearrange("p a b c -> p (a b c)")[:, 0:RG]

        ps = ctx.enter_context(nc.psum_tensor("ps", [P, 8, 512], F32))

        ring_loaded = [sem(f"ring_loaded{s}") for s in range(SLOTS)]
        tile_used = sem("tile_used")
        unit_done = sem("unit_done")
        half_free = [sem("half0_free"), sem("half1_free")]
        x_loaded, mem_loaded, pack_loaded, wbd_loaded, wr_loaded = map(
            sem, ("x_loaded", "mem_loaded", "pack_loaded", "wbd_loaded", "wr_loaded"))
        consts_set, wbd_zeroed, wr_zeroed = map(sem, ("consts_set", "wbd_zeroed", "wr_zeroed"))
        partial_ready = sem("partial_ready")
        dve_step, pool_step = sem("dve_step"), sem("pool_step")
        squares_ready = sem("squares_ready")
        mem_sq_ready = sem("mem_sq_ready")
        h_ready = sem("h_ready")
        root_ready = sem("root_ready")
        m_ready, xc_ready, pads_ready = sem("m_ready"), sem("xc_ready"), sem("pads_ready")
        lam_in, lam_exp = sem("lam_in"), sem("lam_exp")
        clamp_ready, exp_ready, mult_in_ready, mult_ready, scanned = map(
            sem, ("clamp_ready", "exp_ready", "mult_in_ready", "mult_ready", "scanned"))
        kv_stored = [sem("kv_stored0"), sem("kv_stored1")]
        states_ready, states_stored = sem("states_ready"), sem("states_stored")
        max_ready, probs_scaled = sem("max_ready"), sem("probs_scaled")
        gate_in, gate_exp, mask_ready, jobs_ready = map(sem, ("gate_in", "gate_exp", "mask_ready", "jobs_ready"))
        pick_ready, silu_ready = sem("pick_ready"), sem("silu_ready")
        y_stored = sem("y_stored")

        def G(n, w=4):
            return gt[:, :, 4 * n:4 * n + w]

        def gates_unit(h, n):
            return UNIT[("gates", "gates_b")[h]] + n

        def gain(name, b):
            return vec[:, b % GB, ROWS[name] + b // GB:ROWS[name] + b // GB + 1]

        def plus(n, i, per):
            return n if i is None else n + i * per

        def start_unit(pe, u, i=None, per=0):
            if u >= 2:
                pe.wait_ge(half_free[u % 2], plus(2 * (u // 2), i, per))

        def read_out(eng, u, i=None, per=0):
            eng.wait_ge(half_free[u % 2], plus(2 * (u // 2) + 2, i, per))

        def after_event(eng, e, i=None, per=0):
            eng.wait_ge(unit_done, plus(e + 1, i, per))

        def after_tile(eng, t, i=None, per=0):
            eng.wait_ge(tile_used, plus(t + 1, i, per))

        def bank(u, b):
            return ps[:, 4 * (u % 2) + b, :]

        def half(u, n=T, banks=4):
            return ps[:, 4 * (u % 2):4 * (u % 2) + banks, 0:n]

        def from_banks(u, n=P):
            return ps[:, 4 * (u % 2):4 * (u % 2) + 4, :].rearrange("p b (k n) -> p b k n", k=4)[:, :, :, 0:n]

        def quads(x):
            return x.rearrange("p (b k) n -> p b k n", k=4)

        def wait_tile(pe, t, i=None, per=8):
            pe.wait_ge(ring_loaded[t % SLOTS], plus(16 * (t // SLOTS + 1), i, 16 * per // SLOTS))

        def tile_of(t):
            return ring[:, t % SLOTS, :].rearrange("p (k n) -> p k n", k=KT)

        def sample_cols(x, lead, per):
            return x.rearrange("p (b t) -> p b t", t=lead + ST)[:, :, lead + ST - per:]

        def tiles_of(w):
            return w.rearrange("(g k p) m -> g p k m", k=KT, p=P)

        w_in, w_out, w_q, w_k, w_v, w_o = (tiles_of(a[n][0]) for n in (
            "w_in", "w_out", "xa_w_q", "xa_w_k", "xa_w_v", "xa_w_o"))
        e_gate = a["expert_w_gate"][0].rearrange("e (g k p) f -> e g p k f", k=KT, p=P)
        e_up = a["expert_w_up"][0].rearrange("e (g k p) f -> e g p k f", k=KT, p=P)
        e_down = a["expert_w_down"][0].rearrange("e (k p) m -> e p k m", p=P)
        cache = [a[n][0].rearrange("b (c p) h d -> b c p (h d)", p=P) for n in ("cache_mem_k", "cache_mem_v")]
        mem_out = [o[n][0].rearrange("b (c p) h d -> p (b c) (h d)", p=P) for n in ("p_mem_k", "p_mem_v")]

        block = ctx.enter_context(nc.Block())

        @block.sync
        def _(sp):
            sp.dma_start(x_nat[:, 0:2, :], a["x_prompt"][0].rearrange("(c p) d -> p c d", p=P)).then_inc(x_loaded, 16)
            sp.dma_start(x_nat[0:NB * ST, 2, :], a["x_sample"].rearrange("b t d -> (b t) d")).then_inc(x_loaded, 16)
            for name, rows in (("norm_mix", 2), ("norm_xattn", 2), ("norm_mem", 2), ("norm_moe", 2), ("rg_conv_w", CW),
                               ("rg_conv_b", 1), ("rg_b_a", 1), ("rg_b_x", 1), ("rg_lambda", 1), ("sc_conv_w", SW),
                               ("norm_rg_out", 1), ("norm_sc_out", 1), ("state_rglru_conv", NB * (CW - 1)),
                               ("state_rglru_h", NB), ("state_sconv", NB * (SW - 1)), ("norm_final", 2)):
                src = a[name]
                if name == "norm_final":
                    src = src.rearrange("(r c) -> r c", c=RG)
                elif name.startswith("norm") and rows == 2:
                    src = src[0].rearrange("(r c) -> r c", c=RG)
                elif name in ("state_rglru_conv", "state_sconv"):
                    src = src[0].rearrange("b r c -> (b r) c")
                elif len(src.shape) == 3:
                    src = src[0]
                sp.dma_start(pack[ROWS[name]:ROWS[name] + rows, :], src).then_inc(pack_loaded, 16)
            sp.dma_start(mem_nat[:, :, :], a["mem_prompt"][0].rearrange("(c p) d -> p c d", p=P)).then_inc(mem_loaded, 16)
            sp.wait_ge(wbd_zeroed, 1)
            for n, name in enumerate(("rg_w_a", "rg_w_x")):
                for e in range(2):
                    src = a[name][0].rearrange("(b two) i j -> two i b j", two=2)[e]
                    sp.dma_start(wbd[64 * e:64 * e + 64, n, :, 64 * e:64 * e + 64], src).then_inc(wbd_loaded, 16)
            sp.wait_ge(wr_zeroed, 1)
            sp.dma_start(wr[:, :, 0:NG], a["router_group_w"][0].rearrange("(b p) g -> p b g", p=P)).then_inc(wr_loaded, 16)
            sp.dma_start(wr[:, :, NG:NG + NE], a["router_expert_w"][0].rearrange("(b p) g -> p b g", p=P)).then_inc(wr_loaded, 16)
            sp.dma_start(rbias[:, 0:NG], a["router_group_b"][0].partition_broadcast(P)).then_inc(wr_loaded, 16)
            sp.dma_start(rbias[:, NG:], a["router_expert_b"][0].partition_broadcast(P)).then_inc(wr_loaded, 16)

            def load_tile(t, dst, src, i=None, per=8):
                if t >= SLOTS:
                    v = t - SLOTS + 1
                    sp.wait_ge(tile_used, v if i is None else v + i * per)
                sp.dma_start(dst, src).then_inc(ring_loaded[t % SLOTS], 16)

            def load_matrix(name, w, pairs):
                if name == "w_in":
                    for j in range(8):
                        load_tile(j, tile_of(j), w[j % 4, :, :, TW * (j // 4):TW * (j // 4) + TW])
                first = 1 if name == "w_in" else 0
                with sp.Fori(first, pairs) as i:
                    for j in range(8):
                        t = TILE[name] + j
                        v = t - SLOTS + 1
                        sp.wait_ge(tile_used, v + i * 8)
                        sp.dma_start(tile_of(t), w[j % 4, :, :, bass.ds(i * (2 * TW) + TW * (j // 4), TW)]
                                     ).then_inc(ring_loaded[t % SLOTS], 16)

            load_matrix("w_in", w_in, 5)
            load_matrix("w_k", w_k, 2)
            load_matrix("w_v", w_v, 2)
            load_matrix("w_out", w_out, 2)
            load_matrix("w_q", w_q, 2)
            def cache_tiles(t, n, j, i=None):
                for c in range(2):
                    src = cache[n][bass.ds(j, 1), c].rearrange("o p f -> (o p) f")
                    load_tile(t + c, ring[:, (t + c) % SLOTS, :], src, i)

            def prompt_tiles(t, n):
                for c in range(2):
                    load_tile(t + c, ring[:, (t + c) % SLOTS, :], mem_out[n][:, c, :])

            t = TILE["attention"]
            cache_tiles(TILE["keys_0"], 0, 0)
            with sp.Fori(0, NB // 2 - 1) as i:
                for s in range(2):
                    cache_tiles(t + 4 * s, 0, i * 2 + (s + 1), i)
                    cache_tiles(t + 4 * s + 2, 1, i * 2 + s, i)
            cache_tiles(t + 4 * NB - 8, 0, NB - 1)
            cache_tiles(t + 4 * NB - 6, 1, NB - 2)
            sp.wait_ge(kv_stored[0], 16 * 4)
            sp.wait_ge(kv_stored[1], 16 * 4)
            prompt_tiles(t + 4 * NB - 4, 0)
            cache_tiles(t + 4 * NB - 2, 1, NB - 1)
            prompt_tiles(TILE["prompt_v"], 1)
            load_matrix("w_o", w_o, 2)
            def branch_tiles(e, t, i=None):
                for j in range(8):
                    src = (e_gate, e_up)[j % 2][bass.ds(e, 1), j // 2].rearrange("o p k f -> (o p) k f")
                    load_tile(t + j, tile_of(t + j), src, i, per=24)

            branch_tiles(0, TILE["moe"])
            sp.wait_ge(jobs_ready, 2)

            def pair_of_jobs(i, last):
                t = TILE["moe"] + 8
                experts = [sp.value_load(expert_of[0:1, bass.ds(i * 2 + n, 1)], min_val=0, max_val=NE - 1)
                           for n in range(2 if last else 3)]
                branch_tiles(experts[1], t, i)
                for j in range(8):
                    src = e_down[bass.ds(experts[j % 2], 1), :, :, j // 2 * TW:(j // 2 + 1) * TW]
                    load_tile(t + 8 + j, tile_of(t + 8 + j), src.rearrange("o p k f -> (o p) k f"), i, per=24)
                if not last:
                    branch_tiles(experts[2], t + 16, i)

            n_loops = sp.value_load(loops[0:1, 0:1], min_val=NE // 2 - 1, max_val=NJ // 2 - 1)
            with sp.Fori(0, n_loops) as i:
                pair_of_jobs(i, False)
            pair_of_jobs(n_loops, True)
            for c in range(3):
                read_out(sp, UNIT["y"] + c, n_loops, PU)
                if c < 2:
                    sp.dma_start(o["y_prompt"][0, c * P:(c + 1) * P, :], y_nat[:, c, :]).then_inc(y_stored, 16)
                else:
                    sp.dma_start(o["y_sample"].rearrange("b t d -> (b t) d"), y_nat[0:NB * ST, 2, :]
                                 ).then_inc(y_stored, 16)
            sp.wait_ge(y_stored, 16 * 3)

        @block.gpsimd
        def _(pool):
            nc.gpsimd.memset(wbd[:, :, :, :].rearrange("p a b c -> p (a b c)"), 0.0).then_inc(wbd_zeroed, 1)
            nc.gpsimd.memset(wr[:, :, :], 0.0).then_inc(wr_zeroed, 1)
            nc.gpsimd.memset(ident[:, :], 0.0).then_inc(pool_step, 1)
            pool.wait_ge(pool_step, 1)
            nc.gpsimd.affine_select(out=ident[:, :], in_=ident[:, :], compare_op=ALU.not_equal, fill=1.0, base=0,
                                    pattern=[[-1, P]], channel_multiplier=1).then_inc(consts_set, 1)
            nc.gpsimd.memset(mean_d[:, :], 1.0 / (32 * D)).then_inc(consts_set, 1)
            nc.gpsimd.memset(mean_g[:, :], 1.0 / (32 * RG)).then_inc(consts_set, 1)
            nc.gpsimd.memset(ones[:, :], 1.0).then_inc(consts_set, 1)
            nc.gpsimd.memset(consts[:, 0:1], EPS).then_inc(consts_set, 1)
            nc.gpsimd.memset(consts[:, 1:2], -0.5).then_inc(consts_set, 1)
            pool.wait_ge(consts_set, 6)
            nc.gpsimd.affine_select(out=before[:, :], in_=ones[:, :], compare_op=ALU.is_gt, fill=0.0, base=0,
                                    pattern=[[1, P]], channel_multiplier=-1).then_inc(consts_set, 1)
            nc.gpsimd.iota(place_iota[:, :, :], pattern=[[0, 2], [1, C]], base=0, channel_multiplier=0,
                           allow_small_or_imprecise_dtypes=True).then_inc(consts_set, 1)
            nc.gpsimd.affine_select(out=seq_select[:, :], in_=ones[:, 0:NH * NB], compare_op=ALU.is_gt, fill=0.0, base=1,
                                    pattern=[[-ST, NH * NB]], channel_multiplier=1).then_inc(consts_set, 1)
            pool.wait_ge(consts_set, 9)
            nc.gpsimd.affine_select(out=seq_select[:, :], in_=seq_select[:, :], compare_op=ALU.is_gt, fill=0.0, base=ST,
                                    pattern=[[ST, NH * NB]], channel_multiplier=-1).then_inc(consts_set, 1)
            for n, name in enumerate(("w_k", "w_v")):
                for g in range(4):
                    read_out(pool, UNIT[name] + g)
                    pool.dma_start(mem_out[n][:, :, g * TW:(g + 1) * TW], kv_stage[:, g % 2, :, :]
                                   ).then_inc(kv_stored[g % 2], 16)
            read_out(pool, UNIT["states"])
            s = states_nat

            def out_rows(name, r0, n):
                dst = o[name][0]
                if len(dst.shape) == 3:
                    dst = dst.rearrange("b r c -> (b r) c")
                pool.dma_start(dst, s[r0:r0 + n, :]).then_inc(states_stored, 16)

            out_rows("p_conv", S_CONV, CW - 1)
            out_rows("s_conv", S_CONV + CW - 1, NB * (CW - 1))
            out_rows("p_h", S_H, 1)
            out_rows("s_h", S_H + 1, NB)
            out_rows("p_sc", S_SC, SW - 1)
            out_rows("s_sc", S_SC + SW - 1, NB * (SW - 1))
            pool.wait_ge(states_stored, 16 * 6)

        @block.tensor
        def _(pe):
            mm = nc.tensor.matmul

            def turn(u, src_of, rows, blocks=DB):
                start_unit(pe, u)
                for b in range(blocks):
                    t = nc.tensor.transpose(bank(u, b // 4)[:, b % 4 * P:b % 4 * P + rows], src_of(b),
                                            ident[0:rows, 0:rows])
                t.then_inc(unit_done, 1)

            pe.wait_ge(consts_set, 6)
            pe.wait_ge(x_loaded, 32)
            for c in range(3):
                rows = P if c < 2 else NB * ST
                turn(UNIT["x"] + c, lambda b: x_nat[0:rows, c, b * P:(b + 1) * P], rows)
            pe.wait_ge(mem_loaded, 16)
            for c in range(2):
                turn(UNIT["mem"] + c, lambda b: mem_nat[:, c, b * P:(b + 1) * P], P)
            pe.wait_ge(pack_loaded, 16 * 16)
            turn(UNIT["pack"], lambda b: pack[0:NROWS, b * P:(b + 1) * P], NROWS, GB)

            def stat(name, parts, squares, partial, i=None, per=0, groups=True):
                u = UNIT[name]
                start_unit(pe, u, i, per)
                for b, (w, sq, blocks, n) in enumerate(parts):
                    for k in blocks:
                        if groups and k % 4 == 0:
                            pe.wait_ge(squares, partial[0] + k // 4 + 1)
                        elif k == 0:
                            pe.wait_ge(squares, partial[0])
                        c = 32 * (k % 4)
                        m = mm(bank(u, b)[c:c + 32, 0:n], w[:, :], sq[:, k, :], start=(k < blocks[0] + 4),
                               stop=(k > blocks[-1] - 4))
                m.then_inc(unit_done, 1)
                pe.wait_ge(partial_ready, partial[1])
                for b, (w, sq, blocks, n) in enumerate(parts):
                    m = mm(bank(u, 2 + b)[:, 0:n], ones[:, :], rstd[:, partial[2] + b, 0:n], start=True, stop=True)
                m.then_inc(unit_done, 1)

            stat("x_stat", [(mean_d, hT, range(DB), T)], squares_ready, (1, 1, 0), groups=False)
            stat("mem_stat", [(mean_d, mem_sq, range(DB), NM)], mem_sq_ready, (2, 2, 1), groups=False)

            def project(name, pairs, h=None):
                with pe.Fori(0, pairs) as i:
                    for cg in range(2):
                        u = UNIT[name] + cg
                        start_unit(pe, u, i, 2)
                        for g in range(4):
                            t = TILE[name] + 4 * cg + g
                            wait_tile(pe, t, i)
                            if h is not None:
                                pe.wait_ge(h_ready, 4 * h + g + 1)
                            for k in range(KT):
                                for b in range(4):
                                    m = mm(bank(u, b)[:, 0:T], tile_of(t)[:, k, b * P:(b + 1) * P], hT[:, KT * g + k, :],
                                           start=(g == 0 and k == 0), stop=(g == 3 and k == KT - 1))
                            m.then_inc(tile_used, 1)

            def gates(h):
                for n in range(2):
                    u = gates_unit(h, n)
                    start_unit(pe, u)
                    for b in range(HG):
                        m = mm(bank(u, b)[:, 0:XO], wbd[:, n, HG * h + b, :], xc[:, HG * h + b, :], start=True, stop=True)
                    m.then_inc(unit_done, 1)

            project("w_in", 4, 0)
            pe.wait_ge(wbd_loaded, 16 * 4)
            pe.wait_ge(xc_ready, 1)
            gates(0)
            project("w_last", 1, 0)
            gates(1)

            def project_memory(name):
                with pe.Fori(0, 2) as i:
                    for cg in range(2):
                        u = UNIT[name] + cg
                        start_unit(pe, u, i, 2)
                        for g in range(4):
                            t = TILE[name] + 4 * cg + g
                            wait_tile(pe, t, i)
                            for k in range(KT):
                                for c in range(2):
                                    m = mm(bank(u, c), mT[:, KT * g + k, c * P:(c + 1) * P], tile_of(t)[:, k, :],
                                           start=(g == 0 and k == 0), stop=(g == 3 and k == KT - 1))
                            m.then_inc(tile_used, 1)

            pe.wait_ge(m_ready, 1)
            project_memory("w_k")
            stat("mix_stat", [(mean_g, sq_mix, range(GB), T), (mean_g, sq_mix, range(GB, DB), T)], squares_ready, (2, 3, 0),
                 groups=False)
            project_memory("w_v")
            u = UNIT["states"]
            start_unit(pe, u)
            pe.wait_ge(states_ready, 1)
            for b in range(GB):
                t = nc.tensor.transpose(bank(u, b // 4)[0:NSTATE, b % 4 * P:b % 4 * P + P], states[:, b, :], ident[:, :])
            t.then_inc(unit_done, 1)

            project("w_out", 2, 1)
            stat("xattn_stat", [(mean_d, sq_res, range(DB), T)], squares_ready, (2, 4, 0))
            project("w_q", 2, 2)

            def keys(u, t, i=None):
                start_unit(pe, u, i, 10)
                wait_tile(pe, t, i)
                for b in range(DB):
                    m = nc.tensor.transpose(bank(u, b // 4)[:, b % 4 * P:(b % 4 + 1) * P],
                                            ring[:, t % SLOTS, b * P:(b + 1) * P], ident[:, :])
                m.then_inc(tile_used, 1)

            def sequence_pair(u, t, j, i=None):
                for s in range(2):
                    start_unit(pe, u, i, 10)
                    for h in range(NH):
                        for k in range(HB):
                            m = mm(bank(u, 0)[32 * h:32 * h + 32, 0:NM], qT[:, HB * h + k, TP:T], kT[:, HB * h + k, :],
                                   start=(k == 0), stop=(k == HB - 1))
                    m.then_inc(unit_done, 1)
                    keys(u + 1, t, i)
                    start_unit(pe, u + 2, i, 10)
                    pe.wait_ge(probs_scaled, j + s + 1 if i is None else i * 2 + (s + 1))
                    for c in range(2):
                        m = nc.tensor.transpose(bank(u + 2, 0)[:, c * P:(c + 1) * P], pr[:, 0, c * P:(c + 1) * P], ident[:, :])
                    m.then_inc(unit_done, 1)
                    keys(u + 3, t + 1, i)
                    start_unit(pe, u + 4, i, 10)
                    for c in range(2):
                        wait_tile(pe, t + 2 + c, i)
                    for c in range(2):
                        for h in range(NH):
                            m = mm(bank(u + 4, 0)[32 * h:32 * h + 32, :], pT[:, c, 32 * h:32 * h + 32],
                                   ring[:, (t + 2 + c) % SLOTS, TW * h:TW * (h + 1)], start=(c == 0), stop=(c == 1))
                    m.then_inc(tile_used, 2)
                    u, t = u + 5, t + 4

            for g in range(2):
                read_out(pe, UNIT["w_q"] + 2 + g)
            for c in range(2):
                keys(UNIT["keys_0"] + c, TILE["keys_0"] + c)
            for c in range(2):
                read_out(pe, UNIT["keys_0"] + c)
            with pe.Fori(0, NB // 2 - 1) as i:
                sequence_pair(UNIT["sample"], TILE["attention"], 0, i)
            sequence_pair(UNIT["sample"] + 5 * (NB - 2), TILE["attention"] + 4 * (NB - 2), NB - 2)

            u, t = UNIT["prompt"], TILE["prompt_v"]
            for c in range(2):
                start_unit(pe, u + c)
                for h in range(NH):
                    for k in range(HB):
                        m = mm(bank(u + c, h // 2)[:, h % 2 * NM:(h % 2 + 1) * NM], qT[:, HB * h + k, c * P:(c + 1) * P],
                               kT[:, HB * h + k, :], start=(k == 0), stop=(k == HB - 1))
                m.then_inc(unit_done, 1)
            start_unit(pe, u + 2)
            read_out(pe, u - 1)
            for b in range(HB):
                m = nc.tensor.transpose(bank(u + 2, 0)[:, b * P:(b + 1) * P], o_nat[:, b * P:(b + 1) * P], ident[:, :])
            m.then_inc(unit_done, 1)
            for c in range(2):
                start_unit(pe, u + 3 + c)
                pe.wait_ge(probs_scaled, NB + 1 + c)
                for mc in range(2):
                    for h in range(NH):
                        m = nc.tensor.transpose(bank(u + 3 + c, mc)[:, h * P:(h + 1) * P],
                                                pr[:, NH * c + h, mc * P:(mc + 1) * P], ident[:, :])
                m.then_inc(unit_done, 1)
            for c in range(2):
                read_out(pe, u + 3 + c)
                wait_tile(pe, t + c)
            u, t = u + 1, t - 2
            for hf in range(2):
                start_unit(pe, u + 4 + hf)
                for b8 in range(8):
                    b = 8 * hf + b8
                    for c in range(2):
                        m = mm(bank(u + 4 + hf, b8 // 2)[:, b8 % 2 * TP:(b8 % 2 + 1) * TP],
                               ring[:, (t + 2 + c) % SLOTS, b * P:(b + 1) * P],
                               pT[:, c, TP * (b // HB):TP * (b // HB + 1)], start=(c == 0), stop=(c == 1))
                m.then_inc(*((tile_used, 2) if hf else (unit_done, 1)))
            for hf in range(2):
                read_out(pe, u + 4 + hf)
            project("w_o", 2)
            stat("moe_stat", [(mean_d, sq_res, range(DB), T)], squares_ready, (6, 5, 0))

            pe.wait_ge(wr_loaded, 16 * 4)
            u = UNIT["router"]
            start_unit(pe, u)
            for k in range(DB):
                if k % 4 == 0:
                    pe.wait_ge(h_ready, 4 * 3 + k // 4 + 1)
                c = 32 * (k % 4)
                m = mm(bank(u, 0)[c:c + 32, 0:T], wr[:, k, :], hT[:, k, :], start=(k < 4), stop=(k >= DB - 4))
            m.then_inc(unit_done, 1)
            u = UNIT["logits"]
            start_unit(pe, u)
            read_out(pe, u - 1)
            for c in range(3):
                rows = P if c < 2 else NB * ST
                m = mm(bank(u, c)[0:rows, 0:NG + NE], rstd[:, 0, c * P:c * P + rows], same_logit[:, :], start=True, stop=True)
            m.then_inc(unit_done, 1)
            for c in range(3):
                rows = P if c < 2 else NB * ST
                u = UNIT["h_tok"] + c
                start_unit(pe, u)
                for b in range(DB):
                    m = nc.tensor.transpose(bank(u, b // 4)[0:rows, b % 4 * P:(b % 4 + 1) * P],
                                            hT[:, b, c * P:c * P + rows], ident[:, :])
                m.then_inc(unit_done, 1)
            u = UNIT["places"]
            start_unit(pe, u)
            pe.wait_ge(consts_set, 10)
            pe.wait_ge(mask_ready, 1)
            for c in range(3):
                for k in range(c + 1):
                    mm(bank(u, c)[:, 0:NE], before[:, :] if k == c else ones[:, :], mask16[:, k, :],
                       start=(k == 0), stop=(k == c))
            for k in range(3):
                m = mm(bank(u, 3)[:, 0:NE], ones[:, :], mask16[:, k, :], start=(k == 0), stop=(k == 2))
            m.then_inc(unit_done, 1)

            def pick_unit(u, i):
                start_unit(pe, u, i, PU)
                for b in range(4):
                    for c in range(3):
                        rows = P if c < 2 else NB * ST
                        m = mm(bank(u, b), pick[0:rows, c, :], h_tok[0:rows, c, TW * b:TW * (b + 1)],
                               start=(c == 0), stop=(c == 2))
                m.then_inc(unit_done, 1)

            def place_unit(u, i):
                start_unit(pe, u, i, PU)
                for c in range(3):
                    rows = P if c < 2 else NB * ST
                    mm(bank(u, 0)[:, 0:2], pick[0:rows, c, :], job_gate[0:rows, c, :], start=(c == 0), stop=(c == 2))
                for c in range(3):
                    rows = P if c < 2 else NB * ST
                    m = nc.tensor.transpose(bank(u, 1)[:, c * P:c * P + rows], pick[0:rows, c, :], ident[0:rows, 0:rows])
                m.then_inc(unit_done, 1)

            def turn_unit(u, picked, i):
                start_unit(pe, u, i, PU)
                read_out(pe, picked, i, PU)
                for b in range(DB):
                    m = nc.tensor.transpose(bank(u, b // 4)[:, b % 4 * P:(b % 4 + 1) * P], x_pair[:, b * P:(b + 1) * P],
                                            ident[:, :])
                m.then_inc(unit_done, 1)

            def branch_unit(u, s, t, i):
                start_unit(pe, u, i, PU)
                for g in range(4):
                    wait_tile(pe, t + 2 * g, i, 24)
                    wait_tile(pe, t + 2 * g + 1, i, 24)
                    for k in range(KT):
                        b = KT * g + k
                        for n in range(2):
                            m = mm(bank(u, 0)[C * n:C * n + C, :], xe[:, b, C * s:C * s + C], tile_of(t + 2 * g + n)[:, k, :],
                                   start=(b == 0), stop=(b == DB - 1))
                    m.then_inc(tile_used, 2)

            def act_unit(u, branches, i):
                start_unit(pe, u, i, PU)
                read_out(pe, branches, i, PU)
                for k in range(KT):
                    m = mm(bank(u, 0)[:, k * C:(k + 1) * C], act_nat[0:C, k * P:(k + 1) * P], ident[0:C, 0:C],
                           start=True, stop=True)
                m.then_inc(unit_done, 1)

            def pair(i, last):
                u, t = UNIT["moe"] + 4, TILE["moe"] + 8
                uA1, uD, uS = (u + 2, u + 3, u + 4) if last else (u + 3, u + 4, u + 6)
                act_unit(u, u - 2, i)
                branch_unit(u + 1, 1, t, i)
                if not last:
                    pe.wait_ge(pick_ready, i + 2)
                    pick_unit(u + 2, i)
                act_unit(uA1, u + 1, i)
                start_unit(pe, uD, i, PU)
                read_out(pe, u, i, PU)
                read_out(pe, uA1, i, PU)
                for b in range(4):
                    wait_tile(pe, t + 8 + 2 * b, i, 24)
                    wait_tile(pe, t + 9 + 2 * b, i, 24)
                    for k in range(KT):
                        for s in range(2):
                            m = mm(bank(uD, b)[C * s:C * s + C, :], actT[:, s, k, :], tile_of(t + 8 + 2 * b + s)[:, k, :],
                                   start=(k == 0), stop=(k == KT - 1))
                    m.then_inc(tile_used, 2)
                if not last:
                    turn_unit(u + 5, u + 2, i)
                read_out(pe, uD, i, PU)
                for q in range(4):
                    start_unit(pe, uS + q, i, PU)
                    for b in range(4):
                        j = 4 * q + b
                        m = mm(bank(uS + q, b)[:, 0:T], y_pair[:, j * P:(j + 1) * P], spread[:, :], start=True, stop=True)
                    m.then_inc(unit_done, 1)
                if not last:
                    read_out(pe, u + 5, i, PU)
                    branch_unit(u + 10, 0, t + 16, i)
                    place_unit(u + 11, i)

            for c in range(3):
                read_out(pe, UNIT["h_tok"] + c)
            pe.wait_ge(jobs_ready, 2)
            n_loops = pe.value_load(loops[0:1, 0:1], min_val=NE // 2 - 1, max_val=NJ // 2 - 1)
            pe.wait_ge(pick_ready, 1)
            u = UNIT["moe"]
            pick_unit(u, None)
            turn_unit(u + 1, u, None)
            read_out(pe, u + 1)
            branch_unit(u + 2, 0, TILE["moe"], None)
            place_unit(u + 3, None)
            read_out(pe, u + 3)
            with pe.Fori(0, n_loops) as i:
                pair(i, False)
            pair(n_loops, True)

            stat("final_stat", [(mean_d, hT, range(DB), T)], squares_ready, (10, 6, 0), n_loops, PU)
            for c in range(3):
                rows = P if c < 2 else NB * ST
                u = UNIT["y"] + c
                start_unit(pe, u, n_loops, PU)
                for b in range(DB):
                    if c == 0 and b % 4 == 0:
                        pe.wait_ge(h_ready, 4 * 4 + b // 4 + 1)
                    m = nc.tensor.transpose(bank(u, b // 4)[0:rows, b % 4 * P:(b % 4 + 1) * P],
                                            hT[:, b, c * P:c * P + rows], ident[:, :])
                m.then_inc(unit_done, 1)

        @block.scalar
        def _(act):
            fn, copy = nc.scalar.activation, nc.scalar.copy

            u = UNIT["x"] + 1
            after_event(act, EVENT["x"] + 1)
            copy(quads(xT[:, :, P:2 * P]), from_banks(u)).then_inc(half_free[u % 2], 2)
            for c in range(2):
                u = UNIT["mem"] + c
                after_event(act, EVENT["mem"] + c)
                copy(quads(mT[:, :, c * P:(c + 1) * P]), from_banks(u)).then_inc(half_free[u % 2], 2)
                read_out(act, u)
                fn(mem_sq[:, :, c * P:(c + 1) * P], mT[:, :, c * P:(c + 1) * P], ACT.Square).then_inc(mem_sq_ready, 1)
            u = UNIT["pack"]
            after_event(act, EVENT["pack"])
            copy(vec[:, :, :].rearrange("p (b k) n -> p b k n", k=4), from_banks(u, NROWS)[:, 0:2]
                 ).then_inc(half_free[u % 2], 2)
            act.wait_ge(lam_in, 1)
            fn(small[:, 1, :], small[:, 0, :], ACT.Exp, scale=-1.0)
            fn(consts[:, 2:3], consts[:, 1:2], ACT.Exp).then_inc(lam_exp, 1)

            def root(name, dst, src, i=None):
                after_event(act, EVENT[name] + 1, i, PE_EVENTS)
                fn(dst, src, ACT.Sqrt, bias=consts[:, 0:1]).then_inc(half_free[UNIT[name] % 2], 2)

            root("x_stat", rstd[:, 0, :], bank(UNIT["x_stat"], 2)[:, 0:T])
            root("mem_stat", rstd[:, 1, 0:NM], bank(UNIT["mem_stat"], 2)[:, 0:NM])

            def to_padded(dst, u, g, lead):
                copy(dst[:, 4 * g:4 * g + 4, lead:lead + TP], half(u, TP)).then_inc(half_free[u % 2], 1)
                for b in range(4):
                    m = copy(sample_cols(dst[:, 4 * g + b, lead + TP:], lead, ST),
                             bank(u, b)[:, TP:T].rearrange("p (b t) -> p b t", t=ST))
                m.then_inc(half_free[u % 2], 1)

            act.wait_ge(pads_ready, 1)
            for g in range(2):
                after_tile(act, TILE["w_in"] + 4 * g + 3)
                to_padded(rgx, UNIT["w_in"] + g, g, CW - 1)
            for g in range(2):
                u = UNIT["w_in"] + 2 + g
                after_tile(act, TILE["w_in"] + 4 * (2 + g) + 3)
                fn(gelu[:, 4 * g:4 * g + 4, :], half(u), ACT.Gelu_apprx_tanh).then_inc(half_free[u % 2], 2)
            for g in range(2):
                after_tile(act, TILE["w_in"] + 4 * (6 + g) + 3)
                to_padded(usc, UNIT["w_in"] + 6 + g, g, SW - 1)

            for h in range(2):
                if h:
                    act.wait_ge(scanned, 1)
                for n, (dst, bias) in enumerate(((gr, "rg_b_a"), (gi, "rg_b_x"))):
                    u = gates_unit(h, n)
                    after_event(act, EVENT["gates"] + 2 * h + n)
                    for b in range(HG):
                        c = ROWS[bias]
                        m = fn(dst[:, b, :], bank(u, b)[:, 0:XO], ACT.Sigmoid, bias=vec[:, HG * h + b, c:c + 1])
                    m.then_inc(half_free[u % 2], 2)
                act.wait_ge(clamp_ready, h + 1)
                fn(gE[:, :, :], gE[:, :, :], ACT.Exp).then_inc(exp_ready, 1)
                act.wait_ge(mult_in_ready, h + 1)
                fn(gr[:, :, :], gr[:, :, :], ACT.Sqrt, scale=-1.0).then_inc(mult_ready, 1)

            for n, name in enumerate(("w_k", "w_v")):
                if n:
                    u = UNIT["mix_stat"]
                    after_event(act, EVENT["mix_stat"] + 1)
                    fn(rstd[:, :, :], ps[:, 4 * (u % 2) + 2:4 * (u % 2) + 4, 0:T], ACT.Sqrt, bias=consts[:, 0:1]).then_inc(half_free[u % 2], 2)
                for g in range(4):
                    u = UNIT[name] + g
                    after_tile(act, TILE[name] + 4 * g + 3)
                    if n or g >= 2:
                        act.wait_ge(kv_stored[g % 2], 16 * ((4 * n + g) // 2))
                    copy(kv_stage[:, g % 2, :, :], half(u, TW, 2)).then_inc(half_free[u % 2], 2)
            u = UNIT["states"]
            after_event(act, EVENT["states"])
            act.wait_ge(kv_stored[0], 16 * 4)
            act.wait_ge(kv_stored[1], 16 * 4)
            copy(states_nat[0:NSTATE, :].rearrange("p (a b) -> p a b", a=2), half(u, 512, 2)[0:NSTATE]
                 ).then_inc(half_free[u % 2], 2)
            def squares(first, dst, i=None):
                for g in range(4):
                    read_out(act, first + g, i, PU)
                    fn(dst[:, 4 * g:4 * g + 4, :], xT[:, 4 * g:4 * g + 4, :], ACT.Square).then_inc(squares_ready, 1)

            squares(UNIT["w_out"], sq_res)
            root("xattn_stat", rstd[:, 0, :], bank(UNIT["xattn_stat"], 2)[:, 0:T])

            for g in range(4):
                u = UNIT["w_q"] + g
                after_tile(act, TILE["w_q"] + 4 * g + 3)
                copy(qT[:, 4 * g:4 * g + 4, :], half(u)).then_inc(half_free[u % 2], 2)

            def keys(u, c, t, i=None):
                after_tile(act, t, i, 8)
                copy(kT[:, 0:GB, c * P:(c + 1) * P].rearrange("p (b k) n -> p b k n", k=4), from_banks(u)[:, 0:2]
                     ).then_inc(half_free[u % 2], 1)

            def sequence_pair(u, t, j, i=None):
                for s in range(2):
                    act.wait_ge(max_ready, j + s + 1 if i is None else i * 2 + (s + 1))
                    fn(pr[:, 0, :], bank(u, 0)[:, 0:NM], ACT.Exp, bias=st[:, 1, 0:1], scale=SCALE,
                       accum_out=st[:, 2, 0:1]).then_inc(half_free[u % 2], 2)
                    keys(u + 1, 0, t, i)
                    keys(u + 3, 1, t + 1, i)
                    u, t = u + 5, t + 4

            for c in range(2):
                keys(UNIT["keys_0"] + c, c, TILE["keys_0"] + c)
            with act.Fori(0, NB // 2 - 1) as i:
                sequence_pair(UNIT["sample"], TILE["attention"], 0, i)
            sequence_pair(UNIT["sample"] + 5 * (NB - 2), TILE["attention"] + 4 * (NB - 2), NB - 2)
            u = UNIT["prompt"]
            for c in range(2):
                act.wait_ge(max_ready, NB + 1 + c)
                for h in range(NH):
                    n = NH * c + h
                    m = fn(pr[:, n, :], bank(u + c, h // 2)[:, h % 2 * NM:(h % 2 + 1) * NM], ACT.Exp,
                           bias=st[:, 1, n:n + 1], scale=SCALE, accum_out=st[:, 2, n:n + 1])
                m.then_inc(half_free[(u + c) % 2], 2)
            squares(UNIT["w_o"], sq_res)
            root("moe_stat", rstd[:, 0, :], bank(UNIT["moe_stat"], 2)[:, 0:T])

            act.wait_ge(gate_in, 1)
            fn(G(4), G(3), ACT.Exp).then_inc(gate_exp, 1)
            act.wait_ge(gate_in, 2)
            fn(G(17, 1), G(16, 1), ACT.Exp).then_inc(gate_exp, 1)
            for c in range(3):
                rows = P if c < 2 else NB * ST
                u = UNIT["h_tok"] + c
                after_event(act, EVENT["h_tok"] + c)
                copy(h_tok[0:rows, c, :].rearrange("p (a b) -> p a b", a=4), half(u, 512)[0:rows]
                     ).then_inc(half_free[u % 2], 2)

            act.wait_ge(jobs_ready, 2)
            n_loops = act.value_load(loops[0:1, 0:1], min_val=NE // 2 - 1, max_val=NJ // 2 - 1)

            def halves(dst, u, banks):
                b = banks[0]
                return (dst.rearrange("p (a b) -> p a b", a=4)[:, b:b + 2, :],
                        ps[:, 4 * (u % 2) + b:4 * (u % 2) + b + 2, :])

            def picked(u, e, i):
                after_event(act, e, i, PE_EVENTS)
                copy(*halves(x_pair, u, (0, 1))).then_inc(half_free[u % 2], 1)

            def turned(u, e, i):
                after_event(act, e, i, PE_EVENTS)
                copy(*halves(xe[:, :, :].rearrange("p b c -> p (b c)"), u, (0, 1))).then_inc(half_free[u % 2], 1)

            def gate_branch(u, t, i):
                after_tile(act, t + 7, i, 24)
                fn(silu[0:C, :], bank(u, 0)[0:C, :], ACT.Silu).then_inc(silu_ready, 1)

            def places(u, e, i):
                after_event(act, e, i, PE_EVENTS)
                for s in range(2):
                    copy(place_gate[C * s:C * s + C, 0:1], bank(u, 0)[C * s:C * s + C, s:s + 1])
                copy(spread[:, :], bank(u, 1)[:, 0:T]).then_inc(half_free[u % 2], 2)

            def pair(i, last):
                u, t, e = UNIT["moe"] + 4, TILE["moe"] + 8, EVENT["moe"] + 3
                gate_branch(u + 1, t, i)
                if not last:
                    picked(u + 2, e + 1, i)
                uD = u + (3 if last else 4)
                after_tile(act, t + 15, i, 24)
                dst, src = halves(y_pair, uD, (0, 1))
                read_out(act, UNIT["moe"] + 3, i, PU)
                fn(dst, src, ACT.Copy, scale=place_gate[:, 0:1]).then_inc(half_free[uD % 2], 1)
                if not last:
                    turned(u + 5, e + 3, i)
                    gate_branch(u + 10, t + 16, i)
                    places(u + 11, e + 8, i)

            u, e = UNIT["moe"], EVENT["moe"]
            picked(u, e, None)
            turned(u + 1, e + 1, None)
            gate_branch(u + 2, TILE["moe"], None)
            places(u + 3, e + 2, None)
            with act.Fori(0, n_loops) as i:
                pair(i, False)
            pair(n_loops, True)
            squares(UNIT["final_stat"] - 4, hT, n_loops)
            root("final_stat", rstd[:, 0, :], bank(UNIT["final_stat"], 2)[:, 0:T], n_loops)
            for c in range(3):
                rows = P if c < 2 else NB * ST
                u = UNIT["y"] + c
                after_event(act, EVENT["y"] + c, n_loops, PE_EVENTS)
                copy(y_nat[0:rows, c, 0:2 * TW].rearrange("p (a b) -> p a b", a=2), half(u, TW, 2)[0:rows]
                     ).then_inc(half_free[u % 2], 1)

        @block.vector
        def _(dve):
            step = Count(dve_step)
            v = nc.vector
            tt, ts, stt = v.tensor_tensor, v.tensor_scalar, v.scalar_tensor_tensor

            def then(ins):
                step.tick(ins)
                dve.wait_ge(dve_step, step.value())

            for c, rows in ((0, P), (2, NB * ST)):
                u = UNIT["x"] + c
                after_event(dve, EVENT["x"] + c)
                v.tensor_copy(quads(xT[:, :, c * P:c * P + rows]), from_banks(u, rows)).then_inc(half_free[u % 2], 2)
            for c in range(3):
                read_out(dve, UNIT["x"] + c)
            tt(hT[:, :, :], xT[:, :, :], xT[:, :, :], ALU.mult).then_inc(squares_ready, 1)

            read_out(dve, UNIT["pack"])
            lam = vec[:, :, ROWS["rg_lambda"]]
            stt(out=small[:, 0, :], in0=lam, scalar=-1.0, in1=lam, op0=ALU.mult, op1=ALU.max).then_inc(lam_in, 1)

            def partial(name, count, banks, at=0, n=T, i=None):
                u = UNIT[name]
                after_event(dve, EVENT[name], i, PE_EVENTS)
                v.tensor_copy(rstd[:, at:at + banks, 0:n], half(u, n, banks)).then_inc(partial_ready, 1)

            def apply_norm(name, u, src, dst, blocks, rs, n, ready=None, i=None):
                read_out(dve, u, i, PU)
                then(v.reciprocal(rs, rs))
                for b in blocks:
                    m = stt(out=dst[:, b, 0:n], in0=src[:, b, 0:n], scalar=gain(name, b % (2 * GB)), in1=rs,
                            op0=ALU.mult, op1=ALU.mult)
                    if ready is h_ready and b % 4 == 3:
                        m.then_inc(ready, 1)
                if ready is m_ready:
                    m.then_inc(ready, 1)

            partial("x_stat", 1, 1)
            partial("mem_stat", 2, 1, 1, NM)
            apply_norm("norm_mix", UNIT["x_stat"], xT, hT, range(DB), rstd[:, 0, :], T, h_ready)
            apply_norm("norm_mem", UNIT["mem_stat"], mT, mT, range(DB), rstd[:, 1, 0:NM], NM, m_ready)

            v.memset(rgx[:, :, 0:CW - 1], 0.0)
            v.memset(usc[:, :, 0:SW - 1], 0.0)
            for b in range(GB):
                for dst, lead, rows in ((rgx, CW - 1, ROWS["state_rglru_conv"]), (usc, SW - 1, ROWS["state_sconv"])):
                    m = v.tensor_copy(
                        dst[:, b, lead + TP:].rearrange("p (b t) -> p b t", t=lead + ST)[:, :, 0:lead],
                        vec[:, b, rows:rows + NB * lead].rearrange("p (b t) -> p b t", t=lead))
            m.then_inc(pads_ready, 1)

            S = [small[:, n, :] for n in range(8)]
            dve.wait_ge(lam_exp, 1)
            then(ts(S[2], S[1], 2.0, None, ALU.add))
            then(v.reciprocal(S[2], S[2]))
            then(tt(S[3], S[1], S[2], ALU.mult))
            then(tt(S[4], S[3], S[3], ALU.mult))
            then(ts(S[5], S[4], 1.0 / 17, None, ALU.mult))
            for n in (15, 13, 11, 9, 7, 5, 3):
                then(stt(out=S[5], in0=S[5], scalar=1.0 / n, in1=S[4], op0=ALU.add, op1=ALU.mult))
            then(stt(out=S[5], in0=S[5], scalar=1.0, in1=S[3], op0=ALU.add, op1=ALU.mult))
            then(ts(S[7], lam, -1.0, 0.0, ALU.mult, ALU.max))
            then(stt(out=S[5], in0=S[5], scalar=2.0, in1=S[7], op0=ALU.mult, op1=ALU.add))
            then(ts(S[6], S[5], -RG_C, None, ALU.mult))

            def conv(dst, src, n, w, taps, bias):
                for k in range(taps):
                    for b in range(GB):
                        wk = vec[:, b, ROWS[w] + k:ROWS[w] + k + 1]
                        if k:
                            m = stt(out=dst[:, b, :], in0=src[:, b, k:k + n], scalar=wk, in1=dst[:, b, :],
                                    op0=ALU.mult, op1=ALU.add)
                        elif bias:
                            m = ts(dst[:, b, :], src[:, b, 0:n], wk, vec[:, b, ROWS[bias]:ROWS[bias] + 1],
                                   ALU.mult, ALU.add)
                        else:
                            m = ts(dst[:, b, :], src[:, b, 0:n], wk, None, ALU.mult)
                    if k < taps - 1:
                        then(m)
                return m

            for g in range(2):
                read_out(dve, UNIT["w_in"] + g)
            conv(xc, rgx, XO, "rg_conv_w", CW, "rg_conv_b").then_inc(xc_ready, 1)
            v.tensor_copy(states[:, :, S_CONV:S_CONV + CW - 1], rgx[:, :, TP:TP + CW - 1])
            for b in range(GB):
                m = v.tensor_copy(states[:, b, S_CONV + CW - 1:S_H].rearrange("p (b t) -> p b t", t=CW - 1),
                                  sample_cols(rgx[:, b, CW - 1 + TP:], CW - 1, CW - 1))
            then(m)

            for g in range(2):
                u = UNIT["w_in"] + 4 + g
                after_tile(dve, TILE["w_in"] + 4 * (4 + g) + 3)
                v.tensor_copy(scb[:, 4 * g:4 * g + 4, :], half(u)).then_inc(half_free[u % 2], 2)
            def recurrence(h):
                read_out(dve, gates_unit(h, 0))
                read_out(dve, gates_unit(h, 1))
                for b in range(HG):
                    m = ts(gr[:, b, :], gr[:, b, :], small[:, 6, HG * h + b:HG * h + b + 1], None, ALU.mult)
                then(m)
                ts(gE[:, :, :], gr[:, :, :], -0.5, None, ALU.min).then_inc(clamp_ready, 1)
                then(ts(gr[:, :, :], gr[:, :, :], -0.5, None, ALU.max))
                then(ts(ge[:, :, :], gr[:, :, :], 1.0 / math.factorial(8), None, ALU.mult))
                for n in range(7, 0, -1):
                    then(stt(out=ge[:, :, :], in0=ge[:, :, :], scalar=1.0 / math.factorial(n), in1=gr[:, :, :],
                             op0=ALU.add, op1=ALU.mult))
                dve.wait_ge(exp_ready, h + 1)
                then(stt(out=ge[:, :, :], in0=gE[:, :, :], scalar=consts[:, 2:3], in1=ge[:, :, :],
                         op0=ALU.subtract, op1=ALU.add))
                stt(out=gr[:, :, :], in0=ge[:, :, :], scalar=2.0, in1=ge[:, :, :], op0=ALU.add, op1=ALU.mult
                    ).then_inc(mult_in_ready, 1)
                then(ts(gE[:, :, :], ge[:, :, :], 1.0, None, ALU.add))
                then(tt(gi[:, :, :], gi[:, :, :], xc[:, HG * h:HG * h + HG, :], ALU.mult))
                dve.wait_ge(mult_ready, h + 1)
                then(tt(gi[:, :, :], gi[:, :, :], gr[:, :, :], ALU.mult))
                for b in range(HG):
                    r = ROWS["state_rglru_h"]
                    at = lambda x: x[:, b, TP:].rearrange("p (b t) -> p b t", t=CW - 1 + ST)[:, :, CW - 2:CW - 1]
                    v.memset(at(gE), 0.0)
                    m = v.tensor_copy(at(gi), vec[:, HG * h + b, r:r + NB].rearrange("p (b t) -> p b t", t=1))
                then(m)
                for b in range(HG):
                    m = v.tensor_tensor_scan(xc[:, HG * h + b, :], gE[:, b, :], gi[:, b, :], 0.0, ALU.mult, ALU.add)
                m.then_inc(scanned, 1)
            recurrence(0)
            for g in range(2):
                u = UNIT["w_last"] + g
                read_out(dve, UNIT["w_in"] + 6 + g)
                after_tile(dve, TILE["w_in"] + 4 * (8 + g) + 3)
                x = usc[:, 4 * g:4 * g + 4, SW - 1:SW - 1 + TP]
                tt(x, x, half(u, TP), ALU.mult)
                for b in range(4):
                    x = sample_cols(usc[:, 4 * g + b, SW - 1 + TP:], SW - 1, ST)
                    m = tt(x, x, bank(u, b)[:, TP:T].rearrange("p (b t) -> p b t", t=ST), ALU.mult)
                m.then_inc(half_free[u % 2], 2)
            for g in range(2):
                read_out(dve, UNIT["w_last"] + g)
            v.tensor_copy(states[:, :, S_SC:S_SC + SW - 1], usc[:, :, TP:TP + SW - 1])
            for b in range(GB):
                v.tensor_copy(states[:, b, S_SC + SW - 1:NSTATE].rearrange("p (b t) -> p b t", t=SW - 1),
                              sample_cols(usc[:, b, SW - 1 + TP:], SW - 1, SW - 1))

            recurrence(1)
            dve.wait_ge(scanned, 2)
            v.tensor_copy(states[:, :, S_H:S_H + 1], xc[:, :, TP - 1:TP])
            for b in range(GB):
                m = v.tensor_copy(states[:, b, S_H + 1:S_SC].rearrange("p (b t) -> p b t", t=1),
                                  sample_cols(xc[:, b, TP:], CW - 1, 1))
            m.then_inc(states_ready, 1)
            tt(hT[:, 0:GB, 0:TP], xc[:, :, 0:TP], gelu[:, :, 0:TP], ALU.mult)
            for b in range(GB):
                tt(hT[:, b, TP:T].rearrange("p (b t) -> p b t", t=ST), sample_cols(xc[:, b, TP:], CW - 1, ST),
                   gelu[:, b, TP:T].rearrange("p (b t) -> p b t", t=ST), ALU.mult)
            then(conv(uc, usc, UO, "sc_conv_w", SW, None))
            tt(hT[:, GB:DB, 0:TP], uc[:, :, 0:TP], scb[:, :, 0:TP], ALU.mult)
            for b in range(GB):
                m = tt(hT[:, GB + b, TP:T].rearrange("p (b t) -> p b t", t=ST), sample_cols(uc[:, b, TP:], SW - 1, ST),
                       scb[:, b, TP:T].rearrange("p (b t) -> p b t", t=ST), ALU.mult)
            then(m)
            tt(sq_mix[:, :, :], hT[:, :, :], hT[:, :, :], ALU.mult).then_inc(squares_ready, 1)
            partial("mix_stat", 3, 2)
            read_out(dve, UNIT["mix_stat"])
            then(v.reciprocal(rstd[:, :, :], rstd[:, :, :]))
            for n, name in enumerate(("norm_rg_out", "norm_sc_out")):
                for b in range(GB):
                    x = hT[:, GB * n + b, :]
                    m = stt(out=x, in0=x, scalar=vec[:, b, ROWS[name]:ROWS[name] + 1], in1=rstd[:, n, :],
                            op0=ALU.mult, op1=ALU.mult)
                    if b % 4 == 3:
                        m.then_inc(h_ready, 1)

            def add_residual(name):
                for g in range(4):
                    u = UNIT[name] + g
                    after_tile(dve, TILE[name] + 4 * g + 3)
                    x = xT[:, 4 * g:4 * g + 4, :]
                    tt(x, x, half(u), ALU.add).then_inc(half_free[u % 2], 2)

            add_residual("w_out")
            partial("xattn_stat", 4, 1)
            apply_norm("norm_xattn", UNIT["xattn_stat"], xT, hT, range(DB), rstd[:, 0, :], T, h_ready)

            dve.wait_ge(consts_set, 10)
            v.tensor_reduce(seq_mask[:, :], seq_select[:, :].rearrange("p (h j) -> p j h", h=NH), AX.X, ALU.add)
            then(v.memset(o_nat[:, :], 0.0))

            def keys(u, c, t, i=None):
                after_tile(dve, t, i, 8)
                v.tensor_copy(kT[:, GB:DB, c * P:(c + 1) * P].rearrange("p (b k) n -> p b k n", k=4),
                              from_banks(u)[:, 2:4]).then_inc(half_free[u % 2], 1)

            def sequence_pair(u, t, e, j, i=None):
                for s in range(2):
                    after_event(dve, e, i, 4)
                    then(v.tensor_reduce(st[:, 0, 0:1], bank(u, 0)[:, 0:NM], AX.X, ALU.max))
                    ts(st[:, 1, 0:1], st[:, 0, 0:1], -SCALE, None, ALU.mult).then_inc(max_ready, 1)
                    read_out(dve, u, i, 10)
                    then(v.reciprocal(st[:, 3, 0:1], st[:, 2, 0:1]))
                    of_seq = seq_mask[:, j + s:j + s + 1] if i is None else seq_mask[:, bass.ds(i * 2 + s, 1)]
                    then(tt(st[:, 3, 0:1], st[:, 3, 0:1], of_seq, ALU.mult))
                    ts(pr[:, 0, :], pr[:, 0, :], st[:, 3, 0:1], None, ALU.mult).then_inc(probs_scaled, 1)
                    keys(u + 1, 0, t, i)
                    after_event(dve, e + 1, i, 4)
                    v.tensor_copy(pT[:, :, 0:P], bank(u + 2, 0)[:, 0:NM].rearrange("p (c n) -> p c n", c=2)
                                  ).then_inc(half_free[(u + 2) % 2], 2)
                    keys(u + 3, 1, t + 1, i)
                    after_tile(dve, t + 3, i, 8)
                    tt(o_nat[:, :], o_nat[:, :], bank(u + 4, 0), ALU.add).then_inc(half_free[(u + 4) % 2], 2)
                    u, t, e = u + 5, t + 4, e + 2

            for c in range(2):
                keys(UNIT["keys_0"] + c, c, TILE["keys_0"] + c)
            with dve.Fori(0, NB // 2 - 1) as i:
                step.enter(i, 6)
                sequence_pair(UNIT["sample"], TILE["attention"], EVENT["sample"], 0, i)
                step.leave(NB // 2 - 1)
            sequence_pair(UNIT["sample"] + 5 * (NB - 2), TILE["attention"] + 4 * (NB - 2), EVENT["sample"] + 2 * (NB - 2),
                          NB - 2)
            u, e = UNIT["prompt"], EVENT["prompt"]
            for c in range(2):
                after_event(dve, e + c)
                own = slice(NH * c, NH * c + NH)
                then(v.tensor_reduce(st[:, 0, own].rearrange("p (a b) -> p a b", a=2),
                                     half(u + c, 512, 2).rearrange("p b (two n) -> p b two n", two=2), AX.X, ALU.max))
                ts(st[:, 1, own], st[:, 0, own], -SCALE, None, ALU.mult).then_inc(max_ready, 1)
                read_out(dve, u + c)
                then(v.reciprocal(st[:, 3, own], st[:, 2, own]))
                tt(pr[:, own, :], pr[:, own, :], st[:, 3, own].unsqueeze(2).broadcast_to([P, NH, NM]), ALU.mult
                   ).then_inc(probs_scaled, 1)
            after_event(dve, e + 2)
            v.tensor_copy(oT[:, :, TP:T].rearrange("p (h b) n -> p b h n", h=NH),
                          bank(u + 2, 0).rearrange("p (b h n) -> p b h n", b=HB, h=NH)).then_inc(half_free[u % 2], 2)
            for c in range(2):
                after_event(dve, e + 3 + c)
                for mc in range(2):
                    m = v.tensor_copy(pT[:, mc, :].rearrange("p (h n) -> p h n", h=NH)[:, :, c * P:(c + 1) * P],
                                      bank(u + 3 + c, mc).rearrange("p (h n) -> p h n", h=NH))
                m.then_inc(half_free[(u + 3 + c) % 2], 2)
            u, e = u + 1, e + 3
            for hf in range(2):
                if hf:
                    after_tile(dve, TILE["prompt_v"] + 1)
                else:
                    after_event(dve, e + 2)
                v.tensor_copy(oT[:, 8 * hf:8 * hf + 8, 0:TP].rearrange("p (b two) n -> p b two n", two=2),
                              half(u + 4 + hf, 512).rearrange("p b (two n) -> p b two n", two=2)
                              ).then_inc(half_free[(u + 4 + hf) % 2], 2)
            add_residual("w_o")
            partial("moe_stat", 5, 1)
            apply_norm("norm_moe", UNIT["moe_stat"], xT, hT, range(DB), rstd[:, 0, :], T, h_ready)

            def over(x, n):
                return x.broadcast_to([P, 3, n])

            def first_max(x, top, onehot, tmp):
                then(v.tensor_reduce(top, x, AX.X, ALU.max))
                then(tt(tmp, x, over(top, 4), ALU.is_equal))
                then(tt(tmp, tmp, w4.unsqueeze(1).broadcast_to([P, 3, 4]), ALU.mult))
                then(v.tensor_reduce(G(15, 1), tmp, AX.X, ALU.max))
                then(tt(onehot, tmp, over(G(15, 1), 4), ALU.is_equal))

            for n in range(4):
                v.memset(w4[:, n:n + 1], 4.0 - n)
            then(v.memset(lg[:, :, :], 0.0))
            dve.wait_ge(wr_loaded, 16 * 4)
            then(v.tensor_reduce(same_logit, ident[:, :].rearrange("p (j e) -> p e j", j=4)[:, 0:NG + NE, :], AX.X, ALU.add))
            u = UNIT["router"]
            after_event(dve, EVENT["router"])
            v.tensor_copy(rstd[:, 0, :], bank(u, 0)[:, 0:T]).then_inc(half_free[u % 2], 2)
            u = UNIT["logits"]
            after_event(dve, EVENT["logits"])
            for c in range(3):
                rows = P if c < 2 else NB * ST
                m = tt(lg[0:rows, c, :], bank(u, c)[0:rows, 0:NG + NE], rbias[0:rows, :], ALU.add)
            m.then_inc(half_free[u % 2], 2)
            read_out(dve, u)
            first_max(lg[:, :, 0:NG], G(0, 1), G(1), G(2))
            tt(G(3), lg[:, :, 0:NG], over(G(0, 1), 4), ALU.subtract).then_inc(gate_in, 1)
            by_expert = gt[:, :, 4 * 5:4 * 9].rearrange("p c (g j) -> p c g j", g=NG)
            for c in range(3):
                m = tt(by_expert[:, c], lg[:, c, NG:].rearrange("p (g j) -> p g j", g=NG),
                       G(1)[:, c].unsqueeze(2).broadcast_to([P, NG, EG]), ALU.mult)
            then(m)
            for c in range(3):
                m = v.tensor_reduce(G(9)[:, c], by_expert[:, c].rearrange("p g j -> p j g"), AX.X, ALU.add)
            then(m)
            first_max(G(9), G(10, 1), G(11), G(2))
            then(stt(out=G(12), in0=G(11), scalar=-1e30, in1=G(9), op0=ALU.mult, op1=ALU.add))
            first_max(G(12), G(13, 1), G(14), G(2))
            tt(G(16, 1), G(13, 1), G(10, 1), ALU.subtract).then_inc(gate_in, 1)
            dve.wait_ge(gate_exp, 2)
            then(tt(G(2), G(11), G(14), ALU.add))
            for c in range(3):
                m = tt(mask16[:, c, :].rearrange("p (g j) -> p g j", g=NG), G(1)[:, c].unsqueeze(2).broadcast_to([P, NG, EG]),
                       G(2)[:, c].unsqueeze(1).broadcast_to([P, NG, EG]), ALU.mult)
            then(m)
            v.memset(mask16[NB * ST:64, 2, :], 0.0)
            v.memset(mask16[64:P, 2, :], 0.0).then_inc(mask_ready, 1)
            then(v.tensor_reduce(G(18, 1), G(4), AX.X, ALU.add))
            then(stt(out=G(18, 1), in0=G(17, 1), scalar=1.0, in1=G(18, 1), op0=ALU.add, op1=ALU.mult))
            then(v.reciprocal(G(18, 1), G(18, 1)))
            then(tt(G(11), G(11), over(G(18, 1), 4), ALU.mult))
            then(tt(G(18, 1), G(18, 1), G(17, 1), ALU.mult))
            then(tt(G(14), G(14), over(G(18, 1), 4), ALU.mult))
            then(tt(G(11), G(11), G(14), ALU.add))
            for c in range(3):
                m = tt(gate16[:, c, :].rearrange("p (g j) -> p g j", g=NG), G(1)[:, c].unsqueeze(2).broadcast_to([P, NG, EG]),
                       G(11)[:, c].unsqueeze(1).broadcast_to([P, NG, EG]), ALU.mult)
            then(m)

            u = UNIT["places"]
            after_event(dve, EVENT["places"])
            for c in range(3):
                m = stt(out=posm[:, c, :], in0=bank(u, c)[:, 0:NE], scalar=4.0 * NOWHERE, in1=mask16[:, c, :],
                        op0=ALU.add, op1=ALU.mult)
            then(m)
            v.tensor_copy(tab[:, 0, :], bank(u, 3)[:, 0:NE]).then_inc(half_free[u % 2], 2)
            ts(posm[:, :, :], posm[:, :, :], -4.0 * NOWHERE, None, ALU.add)
            read_out(dve, u)
            counts, jobs, ends, onesr = (tab[:, n, :] for n in range(4))
            v.memset(onesr, 1.0)
            then(ts(jobs, counts, float(C), 1.0, ALU.is_gt, ALU.add))
            for n in range(2, -(-T // C)):
                then(stt(out=jobs, in0=counts, scalar=float(C * n), in1=jobs, op0=ALU.is_gt, op1=ALU.add))
            then(v.tensor_tensor_scan(ends, onesr, jobs, 0.0, ALU.mult, ALU.add))
            dve.wait_ge(consts_set, 10)
            iota_g = place_iota[:, 0, 0:NJ]
            over_e = ends.unsqueeze(1).broadcast_to([P, NJ, NE])
            then(tt(cmp[:, :, :], over_e, iota_g.unsqueeze(2).broadcast_to([P, NJ, NE]), ALU.is_le))
            then(v.tensor_reduce(jt[:, 0, :], cmp[:, :, :], AX.X, ALU.add))
            then(tt(cmp[:, :, :], cmp[:, :, :], jobs.unsqueeze(1).broadcast_to([P, NJ, NE]), ALU.mult))
            then(v.tensor_reduce(jt[:, 1, :], cmp[:, :, :], AX.X, ALU.add))
            then(tt(jt[:, 2, :], iota_g, jt[:, 1, :], ALU.subtract))
            then(ts(jt[:, 3, :], jt[:, 0, :], float(NE), float(NOWHERE), ALU.is_ge, ALU.mult))
            then(stt(out=job_first, in0=jt[:, 2, :], scalar=float(C), in1=jt[:, 3, :], op0=ALU.mult, op1=ALU.add))
            then(ts(jt[:, 0, :], jt[:, 0, :], float(NE - 1), None, ALU.min))
            v.tensor_copy(expert_of[0:1, :], jt[0:1, 0, :]).then_inc(jobs_ready, 1)
            then(ts(jt[:, 2, 0:NJ // 2], iota_g[:, 0:NJ // 2], 2.0, ends[:, NE - 1:NE], ALU.mult, ALU.is_lt))
            then(v.tensor_reduce(jt[:, 4, 0:1], jt[:, 2, 1:NJ // 2], AX.X, ALU.add))
            v.tensor_copy(loops[0:1, 0:1], jt[0:1, 4, 0:1]).then_inc(jobs_ready, 1)
            dve.wait_ge(jobs_ready, 2)
            n_loops = dve.value_load(loops[0:1, 0:1], min_val=NE // 2 - 1, max_val=NJ // 2 - 1)

            def make_picks(p):
                for s in range(2):
                    if isinstance(p, int) and p == 0 and s == 0:
                        first = job_first[:, 0:1]
                        cols = lambda x: x[:, :, 0:1]
                    else:
                        g = p * 2 + s
                        e = dve.value_load(expert_of[0:1, bass.ds(g, 1)], min_val=0, max_val=NE - 1)
                        first = job_first[:, bass.ds(g, 1)]
                        cols = lambda x: x[:, :, bass.ds(e, 1)]
                    v.tensor_copy(job_gate[:, :, s:s + 1], cols(gate16))
                    then(ts(shifted[:, s, 0:3], cols(posm).rearrange("p c o -> p (c o)"), first, None, ALU.subtract))
                    for c in range(3):
                        m = ts(pick[:, c, C * s:C * s + C], place_iota[:, 0, :], shifted[:, s, c:c + 1], None, ALU.is_equal)
                m.then_inc(pick_ready, 1)

            def upper(dst, u):
                return dst.rearrange("p (a b) -> p a b", a=4)[:, 2:4, :], ps[:, 4 * (u % 2) + 2:4 * (u % 2) + 4, :]

            def picked(u, e, i):
                after_event(dve, e, i, PE_EVENTS)
                v.tensor_copy(*upper(x_pair, u)).then_inc(half_free[u % 2], 1)

            def turned(u, e, i):
                after_event(dve, e, i, PE_EVENTS)
                v.tensor_copy(*upper(xe[:, :, :].rearrange("p b c -> p (b c)"), u)).then_inc(half_free[u % 2], 1)

            def act_out(u, s, e, i):
                after_event(dve, e, i, PE_EVENTS)
                v.tensor_copy(actT[:, s, :, :].rearrange("p k c -> p (k c)"), bank(u, 0)[:, 0:KT * C]
                              ).then_inc(half_free[u % 2], 2)

            def product(u, t, n, i):
                after_tile(dve, t + 7, i, 24)
                dve.wait_ge(silu_ready, plus(n, i, 2))
                tt(act_nat[0:C, :], silu[0:C, :], bank(u, 0)[C:2 * C, :], ALU.mult).then_inc(half_free[u % 2], 2)

            def pair(i, last):
                u, t, e = UNIT["moe"] + 4, TILE["moe"] + 8, EVENT["moe"] + 3
                if not last:
                    after_event(dve, e - 1, i, PE_EVENTS)
                    make_picks(i + 1)
                act_out(u, 0, e, i)
                product(u + 1, t, 2, i)
                if not last:
                    picked(u + 2, e + 1, i)
                uA1, uD, uS, eA1, eS = (u + 2, u + 3, u + 4, e + 1, e + 2) if last else (u + 3, u + 4, u + 6, e + 2, e + 4)
                act_out(uA1, 1, eA1, i)
                after_tile(dve, t + 15, i, 24)
                read_out(dve, UNIT["moe"] + 3, i, PU)
                dst, src = upper(y_pair, uD)
                ts(dst, src, place_gate[:, 0:1], None, ALU.mult).then_inc(half_free[uD % 2], 1)
                if not last:
                    turned(u + 5, e + 3, i)
                for q in range(4):
                    after_event(dve, eS + q, i, PE_EVENTS)
                    x = xT[:, 4 * q:4 * q + 4, :]
                    tt(x, x, half(uS + q), ALU.add).then_inc(half_free[(uS + q) % 2], 2)
                if not last:
                    product(u + 10, t + 16, 3, i)

            make_picks(0)
            u, e = UNIT["moe"], EVENT["moe"]
            picked(u, e, None)
            turned(u + 1, e + 1, None)
            product(u + 2, TILE["moe"], 1, None)
            with dve.Fori(0, n_loops) as i:
                step.enter(i, 2)
                pair(i, False)
            step.leave_dynamic(n_loops)
            pair(n_loops, True)
            partial("final_stat", 6, 1, i=n_loops)
            apply_norm("norm_final", UNIT["final_stat"], xT, hT, range(DB), rstd[:, 0, :], T, h_ready, n_loops)
            for c in range(3):
                rows = P if c < 2 else NB * ST
                u = UNIT["y"] + c
                after_event(dve, EVENT["y"] + c, n_loops, PE_EVENTS)
                v.tensor_copy(y_nat[0:rows, c, 2 * TW:D].rearrange("p (a b) -> p a b", a=2),
                              ps[0:rows, 4 * (u % 2) + 2:4 * (u % 2) + 4, :]).then_inc(half_free[u % 2], 1)
    return nc


_INS = ['x_prompt', 'x_sample', 'state_rglru_h', 'state_rglru_conv', 'state_sconv', 'cache_mem_k', 'cache_mem_v',
        'mem_prompt', 'norm_mix', 'w_in', 'rg_conv_w', 'rg_conv_b', 'rg_w_a', 'rg_b_a', 'rg_w_x', 'rg_b_x',
        'rg_lambda', 'sc_conv_w', 'norm_rg_out', 'norm_sc_out', 'w_out', 'norm_xattn', 'norm_mem', 'xa_w_q',
        'xa_w_k', 'xa_w_v', 'xa_w_o', 'norm_moe', 'router_group_w', 'router_group_b', 'router_expert_w',
        'router_expert_b', 'expert_w_gate', 'expert_w_up', 'expert_w_down', 'norm_final']
_OUTS = [('y_prompt', (1, TP, D)), ('y_sample', (NB, ST, D)), ('p_h', (1, 1, RG)), ('p_conv', (1, 1, CW - 1, RG)),
         ('p_sc', (1, 1, SW - 1, RG)), ('p_mem_k', (1, 1, NM, NH, D // NH)), ('p_mem_v', (1, 1, NM, NH, D // NH)),
         ('s_h', (1, NB, RG)), ('s_conv', (1, NB, CW - 1, RG)), ('s_sc', (1, NB, SW - 1, RG))]


def kernel(**inputs):
    import numpy as _np
    import concourse.bacc as _bacc
    from concourse import mybir as _mybir
    from concourse.bass_utils import run_bass_kernel_spmd as _run

    nc = _bacc.Bacc("TRN2", target_bir_lowering=False, num_devices=1)
    arrays, a, o = {}, {}, {}
    for name in _INS:
        x = _np.ascontiguousarray(inputs[name])
        arrays[f"in_{name}"] = x
        a[name] = nc.dram_tensor(f"in_{name}", x.shape, _mybir.dt.from_np(x.dtype), kind="ExternalInput").ap()
    for name, shape in _OUTS:
        o[name] = nc.dram_tensor(f"out_{name}", shape, _mybir.dt.float32, kind="ExternalOutput").ap()
    build(nc, a, o)
    r = _run(nc, [arrays], core_ids=[0])
    return tuple(r.results[0][f"out_{name}"] for name, _ in _OUTS)
```
